# Optimizing a Trainium2 kernel written in Bass

```python
import math
import jax, jax.numpy as jnp
from jax import lax
import numpy as np

D_MODEL = 1024
BATCH = 1
SEQ = 512
DEPTH = 1
DEC_BATCH = 8
DEC_SEQ = 16
PAST_LEN = 128

CHUNK = 64
N_HEADS = 8
HEAD_DIM = 64
V_DIM = 2 * HEAD_DIM
QK_WIDTH = N_HEADS * 2 * HEAD_DIM
ATTN_WIDTH = N_HEADS * V_DIM
ATTN_SCALE = HEAD_DIM ** -0.5
Q_BLOCK = 128
C_CONV = D_MODEL
CONV_K = 31
SPLITS = [QK_WIDTH, 2 * QK_WIDTH, 2 * QK_WIDTH + ATTN_WIDTH, 2 * QK_WIDTH + ATTN_WIDTH + 2 * C_CONV]
W_IN_COLS = SPLITS[-1] + 2 * D_MODEL
PEER_HEADS = 8
N_KEYS = 128
N_EXPERTS = N_KEYS * N_KEYS
PEER_TOPK = 16
D_KEY = 256
D_KEY_HALF = D_KEY // 2
PEER_BLOCK = 128

EPS = 1e-6
NEG_INF = -1e30

kernel_name = "chunk_causal_diffattn_conformer_peer"

def rms_norm(x, g):
    xf = x.astype(jnp.float32)
    y = xf * lax.rsqrt(jnp.mean(xf * xf, axis=-1, keepdims=True) + EPS)
    return (y * g.astype(jnp.float32)).astype(x.dtype)

def layer_norm(x, g, b):
    xf = x.astype(jnp.float32)
    mu = jnp.mean(xf, axis=-1, keepdims=True)
    xc = xf - mu
    y = xc * lax.rsqrt(jnp.mean(xc * xc, axis=-1, keepdims=True) + EPS)
    return (y * g.astype(jnp.float32) + b.astype(jnp.float32)).astype(x.dtype)

def diff_attend(q, k, v, lam, mask):
    s = jnp.einsum('bqhmd,bkhmd->bhmqk', q, k).astype(jnp.float32) * ATTN_SCALE
    if mask is not None:
        s = jnp.where(mask, s, NEG_INF)
    p = jax.nn.softmax(s, axis=-1)
    a = p[:, :, 0] - lam * p[:, :, 1]
    return jnp.einsum('bhqk,bkhe->bqhe', a, v.astype(jnp.float32))

def prompt_attention(q, k, v, lam):
    B, T = q.shape[0], q.shape[1]
    nb = T // Q_BLOCK
    qb = q.reshape(B, nb, Q_BLOCK, N_HEADS, 2, HEAD_DIM).transpose(1, 0, 2, 3, 4, 5)
    k_chunk = jnp.arange(T) // CHUNK

    def one(args):
        q_blk, i = args
        q_chunk = (i * Q_BLOCK + jnp.arange(Q_BLOCK)) // CHUNK
        mask = k_chunk[None, :] <= q_chunk[:, None]
        return diff_attend(q_blk, k, v, lam, mask)

    o = lax.map(one, (qb, jnp.arange(nb)))
    return o.transpose(1, 0, 2, 3, 4).reshape(B, T, N_HEADS, V_DIM)

def conv_branch(c, hist, w_dw, b_dw, g_cln, b_cln, w_conv_out):
    a, gate = jnp.split(c, 2, axis=-1)
    u = a * jax.nn.sigmoid(gate)
    full = jnp.concatenate([hist, u], axis=1)
    y = lax.conv_general_dilated(full, w_dw, window_strides=(1,), padding='VALID',
                                 dimension_numbers=('NWC', 'WIO', 'NWC'),
                                 feature_group_count=C_CONV) + b_dw
    y = jax.nn.silu(layer_norm(y, g_cln, b_cln))
    return y @ w_conv_out, full[:, -(CONV_K - 1):]

def peer(xn, w_pq, sub_keys, expert_u, expert_v):
    B, T, D = xn.shape
    n = B * T
    pad = (-n) % PEER_BLOCK
    xb = jnp.pad(xn.reshape(n, D), ((0, pad), (0, 0))).reshape(-1, PEER_BLOCK, D)

    def one(xt):
        q = (xt @ w_pq).reshape(PEER_BLOCK, PEER_HEADS, 2, D_KEY_HALF)
        s = jnp.einsum('thpd,hpkd->thpk', q, sub_keys).astype(jnp.float32)
        ts, ti = lax.top_k(s, PEER_TOPK)
        cand_s = (ts[:, :, 0, :, None] + ts[:, :, 1, None, :]).reshape(PEER_BLOCK, PEER_HEADS, PEER_TOPK * PEER_TOPK)
        cand_i = (ti[:, :, 0, :, None] * N_KEYS + ti[:, :, 1, None, :]).reshape(PEER_BLOCK, PEER_HEADS, PEER_TOPK * PEER_TOPK)
        best_s, best_j = lax.top_k(cand_s, PEER_TOPK)
        idx = jnp.take_along_axis(cand_i, best_j, axis=-1)
        g = jax.nn.softmax(best_s, axis=-1)
        u = expert_u[idx]
        act = jax.nn.gelu(jnp.einsum('thkd,td->thk', u, xt).astype(jnp.float32))
        w = (g * act).astype(xt.dtype)
        return jnp.einsum('thk,thkd->td', w, expert_v[idx])

    out = lax.map(one, xb).reshape(-1, D)[:n]
    return out.reshape(B, T, D)

def layer_forward(x, cache_k, cache_v, cache_conv, lambda_init,
                  g_mix, w_in, b_gate, g_qn, g_kn, lam_q1, lam_k1, lam_q2, lam_k2, g_sub,
                  w_attn_out, w_dw, b_dw, g_cln, b_cln, w_conv_out, w_out,
                  g_ffn, w_pq, sub_keys, expert_u, expert_v):
    B, T, _ = x.shape
    xn = rms_norm(x, g_mix)
    q, k, v, c, gt = jnp.split(xn @ w_in, SPLITS, axis=-1)
    q = rms_norm(q.reshape(B, T, N_HEADS, 2, HEAD_DIM), g_qn)
    k = rms_norm(k.reshape(B, T, N_HEADS, 2, HEAD_DIM), g_kn)
    v = v.reshape(B, T, N_HEADS, V_DIM)
    lam = (jnp.exp(jnp.sum(lam_q1.astype(jnp.float32) * lam_k1.astype(jnp.float32)))
           - jnp.exp(jnp.sum(lam_q2.astype(jnp.float32) * lam_k2.astype(jnp.float32)))
           + lambda_init)
    if cache_k is None:
        o = prompt_attention(q, k, v, lam)
        hist = jnp.zeros((B, CONV_K - 1, C_CONV), x.dtype)
    else:
        o = diff_attend(q, jnp.concatenate([cache_k, k], axis=1),
                        jnp.concatenate([cache_v, v], axis=1), lam, None)
        hist = cache_conv
    o = (rms_norm(o, g_sub) * (1.0 - lambda_init)).astype(x.dtype).reshape(B, T, ATTN_WIDTH)
    attn_out = o @ w_attn_out
    conv_out, conv_state = conv_branch(c, hist, w_dw, b_dw, g_cln, b_cln, w_conv_out)
    ga, gc = jnp.split(jax.nn.sigmoid((gt + b_gate).astype(jnp.float32)).astype(x.dtype), 2, axis=-1)
    h = x + (ga * attn_out + gc * conv_out) @ w_out
    y = h + peer(rms_norm(h, g_ffn), w_pq, sub_keys, expert_u, expert_v)
    return y, k, v, conv_state

def setup_inputs(seed: int = 0) -> dict:
    key = jax.random.key(seed)
    ks = jax.random.split(key, 32)
    f32 = jnp.float32

    def nrm(k, shape, scale):
        return jax.random.normal(k, shape, f32) * scale

    L = DEPTH
    return {
        "x_prompt": nrm(ks[0], (BATCH, SEQ, D_MODEL), 1.0),
        "x_sample": nrm(ks[1], (DEC_BATCH, DEC_SEQ, D_MODEL), 1.0),
        "cache_k": nrm(ks[2], (L, DEC_BATCH, PAST_LEN, N_HEADS, 2, HEAD_DIM), 1.0),
        "cache_v": nrm(ks[3], (L, DEC_BATCH, PAST_LEN, N_HEADS, V_DIM), 1.0),
        "cache_conv": nrm(ks[4], (L, DEC_BATCH, CONV_K - 1, C_CONV), 1.0),
        "g_mix": 1.0 + nrm(ks[5], (L, D_MODEL), 0.02),
        "w_in": nrm(ks[6], (L, D_MODEL, W_IN_COLS), D_MODEL ** -0.5),
        "b_gate": nrm(ks[7], (L, 2 * D_MODEL), 0.01),
        "g_qn": 1.0 + nrm(ks[8], (L, HEAD_DIM), 0.02),
        "g_kn": 1.0 + nrm(ks[9], (L, HEAD_DIM), 0.02),
        "lam_q1": nrm(ks[10], (L, HEAD_DIM), 0.1),
        "lam_k1": nrm(ks[11], (L, HEAD_DIM), 0.1),
        "lam_q2": nrm(ks[12], (L, HEAD_DIM), 0.1),
        "lam_k2": nrm(ks[13], (L, HEAD_DIM), 0.1),
        "g_sub": 1.0 + nrm(ks[14], (L, V_DIM), 0.02),
        "w_attn_out": nrm(ks[15], (L, ATTN_WIDTH, D_MODEL), ATTN_WIDTH ** -0.5),
        "w_dw": nrm(ks[16], (L, CONV_K, 1, C_CONV), CONV_K ** -0.5),
        "b_dw": nrm(ks[17], (L, C_CONV), 0.01),
        "g_cln": 1.0 + nrm(ks[18], (L, C_CONV), 0.02),
        "b_cln": nrm(ks[19], (L, C_CONV), 0.01),
        "w_conv_out": nrm(ks[20], (L, C_CONV, D_MODEL), C_CONV ** -0.5),
        "w_out": nrm(ks[21], (L, D_MODEL, D_MODEL), D_MODEL ** -0.5),
        "g_ffn": 1.0 + nrm(ks[22], (L, D_MODEL), 0.02),
        "w_pq": nrm(ks[23], (L, D_MODEL, PEER_HEADS * D_KEY), D_MODEL ** -0.5),
        "sub_keys": nrm(ks[24], (L, PEER_HEADS, 2, N_KEYS, D_KEY_HALF), D_KEY_HALF ** -0.5),
        "expert_u": nrm(ks[25], (L, N_EXPERTS, D_MODEL), D_MODEL ** -0.5),
        "expert_v": nrm(ks[26], (L, N_EXPERTS, D_MODEL), PEER_HEADS ** -0.5),
    }

def reference(x_prompt, x_sample, cache_k, cache_v, cache_conv,
              g_mix, w_in, b_gate, g_qn, g_kn, lam_q1, lam_k1, lam_q2, lam_k2, g_sub,
              w_attn_out, w_dw, b_dw, g_cln, b_cln, w_conv_out, w_out,
              g_ffn, w_pq, sub_keys, expert_u, expert_v):
    yp, ys = x_prompt, x_sample
    kp_l, vp_l, cp_l, ks_l, vs_l, cs_l = [], [], [], [], [], []
    for l in range(DEPTH):
        lambda_init = 0.8 - 0.6 * math.exp(-0.3 * l)
        w = (g_mix[l], w_in[l], b_gate[l], g_qn[l], g_kn[l], lam_q1[l], lam_k1[l],
             lam_q2[l], lam_k2[l], g_sub[l], w_attn_out[l], w_dw[l], b_dw[l], g_cln[l],
             b_cln[l], w_conv_out[l], w_out[l], g_ffn[l], w_pq[l], sub_keys[l],
             expert_u[l], expert_v[l])
        yp, kp, vp, cp = layer_forward(yp, None, None, None, lambda_init, *w)
        ys, kn, vn, cn = layer_forward(ys, cache_k[l], cache_v[l], cache_conv[l], lambda_init, *w)
        kp_l.append(kp); vp_l.append(vp); cp_l.append(cp)
        ks_l.append(kn); vs_l.append(vn); cs_l.append(cn)
    k_prompt = jnp.stack(kp_l)
    v_prompt = jnp.stack(vp_l)
    conv_prompt = jnp.stack(cp_l)
    k_sample = jnp.stack(ks_l)
    v_sample = jnp.stack(vs_l)
    conv_sample = jnp.stack(cs_l)
    return (yp, ys, k_prompt, v_prompt, conv_prompt, k_sample, v_sample, conv_sample)


_drawn_inputs = setup_inputs


def setup_inputs(seed=0):
    import zlib

    import numpy as np

    out = dict(_drawn_inputs(seed))
    spreads = {}
    factors = {'b_gate': 6.527,
     'g_qn': 3.113,
     'lam_q1': 132.067,
     'g_sub': 37.352,
     'b_dw': 3.855,
     'g_cln': 43.871,
     'b_cln': 83.431,
     'lam_q2': 28.728,
     'g_ffn': 16.35,
     'lam_k2': 8.0}
    for name, (base, spread) in spreads.items():
        noise = np.random.default_rng([zlib.crc32(name.encode()), seed]).standard_normal(out[name].shape)
        drawn = base * np.exp(spread * noise) if base else spread * noise
        out[name] = __import__('jax').numpy.asarray(drawn.astype(out[name].dtype))
    for name, factor in factors.items():
        out[name] = (out[name] * factor).astype(out[name].dtype)
    return out
```

```python
import math
from contextlib import ExitStack

import concourse.bass as bass
from concourse import mybir

ALU = mybir.AluOpType
ACT = mybir.ActivationFunctionType
AX_X = mybir.AxisListType.X
F32 = mybir.dt.float32
U32 = mybir.dt.uint32

P = 128
D = 1024
DT = D // P
PROMPT = 512
TOK = 640
TILES = TOK // P
PT = PROMPT // P
CHUNK = 64
HEADS = 8
DH = 64
STREAMS = 8
NEW = 16
PAST = 128
TAPS = 31
HIST = TAPS - 1
EPS = 1e-6
NEG = -1e30
SCALE = DH ** -0.5
LAMBDA_INIT = 0.8 - 0.6 * math.exp(-0.3 * 0)
K_COL, V_COL, C_COL, G_COL = D, 2 * D, 3 * D, 5 * D
WCH = 256
PH = 8
TOPK = 16
NKEYS = 128
U_RING = 8
V_RING = 4
U_LEN = HIST + PROMPT + STREAMS * (HIST + NEW)
US = HIST + PROMPT

C_GMIX, C_BGATE, C_BDW, C_GCLN, C_BCLN, C_GFFN, C_GSUB = 0, 8, 24, 32, 40, 48, 56
C_M, C_NM, C_SEL, C_DW = 57, 58, 59, 59 + 2 * HEADS - 1
COLS = C_DW + DT * TAPS
R_GQ, R_GK, R_LAM, R_IOTA, R_GFFN = 0, DH, 2 * DH, 6 * DH, 6 * DH + TOPK
ROWS = R_GFFN + D


class Chain:

    def __init__(self, eng, sem):
        self.eng, self.sem, self.n = eng, sem, 0

    def did(self, instruction):
        self.n += 1
        instruction.then_inc(self.sem, 1)

    def settled(self):
        self.eng.wait_ge(self.sem, self.n)

    def restart(self):
        self.settled()
        self.eng.sem_clear(self.sem)
        self.n = 0




class Memory:

    def __init__(self, nc, ctx):
        def sb(name, shape, dt=F32):
            return ctx.enter_context(nc.sbuf_tensor(name, shape, dt))

        slab_a = sb("slab_a", [P, DT * TOK])
        slab_d = sb("slab_d", [P, DT * TOK])
        slab_e = sb("slab_e", [P, DT * TOK])
        slab_qk = sb("slab_qk", [P, 2 * DT * TOK])
        slab_u = sb("slab_u", [P, DT * U_LEN])
        self.slab_u = slab_u
        self.slab_w = slab_w = sb("slab_w", [P, 8192])
        self.work = sb("work", [P, 7168])
        self.cols = cols = sb("cols", [P, COLS])
        self.rows = sb("rows", [P, ROWS])
        self.ident = sb("ident", [P, P])
        self.ones = sb("ones", [P, P])
        self.lam = sb("lam", [P, 16])
        self.small = sb("small", [P, 64])
        self.psum = ctx.enter_context(nc.psum_tensor("psum", [P, 8, 512], F32))

        channels = lambda s: s[:, :].rearrange("p (c t) -> p c t", c=DT)
        tiles = lambda s: s[:, :].rearrange("p (i n) -> p i n", i=TILES)
        self.xnT, self.h = channels(slab_a), tiles(slab_a)
        self.v, self.mT = tiles(slab_d), channels(slab_d)
        self.oT, self.xn2 = channels(slab_e), tiles(slab_e)
        self.qkT = slab_qk[:, :].rearrange("p (g t) -> p g t", g=2 * HEADS)
        self.scores = slab_qk[:, :].rearrange("p (n k) -> p n k", k=2 * NKEYS)
        self.scores_ig = slab_qk[:, :].rearrange("p (i g k) -> p i g k", i=TILES, g=2 * PH)
        self.uT = slab_u[:, :].rearrange("p (c t) -> p c t", c=DT)
        self.yT = self.uT[:, :, 0:TOK]
        self.wk = [slab_w[:, s * DT * WCH:(s + 1) * DT * WCH].rearrange("p (c n) -> p c n", c=DT) for s in range(2)]
        self.wu = [slab_w[:, s * D:(s + 1) * D].rearrange("p (c n) -> p c n", c=DT) for s in range(8)]
        self.wo = [slab_w[:, s * 4 * D:(s + 1) * 4 * D].rearrange("p (c n) -> p c n", c=DT) for s in range(2)]
        self.w_dw = cols[:, C_DW:C_DW + DT * TAPS].rearrange("p (c k) -> p c k", c=DT)

    def col(self, c, j=0):
        return self.cols[:, bass.ds(c + j, 1)]


def by_channels(w, c0, n):
    return w.rearrange("(c p) n -> p c n", p=P)[:, :, bass.ds(c0, n)]


def columns_of(t):
    return t[:, 0:PROMPT], t[:, PROMPT:TOK]


def project(nc, ctx, m, xT, w_in, cols_d, rows_d, ident_d, cc_T, k_p, k_s, v_p, v_s, c_p, c_s):
    def sem(name):
        return ctx.enter_context(nc.semaphore(name))

    consts_in, xT_in, hist_in = sem("consts_in"), sem("xT_in"), sem("hist_in")
    w_landed = [sem("w_landed0"), sem("w_landed1")]
    ones_set, hist_zero = sem("ones_set"), sem("hist_zero")
    sq_ready, sq_used = sem("sq_ready"), sem("sq_used")
    var_ready, std_ready, xnT_ready = sem("var_ready"), sem("std_ready"), sem("xnT_ready")
    z_ps, z_sq, z_var, z_std, z_ready = [sem(n) for n in ("z_ps", "z_sq", "z_var", "z_std", "z_ready")]
    zT_ps, zT_free = sem("zT_ps"), sem("zT_free")
    k_stored = [sem("k_stored0"), sem("k_stored1")]
    v_stored, c_stored = sem("v_stored"), sem("c_stored")
    glu_ps, gate_ready, u_ready = sem("glu_ps"), sem("gate_ready"), sem("u_ready")
    dve_did = sem("dve_did1")

    work, psum, xnT, uT, wk = m.work, m.psum, m.xnT, m.uT, m.wk
    sq = [work[:, s * TOK:(s + 1) * TOK] for s in range(2)]
    rB, std = work[:, 1280:1920], work[:, 1920:2560]
    zq = [work[:, 2560 + s * WCH:2560 + (s + 1) * WCH] for s in range(2)]
    zs = [work[:, 3072 + s * WCH:3072 + (s + 1) * WCH] for s in range(2)]
    zg = work[:, 3584:3584 + WCH]
    sg = [work[:, 3840 + s * TOK:3840 + (s + 1) * TOK] for s in range(2)]
    zsum, zvar, zstd, zr = [m.small[:, 4 * k:4 * k + 4] for k in range(4)]
    NCH = 3 * D // WCH
    QK = 2 * D // WCH
    groups = lambda a: a.rearrange("p (g d) -> p g d", d=DH)
    glu = [(0, 1, 2), (3, 4, 7)]

    block = ctx.enter_context(nc.Block())

    @block.sync
    def _(sp):
        sp.dma_start(m.cols[:, :], cols_d).then_inc(consts_in, 16)
        sp.dma_start(m.rows[:, :], rows_d).then_inc(consts_in, 16)
        sp.dma_start(m.ident[:, :], ident_d).then_inc(consts_in, 16)
        sp.dma_start(xnT, xT.rearrange("(c p) t -> p c t", p=P)).then_inc(xT_in, 16)
        for s in range(2):
            sp.dma_start(wk[s], by_channels(w_in, s * WCH, WCH)).then_inc(w_landed[s], 16)
        for j in range(DT):
            sp.dma_start(uT[:, j, US:].rearrange("p (b t) -> p b t", b=STREAMS)[:, :, 0:HIST],
                         cc_T[j]).then_inc(hist_in, 16)
        with sp.Fori(1, NCH // 2) as c:
            for s in range(2):
                sp.wait_ge(z_ps, 2 * TILES * c + TILES * (s - 1))
                sp.dma_start(wk[s], by_channels(w_in, 2 * WCH * c + s * WCH, WCH)).then_inc(w_landed[s], 16)
        for s in range(2):
            sp.wait_ge(z_ps, TILES * (NCH - 1 + s))
            for part in range(2):
                sp.dma_start(wk[s][:, :, part * P:(part + 1) * P],
                             by_channels(w_in, C_COL + part * D + s * P, P)).then_inc(w_landed[s], 16)
        with sp.Fori(1, DT // 2) as c:
            for s in range(2):
                sp.wait_ge(glu_ps, 2 * c + s - 1)
                for part in range(2):
                    sp.dma_start(wk[s][:, :, part * P:(part + 1) * P],
                                 by_channels(w_in, 2 * P * c + (C_COL + part * D + s * P), P)).then_inc(w_landed[s], 16)

    @block.gpsimd
    def _(pool):
        nc.gpsimd.memset(m.ones[:, :], 1.0).then_inc(ones_set, 1)
        nc.gpsimd.memset(uT[:, :, 0:HIST], 0.0).then_inc(hist_zero, 1)
        pool.wait_ge(z_ready, TILES * NCH)
        pool.dma_start(v_p.rearrange("(i p) n -> p i n", p=P), m.v[:, 0:PT, :]).then_inc(v_stored, 16)
        pool.dma_start(v_s, m.v[:, PT, :]).then_inc(v_stored, 16)
        pool.wait_ge(u_ready, DT)
        pool.wait_ge(hist_in, 16 * DT)
        for j in range(DT):
            pool.dma_start(c_p[j], uT[:, j, US - HIST:US]).then_inc(c_stored, 16)
            pool.dma_start(c_s[j], uT[:, j, US:].rearrange("p (b t) -> p b t", b=STREAMS)[:, :, NEW:]).then_inc(c_stored, 16)
        pool.wait_ge(k_stored[0], 16 * TILES * QK // 4)
        pool.wait_ge(k_stored[1], 16 * TILES * QK // 4)
        pool.wait_ge(v_stored, 32)
        pool.wait_ge(c_stored, 32 * DT)
        pool.wait_ge(hist_zero, 1)

    @block.tensor
    def _(pe):
        pe.wait_ge(ones_set, 1)
        pe.wait_ge(consts_in, 48)
        for c in range(DT):
            pe.wait_ge(sq_ready, c + 1)
            a, b = columns_of(sq[c % 2])
            nc.tensor.matmul(psum[:, 0, :], m.ones[:, :], a, start=(c == 0), stop=(c == DT - 1))
            nc.tensor.matmul(psum[:, 1, 0:P], m.ones[:, :], b, start=(c == 0), stop=(c == DT - 1)).then_inc(sq_used, 1)
        pe.wait_ge(xnT_ready, DT)

        def products(s, i):
            for c in range(DT):
                last = nc.tensor.matmul(psum[:, i, 0:WCH], xnT[:, c, i * P:(i + 1) * P], wk[s][:, c, :],
                                        start=(c == 0), stop=(c == DT - 1))
            last.then_inc(z_ps, 1)

        def turn(c, n, first):
            pe.wait_ge(z_ready, 2 * TILES * c + (n + 1))
            if not first or n >= 2:
                pe.wait_ge(zT_free, 2 * TILES * c + (n - 1))
            for g in range(2):
                last = nc.tensor.transpose(psum[:, 5 + n % 2, g * P:(g + 1) * P], zq[n % 2][:, g * P:(g + 1) * P],
                                           m.ident[:, :])
            last.then_inc(zT_ps, 1)

        def qk_body(c, first):
            for n in range(2 * TILES):
                s, i = divmod(n, TILES)
                if i == 0:
                    pe.wait_ge(w_landed[s], 16 * c + 16)
                if not first or n >= TILES:
                    pe.wait_ge(z_ready, 2 * TILES * c + (n - TILES + 1))
                products(s, i)
                if n >= 1:
                    turn(c, n - 1, first)
            turn(c, 2 * TILES - 1, first)

        qk_body(0, True)
        with pe.Fori(1, QK // 2) as c:
            qk_body(c, False)
        with pe.Fori(QK // 2, NCH // 2) as c:
            for n in range(2 * TILES):
                s, i = divmod(n, TILES)
                if i == 0:
                    pe.wait_ge(w_landed[s], 16 * c + 16)
                pe.wait_ge(z_ready, 2 * TILES * c + (n - TILES + 1))
                products(s, i)
        pe.wait_ge(z_ready, TILES * NCH)
        pe.wait_ge(zT_free, TILES * QK)
        with pe.Fori(0, DT // 2) as c:
            for s in range(2):
                pe.wait_ge(w_landed[s], 32 * c + (16 * NCH // 2 + 32))
                if s == 0:
                    pe.wait_ge(u_ready, 2 * c)
                for part in range(2):
                    for k in range(DT):
                        w = wk[s][:, k, part * P:(part + 1) * P]
                        nc.tensor.matmul(psum[:, glu[s][part], :], w, xnT[:, k, 0:PROMPT],
                                         start=(k == 0), stop=(k == DT - 1))
                        last = nc.tensor.matmul(psum[:, glu[s][2], part * P:(part + 1) * P], w, xnT[:, k, PROMPT:TOK],
                                                start=(k == 0), stop=(k == DT - 1))
                last.then_inc(glu_ps, 1)

    @block.scalar
    def _(act):
        act.wait_ge(xT_in, 16)
        for c in range(DT):
            if c >= 2:
                act.wait_ge(sq_used, c - 1)
            nc.scalar.activation(sq[c % 2], xnT[:, c, :], ACT.Square).then_inc(sq_ready, 1)
        act.wait_ge(var_ready, 2)
        nc.scalar.activation(std, rB, ACT.Sqrt).then_inc(std_ready, 1)

        def turned(c, n):
            s, i = divmod(n, TILES)
            act.wait_ge(zT_ps, 2 * TILES * c + (n + 1))
            nc.scalar.activation(m.qkT[:, bass.ds(4 * c + 2 * s, 2), i * P:(i + 1) * P],
                                 psum[:, 5 + n % 2, 0:WCH].rearrange("p (g t) -> p g t", g=2), ACT.Copy).then_inc(zT_free, 1)

        def store(c, n):
            s, i = divmod(n, TILES)
            act.wait_ge(z_ready, 2 * TILES * c + (n + 1))
            col = bass.ds(2 * WCH * c + (s * WCH - D), WCH)
            dst = k_p[i * P:(i + 1) * P, col] if i < PT else k_s[:, col]
            act.dma_start(dst, zq[n % 2]).then_inc(k_stored[n % 2], 16)

        for kind in range(2):
            with act.Fori(kind * QK // 4, (kind + 1) * QK // 4) as c:
                for n in range(2 * TILES):
                    i = n % TILES
                    act.wait_ge(z_ps, 2 * TILES * c + (n + 1))
                    if n >= 2:
                        act.wait_ge(z_ready, 2 * TILES * c + (n - 1))
                    nc.scalar.activation(zs[n % 2], psum[:, i, 0:WCH], ACT.Square).then_inc(z_sq, 1)
                    act.wait_ge(z_var, 2 * TILES * c + (n + 1))
                    nc.scalar.activation(zstd, zvar, ACT.Sqrt).then_inc(z_std, 1)
                    if n >= 1:
                        if kind == 1:
                            store(c, n - 1)
                        turned(c, n - 1)
                if kind == 1:
                    store(c, 2 * TILES - 1)
                turned(c, 2 * TILES - 1)
        with act.Fori(0, DT // 2) as c:
            for s in range(2):
                act.wait_ge(glu_ps, 2 * c + (s + 1))
                if s == 0:
                    act.wait_ge(u_ready, 2 * c)
                nc.scalar.activation(sg[s][:, 0:PROMPT], psum[:, glu[s][1], :], ACT.Sigmoid)
                nc.scalar.activation(sg[s][:, PROMPT:TOK], psum[:, glu[s][2], P:2 * P], ACT.Sigmoid).then_inc(gate_ready, 1)

    @block.vector
    def _(dve):
        steps = Chain(dve, dve_did)
        dve.wait_ge(consts_in, 48)
        lam = m.lam
        for k in range(2):
            a = m.rows[:, R_LAM + 2 * k * DH:R_LAM + (2 * k + 1) * DH]
            b = m.rows[:, R_LAM + (2 * k + 1) * DH:R_LAM + (2 * k + 2) * DH]
            steps.did(nc.vector.tensor_tensor(zg[:, k * DH:(k + 1) * DH], a, b, ALU.mult))
        steps.settled()
        steps.did(nc.vector.tensor_reduce(lam[:, 0:2], zg[:, 0:2 * DH].rearrange("p (k d) -> p k d", k=2), AX_X, ALU.add))
        steps.settled()
        dve.wait_ge(sq_used, DT)
        for (a, b) in zip(columns_of(rB), (psum[:, 0, :], psum[:, 1, 0:P])):
            nc.vector.tensor_scalar(a, b, 1.0 / D, EPS, ALU.mult, ALU.add).then_inc(var_ready, 1)
        dve.wait_ge(std_ready, 1)
        steps.did(nc.vector.reciprocal(rB, std))
        steps.settled()
        for c in range(DT):
            nc.vector.scalar_tensor_tensor(xnT[:, c, :], xnT[:, c, :], m.col(C_GMIX + c), rB, ALU.mult, ALU.mult).then_inc(xnT_ready, 1)
        for kind in range(2):
            gain = m.rows[:, R_GQ + kind * DH:R_GQ + (kind + 1) * DH]
            steps.restart()
            with dve.Fori(kind * QK // 4, (kind + 1) * QK // 4) as c:
                for n in range(2 * TILES):
                    i = n % TILES
                    dve.wait_ge(z_sq, 2 * TILES * c + (n + 1))
                    steps.did(nc.vector.tensor_reduce(zsum, groups(zs[n % 2]), AX_X, ALU.add))
                    steps.settled()
                    nc.vector.tensor_scalar(zvar, zsum, 1.0 / DH, EPS, ALU.mult, ALU.add).then_inc(z_var, 1)
                    steps.did(nc.vector.tensor_tensor(groups(zg), groups(psum[:, i, 0:WCH]),
                                                      gain[:, None, :].to_broadcast([P, 4, DH]), ALU.mult))
                    dve.wait_ge(z_std, 2 * TILES * c + (n + 1))
                    steps.did(nc.vector.reciprocal(zr, zstd))
                    steps.settled()
                    if n >= 2:
                        dve.wait_ge(zT_ps, 2 * TILES * c + (n - 1))
                    if kind == 1:
                        dve.wait_ge(k_stored[n % 2], 16 * TILES * c + 16 * (n // 2) - 16 * TILES * QK // 4)
                    nc.vector.tensor_tensor(groups(zq[n % 2]), groups(zg),
                                            zr[:, :, None].to_broadcast([P, 4, DH]), ALU.mult).then_inc(z_ready, 1)
                steps.restart()
        with dve.Fori(QK // 2, NCH // 2) as c:
            for n in range(2 * TILES):
                s, i = divmod(n, TILES)
                dve.wait_ge(z_ps, 2 * TILES * c + (n + 1))
                nc.vector.tensor_copy(m.v[:, i, bass.ds(2 * WCH * c + (s * WCH - 2 * D), WCH)],
                                      psum[:, i, 0:WCH]).then_inc(z_ready, 1)
        with dve.Fori(0, DT // 2) as c:
            for s in range(2):
                dve.wait_ge(gate_ready, 2 * c + (s + 1))
                nc.vector.tensor_tensor(uT[:, bass.ds(2 * c + s, 1), HIST:US].rearrange("p a t -> p (a t)"),
                                        psum[:, glu[s][0], :], sg[s][:, 0:PROMPT], ALU.mult)
                streams = uT[:, bass.ds(2 * c + s, 1), US:].rearrange("p a (b t) -> p (a b) t", b=STREAMS)[:, :, HIST:]
                nc.vector.tensor_tensor(streams, psum[:, glu[s][2], 0:P].rearrange("p (b t) -> p b t", b=STREAMS),
                                        sg[s][:, PROMPT:TOK].rearrange("p (b t) -> p b t", b=STREAMS),
                                        ALU.mult).then_inc(u_ready, 1)


def attend(nc, ctx, m, ck_T, cv, v_s):
    def sem(name):
        return ctx.enter_context(nc.semaphore(name))

    cache_in = [sem("cache_in0"), sem("cache_in1")]
    laid = sem("laid")
    bd_zero, bd_ready, lam_exp, lam_ready = sem("bd_zero"), sem("bd_ready"), sem("lam_exp"), sem("lam_ready")
    names = ("logits", "max_ready", "exp_ready", "probs", "probsT_ps", "probsT", "out_ps", "out_done")
    s_ps, s_max, s_exp, s_prob, s_pT, s_pTs, s_out, s_done = [sem("s_" + n) for n in names]
    p_ps, p_max, p_exp, p_prob, p_pT, p_pTs, p_out, p_done = [sem("p_" + n) for n in names]
    masked, head_ready = sem("masked"), sem("head_ready")
    tap, y_copied = sem("tap"), sem("y_copied")
    dve_did = sem("dve_did2")

    work, psum, slab_w, small = m.work, m.psum, m.slab_w, m.small
    T = PAST + NEW
    UNIT = HEADS // 2
    ckT = [slab_w[:, s * 3072:s * 3072 + 1024].rearrange("p (h t) -> p h t", h=HEADS) for s in range(2)]
    cvv = [slab_w[:, s * 3072 + 1024:s * 3072 + 2048].rearrange("p (h e) -> p h e", h=HEADS) for s in range(2)]
    vnew = [slab_w[0:NEW, s * 3072 + 2048:s * 3072 + 3072].rearrange("p (h e) -> p h e", h=HEADS) for s in range(2)]
    qh = [slab_w[:, s * 1536:s * 1536 + 512] for s in range(2)]
    kh = [slab_w[:, s * 1536 + 512:s * 1536 + 1024] for s in range(2)]
    vh = [slab_w[:, s * 1536 + 1024:s * 1536 + 1536].rearrange("p (i e) -> p i e", i=PT) for s in range(2)]
    probs = [work[:, s * 1024:(s + 1) * 1024].rearrange("p (m k) -> p m k", m=2) for s in range(2)]
    diff = [work[:, 2048 + s * 512:2560 + s * 512] for s in range(2)]
    second = work[:, 3072:3584]
    diffT = [work[:, 3584 + s * 512:4096 + s * 512] for s in range(2)]
    acc = work[:, 4608:4608 + TOK]
    sp_probs = [work[:, 5248 + s * T:5248 + (s + 1) * T] for s in range(2)]
    bd = [work[:, 5536 + s * 256:5792 + s * 256] for s in range(2)]
    kn = [work[:, 6048 + s * P:6176 + s * P].rearrange("p (h q) -> p h q", h=HEADS) for s in range(2)]
    sprobsT = [work[:, 6304 + s * 256:6560 + s * 256] for s in range(2)]
    mx = [small[:, 16 + 4 * s:18 + 4 * s] for s in range(2)]
    nmx = [small[:, 24 + 4 * s:26 + 4 * s] for s in range(2)]
    den = [small[:, 32 + 4 * s:34 + 4 * s] for s in range(2)]
    rden = [small[:, 40 + 4 * s:42 + 4 * s] for s in range(2)]
    minus_lam, row_sign = m.lam[:, 4:5], m.lam[:, 5:6]
    LU = 4
    bdv = lambda s: bd[s].rearrange("p (h m q) -> p h m q", h=HEADS, m=2)

    block = ctx.enter_context(nc.Block())

    @block.sync
    def _(sp):
        def load(s, b):
            sp.dma_start(slab_w[:, s * 3072:s * 3072 + 1024], ck_T[bass.ds(b, 1)].rearrange("a p n -> (a p) n")).then_inc(cache_in[s], 16)
            sp.dma_start(slab_w[:, s * 3072 + 1024:s * 3072 + 2048], cv[bass.ds(b, 1)].rearrange("a p n -> (a p) n")).then_inc(cache_in[s], 16)
            sp.dma_start(slab_w[0:NEW, s * 3072 + 2048:s * 3072 + 3072], v_s[bass.ds(b * NEW, NEW), :]).then_inc(cache_in[s], 16)

        for s in range(2):
            load(s, s)
        with sp.Fori(1, STREAMS // 2) as c:
            for s in range(2):
                sp.wait_ge(s_out, LU * c + (2 * s - 2))
                load(s, 2 * c + s)

    @block.gpsimd
    def _(pool):
        for s in range(2):
            nc.gpsimd.memset(bd[s], 0.0).then_inc(bd_zero, 1)
        pool.wait_ge(bd_zero, 2)

        def lay(s, b):
            new = bass.ds(b * NEW + PROMPT, NEW)
            for k in range(2):
                rows = slice(k * DH, (k + 1) * DH)
                nc.gpsimd.tensor_copy(bdv(s)[rows, :, k, :], m.qkT[rows, 0:HEADS, new]).then_inc(laid, 1)
                pool.wait_ge(laid, 2 * b + (k + 1))
            nc.gpsimd.tensor_copy(kn[s], m.qkT[:, HEADS:, new]).then_inc(bd_ready, 1)

        for s in range(2):
            lay(s, s)
        with pool.Fori(1, STREAMS // 2) as c:
            for s in range(2):
                pool.wait_ge(s_ps, LU * c + (2 * s - 2))
                lay(s, 2 * c + s)
        pool.wait_ge(s_out, 2 * STREAMS)

        def head(s, h):
            nc.gpsimd.tensor_copy(qh[s], m.qkT[:, bass.ds(h, 1), 0:PROMPT].rearrange("p a t -> p (a t)"))
            nc.gpsimd.tensor_copy(kh[s], m.qkT[:, bass.ds(h + HEADS, 1), 0:PROMPT].rearrange("p a t -> p (a t)"))
            nc.gpsimd.tensor_copy(vh[s], m.v[:, 0:PT, bass.ds(h * P, P)]).then_inc(head_ready, 1)

        for s in range(2):
            head(s, s)
        with pool.Fori(1, HEADS // 2) as c:
            for s in range(2):
                pool.wait_ge(p_out, 2 * PT * c + PT * (s - 1))
                head(s, 2 * c + s)

    @block.tensor
    def _(pe):
        def stream_logits(c, u):
            s, g = divmod(u, 2)
            if g == 0:
                pe.wait_ge(cache_in[s], 48 * c + 48)
                pe.wait_ge(bd_ready, 2 * c + (s + 1))
            if u >= 2:
                pe.wait_ge(s_exp, LU * c + (u - 1))
            for k in range(UNIT):
                h = g * UNIT + k
                out = psum[32 * k:32 * k + 32, u % 2, :]
                lhsT = bd[s][:, 32 * h:32 * h + 32]
                nc.tensor.matmul(out[:, 0:PAST], lhsT, ckT[s][:, h, :], start=True, stop=True)
                last = nc.tensor.matmul(out[:, PAST:T], lhsT, kn[s][:, h, :], start=True, stop=True)
            last.then_inc(s_ps, 1)

        def stream_turn(c, u):
            pe.wait_ge(s_prob, LU * c + (u + 1))
            if u >= 2:
                pe.wait_ge(s_pTs, LU * c + (u - 1))
            nc.tensor.transpose(psum[:, 2 + u % 2, 0:P], sp_probs[u % 2][:, 0:PAST], m.ident[:, :])
            nc.tensor.transpose(psum[0:NEW, 2 + u % 2, P:2 * P], sp_probs[u % 2][:, PAST:T], m.ident[:, :]).then_inc(s_pT, 1)

        def stream_values(c, u):
            s, g = divmod(u, 2)
            pe.wait_ge(s_pTs, LU * c + (u + 1))
            for k in range(UNIT):
                h = g * UNIT + k
                out = psum[:, 4 + s, h * NEW:(h + 1) * NEW]
                for j in range(2):
                    a = 32 * k + NEW * j
                    nc.tensor.matmul(out, cvv[s][:, h, :], sprobsT[u % 2][:, a:a + NEW], start=(j == 0), stop=False)
                    last = nc.tensor.matmul(out, vnew[s][:, h, :], sprobsT[u % 2][0:NEW, P + a:P + a + NEW],
                                            start=False, stop=(j == 1))
            last.then_inc(s_out, 1)

        with pe.Fori(0, STREAMS // 2) as c:
            pe.wait_ge(s_done, 2 * c)
            for u in range(LU):
                stream_logits(c, u)
                if u >= 1:
                    stream_turn(c, u - 1)
                if u >= 2:
                    stream_values(c, u - 2)
            stream_turn(c, LU - 1)
            stream_values(c, LU - 2)
            stream_values(c, LU - 1)
        pe.wait_ge(s_done, STREAMS)

        U = 2 * PT

        def logits(c, u):
            s, i = divmod(u, PT)
            n = (i + 1) * P
            if i == 0:
                pe.wait_ge(head_ready, 2 * c + (s + 1))
            if u >= 2:
                pe.wait_ge(p_exp, U * c + (u - 1))
            for j in range(2):
                rows = slice(j * DH, (j + 1) * DH)
                last = nc.tensor.matmul(psum[:, 2 * (u % 2) + j, 0:n], qh[s][rows, i * P:(i + 1) * P], kh[s][rows, 0:n],
                                        start=True, stop=True)
            last.then_inc(p_ps, 1)

        def turn(c, u):
            i = u % PT
            pe.wait_ge(p_prob, U * c + (u + 1))
            if u >= 2:
                pe.wait_ge(p_pTs, U * c + (u - 1))
            for k in range(i + 1):
                last = nc.tensor.transpose(psum[:, 4 + u % 2, k * P:(k + 1) * P], diff[u % 2][:, k * P:(k + 1) * P], m.ident[:, :])
            last.then_inc(p_pT, 1)

        def values(c, u):
            s, i = divmod(u, PT)
            pe.wait_ge(p_pTs, U * c + (u + 1))
            for k in range(i + 1):
                last = nc.tensor.matmul(psum[:, 6 + s, i * P:(i + 1) * P], vh[s][:, k, :], diffT[u % 2][:, k * P:(k + 1) * P],
                                        start=(k == 0), stop=(k == i))
            last.then_inc(p_out, 1)

        with pe.Fori(0, HEADS // 2) as c:
            pe.wait_ge(p_done, 2 * c)
            for u in range(U):
                logits(c, u)
                if u >= 1:
                    turn(c, u - 1)
                if u >= 2:
                    values(c, u - 2)
            turn(c, U - 1)
            values(c, U - 2)
            values(c, U - 1)

    @block.scalar
    def _(act):
        nc.scalar.activation(m.lam[:, 2:4], m.lam[:, 0:2], ACT.Exp).then_inc(lam_exp, 1)

        def stream_exp(c, u):
            act.wait_ge(s_max, LU * c + (u + 1))
            if u >= 2:
                act.wait_ge(s_pT, LU * c + (u - 1))
            nc.scalar.activation(sp_probs[u % 2], psum[:, u % 2, 0:T], ACT.Exp, bias=nmx[u % 2][:, 0:1], scale=SCALE,
                                 accum_out=den[u % 2][:, 0:1]).then_inc(s_exp, 1)

        def stream_copy(c, u):
            act.wait_ge(s_pT, LU * c + (u + 1))
            if u >= 2:
                act.wait_ge(s_out, LU * c + (u - 1))
            nc.scalar.activation(sprobsT[u % 2][:, 0:P], psum[:, 2 + u % 2, 0:P], ACT.Copy)
            nc.scalar.activation(sprobsT[u % 2][0:NEW, P:2 * P], psum[0:NEW, 2 + u % 2, P:2 * P], ACT.Copy).then_inc(s_pTs, 1)

        def stream_out(c, s):
            act.wait_ge(s_out, LU * c + 2 * (s + 1))
            nc.scalar.activation(m.oT[:, :, bass.ds(2 * NEW * c + (PROMPT + NEW * s), NEW)],
                                 psum[:, 4 + s, 0:P].rearrange("p (h q) -> p h q", h=HEADS), ACT.Copy).then_inc(s_done, 1)

        with act.Fori(0, STREAMS // 2) as c:
            for u in range(LU):
                stream_exp(c, u)
                if u >= 1:
                    stream_copy(c, u - 1)
            stream_copy(c, LU - 1)
            for s in range(2):
                stream_out(c, s)

        U = 2 * PT

        def exps(c, u):
            n = (u % PT + 1) * P
            act.wait_ge(p_max, U * c + (u + 1))
            if u >= 2:
                act.wait_ge(p_prob, U * c + (u - 1))
            for j in range(2):
                last = nc.scalar.activation(probs[u % 2][:, j, 0:n], psum[:, 2 * (u % 2) + j, 0:n], ACT.Exp,
                                            bias=nmx[u % 2][:, j:j + 1], scale=SCALE, accum_out=den[u % 2][:, j:j + 1])
            last.then_inc(p_exp, 1)

        def copy(c, u):
            n = (u % PT + 1) * P
            act.wait_ge(p_pT, U * c + (u + 1))
            if u >= 2:
                act.wait_ge(p_out, U * c + (u - 1))
            nc.scalar.activation(diffT[u % 2][:, 0:n], psum[:, 4 + u % 2, 0:n], ACT.Copy).then_inc(p_pTs, 1)

        def out(c, s):
            act.wait_ge(p_out, U * c + PT * (s + 1))
            nc.scalar.activation(m.oT[:, bass.ds(2 * c + s, 1), 0:PROMPT].rearrange("p a t -> p (a t)"), psum[:, 6 + s, :],
                                 ACT.Copy).then_inc(p_done, 1)

        def conv_out(c, s):
            act.wait_ge(tap, 2 * TAPS * (2 * c + s + 1))
            nc.scalar.activation(m.yT[:, bass.ds(2 * c + s, 1), :].rearrange("p a t -> p (a t)"), acc, ACT.Identity,
                                 bias=m.col(C_BDW, 2 * c + s)).then_inc(y_copied, 1)

        with act.Fori(0, HEADS // 2) as c:
            for u in range(U):
                exps(c, u)
                if u >= 1:
                    copy(c, u - 1)
                if u == PT:
                    conv_out(c, 0)
            copy(c, U - 1)
            for s in range(2):
                out(c, s)
            conv_out(c, 1)

    @block.vector
    def _(dve):
        steps = Chain(dve, dve_did)
        lam = m.lam
        dve.wait_ge(lam_exp, 1)
        steps.did(nc.vector.tensor_scalar(lam[:, 6:7], lam[:, 3:4], -LAMBDA_INIT, None, ALU.add))
        steps.settled()
        steps.did(nc.vector.tensor_tensor(minus_lam, lam[:, 6:7], lam[:, 2:3], ALU.subtract))
        steps.settled()
        steps.did(nc.vector.scalar_tensor_tensor(row_sign, m.col(C_M), minus_lam, m.col(C_NM), ALU.mult, ALU.add))
        steps.restart()

        def stream_max(c, u):
            dve.wait_ge(s_ps, LU * c + (u + 1))
            steps.did(nc.vector.reduce_max(mx[u % 2][:, 0:1], psum[:, u % 2, 0:T], AX_X))
            steps.settled()
            nc.vector.tensor_scalar(nmx[u % 2][:, 0:1], mx[u % 2][:, 0:1], -SCALE, None, ALU.mult).then_inc(s_max, 1)

        def stream_scale(c, u):
            dve.wait_ge(s_exp, LU * c + (u + 1))
            steps.did(nc.vector.reciprocal(rden[u % 2][:, 0:1], den[u % 2][:, 0:1]))
            steps.settled()
            steps.did(nc.vector.tensor_scalar(rden[u % 2][:, 1:2], rden[u % 2][:, 0:1], row_sign, None, ALU.mult))
            steps.settled()
            nc.vector.tensor_scalar(sp_probs[u % 2], sp_probs[u % 2], rden[u % 2][:, 1:2], None, ALU.mult).then_inc(s_prob, 1)

        with dve.Fori(0, STREAMS // 2) as c:
            for u in range(LU):
                stream_max(c, u)
                if u >= 1:
                    stream_scale(c, u - 1)
            stream_scale(c, LU - 1)
            steps.restart()

        U = 2 * PT

        def maxima(c, u):
            n = (u % PT + 1) * P
            b = 2 * (u % 2)
            dve.wait_ge(p_ps, U * c + (u + 1))
            nc.vector.memset(psum[0:CHUNK, b:b + 2, n - CHUNK:n], NEG).then_inc(masked, 1)
            dve.wait_ge(masked, U * c + (u + 1))
            steps.did(nc.vector.reduce_max(mx[u % 2], psum[:, b:b + 2, 0:n], AX_X))
            steps.settled()
            nc.vector.tensor_scalar(nmx[u % 2], mx[u % 2], -SCALE, None, ALU.mult).then_inc(p_max, 1)

        def combine(c, u):
            n = (u % PT + 1) * P
            dve.wait_ge(p_exp, U * c + (u + 1))
            steps.did(nc.vector.reciprocal(rden[u % 2], den[u % 2]))
            steps.settled()
            steps.did(nc.vector.tensor_scalar(second[:, 0:n], probs[u % 2][:, 1, 0:n], rden[u % 2][:, 1:2], minus_lam,
                                              ALU.mult, ALU.mult))
            steps.settled()
            if u >= 2:
                dve.wait_ge(p_pT, U * c + (u - 1))
            nc.vector.scalar_tensor_tensor(diff[u % 2][:, 0:n], probs[u % 2][:, 0, 0:n], rden[u % 2][:, 0:1], second[:, 0:n],
                                           ALU.mult, ALU.add).then_inc(p_prob, 1)

        def taps(c, s, k0, k1):
            row = m.uT[:, bass.ds(2 * c + s, 1), :].rearrange("p a t -> p (a t)")
            a, b = columns_of(acc)
            b = b.rearrange("p (n q) -> p n q", n=STREAMS)
            for k in range(k0, k1):
                w = m.w_dw[:, bass.ds(2 * c + s, 1), k:k + 1].rearrange("p a k -> p (a k)")
                u = row[:, k:k + PROMPT]
                v = row[:, US:].rearrange("p (n t) -> p n t", n=STREAMS)[:, :, k:k + NEW]
                if k == 0:
                    dve.wait_ge(y_copied, 2 * c + s)
                    nc.vector.tensor_scalar(a, u, w, None, ALU.mult).then_inc(tap, 1)
                    nc.vector.tensor_scalar(b, v, w, None, ALU.mult).then_inc(tap, 1)
                else:
                    dve.wait_ge(tap, 4 * TAPS * c + (2 * TAPS * s + 2 * k))
                    nc.vector.scalar_tensor_tensor(a, u, w, a, ALU.mult, ALU.add).then_inc(tap, 1)
                    nc.vector.scalar_tensor_tensor(b, v, w, b, ALU.mult, ALU.add).then_inc(tap, 1)

        with dve.Fori(0, HEADS // 2) as c:
            for u in range(U):
                maxima(c, u)
                if u >= 1:
                    combine(c, u - 1)
                s, q = divmod(u, PT)
                taps(c, s, q * 8, min(q * 8 + 8, TAPS))
            combine(c, U - 1)
            steps.restart()


def merge(nc, ctx, m, x, w_in, w_ao, w_co, w_out):
    def sem(name):
        return ctx.enter_context(nc.semaphore(name))

    w_landed = [sem(f"unit_landed{s}") for s in range(4)]
    wo_landed, x_in = [sem("wo_landed0"), sem("wo_landed1")], sem("x_in")
    o_sq, o_sum, o_var, o_std, o_rstd, o_spread, o_ready = [sem("o_" + n) for n in ("sq", "sum", "var", "std", "rstd", "spread", "ready")]
    y_sum, y_centred, y_sq, y_sq_sum, y_var, y_std, y_norm, y_ready = [
        sem("y_" + n) for n in ("sum", "centred", "sq", "sq_sum", "var", "std", "norm", "ready")]
    gp_ps, gate_ready, gp_done = sem("gp_ps"), sem("mgate_ready"), sem("gp_done")
    h_ps, h_done, h_sq, r_std, xn2_ready, x2T_ps, x2T_done = [sem(n) for n in ("h_ps", "h_done", "h_sq", "r_std", "xn2_ready", "x2T_ps", "x2T_done")]
    r_var, gain_ready = sem("r_var"), sem("gain_ready")
    dve_did = sem("dve_did3")

    work, psum = m.work, m.psum
    sq = [work[:, s * TOK:(s + 1) * TOK] for s in range(2)]
    rB, std, muB, bR, bstd = [work[:, (2 + k) * TOK:(3 + k) * TOK] for k in range(5)]
    sg = [work[:, (7 + k) * TOK:(8 + k) * TOK] for k in range(2)]
    first = work[:, 9 * TOK:10 * TOK]
    other = work[:, 10 * TOK:11 * TOK]
    hsq = work[:, 0:D]
    ss, var, hstd, rstd = [m.small[:, 16 + 2 * k:17 + 2 * k] for k in range(4)]
    sets = [(0, 1, 2), (3, 4, 5)]

    block = ctx.enter_context(nc.Block())

    @block.sync
    def _(sp):
        def unit(q, j):
            br = q % 2
            sp.dma_start(m.wu[2 * q], by_channels(w_in, j * P + (G_COL + br * D), P)).then_inc(w_landed[q], 16)
            sp.dma_start(m.wu[2 * q + 1], by_channels((w_ao, w_co)[br], j * P, P)).then_inc(w_landed[q], 16)

        for q in range(4):
            unit(q, q // 2)
        with sp.Fori(1, DT // 2) as c:
            for q in range(4):
                sp.wait_ge(gp_ps, 4 * c + (q - 3))
                unit(q, 2 * c + q // 2)
        sp.wait_ge(gp_ps, 2 * DT)
        for s in range(2):
            sp.dma_start(m.wo[s], by_channels(w_out, s * 512, 512)).then_inc(wo_landed[s], 16)
        sp.dma_start(m.h, x.rearrange("(i p) n -> p i n", p=P)).then_inc(x_in, 16)

    @block.tensor
    def _(pe):
        for h in range(HEADS):
            pe.wait_ge(o_sq, h + 1)
            sel = m.cols[:, C_SEL + HEADS - 1 - h:C_SEL + 2 * HEADS - 1 - h]
            a, b = columns_of(sq[h % 2])
            nc.tensor.matmul(psum[0:HEADS, 0, :], sel, a, start=(h == 0), stop=(h == HEADS - 1))
            nc.tensor.matmul(psum[0:HEADS, 1, 0:P], sel, b, start=(h == 0), stop=(h == HEADS - 1)).then_inc(o_sum, 1)
        for j in range(DT):
            a, b = columns_of(m.yT[:, j, :])
            nc.tensor.matmul(psum[:, 2, :], m.ones[:, :], a, start=(j == 0), stop=(j == DT - 1))
            last = nc.tensor.matmul(psum[:, 3, 0:P], m.ones[:, :], b, start=(j == 0), stop=(j == DT - 1))
        last.then_inc(y_sum, 1)
        pe.wait_ge(o_rstd, 1)
        for h in range(HEADS):
            if h >= 2:
                pe.wait_ge(o_ready, h - 1)
            sel = m.ident[0:HEADS, h:h + 1].to_broadcast([HEADS, P])
            a, b = columns_of(rB[0:HEADS, :])
            nc.tensor.matmul(psum[:, 4 + 2 * (h % 2), :], sel, a, start=True, stop=True)
            nc.tensor.matmul(psum[:, 5 + 2 * (h % 2), 0:P], sel, b, start=True, stop=True).then_inc(o_spread, 1)
        pe.wait_ge(o_var, 2)
        for j in range(DT):
            pe.wait_ge(y_sq, j + 1)
            a, b = columns_of(sq[j % 2])
            nc.tensor.matmul(psum[:, 0, :], m.ones[:, :], a, start=(j == 0), stop=(j == DT - 1))
            nc.tensor.matmul(psum[:, 1, 0:P], m.ones[:, :], b, start=(j == 0), stop=(j == DT - 1)).then_inc(y_sq_sum, 1)
        pe.wait_ge(y_ready, DT)
        pe.wait_ge(o_ready, HEADS)
        with pe.Fori(0, DT // 2) as c:
            for q in range(4):
                t = sets[q % 2]
                pe.wait_ge(w_landed[q], 32 * c + 32)
                if q >= 2:
                    pe.wait_ge(gp_done, 4 * c + (q - 1))
                elif q == 0:
                    pe.wait_ge(gp_done, 4 * c)
                for part, rhs in enumerate((m.xnT, (m.oT, m.yT)[q % 2])):
                    for k in range(DT):
                        a, b = columns_of(rhs[:, k, :])
                        w = m.wu[2 * q + part][:, k, :]
                        nc.tensor.matmul(psum[:, t[part], :], w, a, start=(k == 0), stop=(k == DT - 1))
                        last = nc.tensor.matmul(psum[:, t[2], part * P:(part + 1) * P], w, b, start=(k == 0), stop=(k == DT - 1))
                last.then_inc(gp_ps, 1)
        pe.wait_ge(gp_done, 2 * DT)

        def turn(i):
            pe.wait_ge(xn2_ready, i + 1)
            if i >= 1:
                pe.wait_ge(x2T_done, i)
            for k in range(DT):
                last = nc.tensor.transpose(psum[:, 4 + k // 4, (k % 4) * P:(k % 4 + 1) * P], m.xn2[:, i, k * P:(k + 1) * P], m.ident[:, :])
            last.then_inc(x2T_ps, 1)

        for i in range(TILES):
            b = 2 * (i % 2)
            if i >= 2:
                pe.wait_ge(h_done, i - 1)
            for s in range(2):
                pe.wait_ge(wo_landed[s], 16)
                for k in range(DT):
                    last = nc.tensor.matmul(psum[:, b + s, :], m.mT[:, k, i * P:(i + 1) * P], m.wo[s][:, k, :],
                                            start=(k == 0), stop=(k == DT - 1))
            last.then_inc(h_ps, 1)
            if i >= 1:
                turn(i - 1)
        turn(TILES - 1)

    @block.scalar
    def _(act):
        for h in range(HEADS):
            if h >= 2:
                act.wait_ge(o_sum, h - 1)
            nc.scalar.activation(sq[h % 2], m.oT[:, h, :], ACT.Square).then_inc(o_sq, 1)
        act.wait_ge(o_var, 2)
        nc.scalar.activation(std[0:HEADS, :], rB[0:HEADS, :], ACT.Sqrt).then_inc(o_std, 1)
        act.wait_ge(o_sum, HEADS)
        for j in range(DT):
            act.wait_ge(y_centred, j + 1)
            if j >= 2:
                act.wait_ge(y_sq_sum, j - 1)
            nc.scalar.activation(sq[j % 2], m.yT[:, j, :], ACT.Square).then_inc(y_sq, 1)
        act.wait_ge(y_var, 2)
        nc.scalar.activation(bstd, bR, ACT.Sqrt).then_inc(y_std, 1)
        for j in range(DT):
            act.wait_ge(y_norm, j + 1)
            nc.scalar.activation(m.yT[:, j, :], m.yT[:, j, :], ACT.Silu, bias=m.col(C_BCLN + j), scale=m.col(C_GCLN + j)).then_inc(y_ready, 1)
        with act.Fori(0, DT // 2) as c:
            for q in range(4):
                t = sets[q % 2]
                act.wait_ge(gp_ps, 4 * c + (q + 1))
                if q >= 2:
                    act.wait_ge(gp_done, 4 * c + (q - 1))
                bias = m.col(C_BGATE + DT * (q % 2) + q // 2, 2 * c)
                a, b = columns_of(sg[q % 2])
                nc.scalar.activation(a, psum[:, t[0], :], ACT.Sigmoid, bias=bias)
                nc.scalar.activation(b, psum[:, t[2], 0:P], ACT.Sigmoid, bias=bias).then_inc(gate_ready, 1)
        for i in range(TILES):
            act.wait_ge(h_done, i + 1)
            nc.scalar.activation(hsq, m.h[:, i, :], ACT.Square, accum_out=ss).then_inc(h_sq, 1)
            act.wait_ge(r_var, i + 1)
            nc.scalar.activation(hstd, var, ACT.Sqrt).then_inc(r_std, 1)
            act.wait_ge(x2T_ps, i + 1)
            for k in range(2):
                last = nc.scalar.activation(m.mT[:, 4 * k:4 * k + 4, i * P:(i + 1) * P],
                                            psum[:, 4 + k, :].rearrange("p (c t) -> p c t", c=4), ACT.Copy)
            last.then_inc(x2T_done, 1)

    @block.vector
    def _(dve):
        steps = Chain(dve, dve_did)
        nc.vector.tensor_scalar(m.lam[:, 7:8], m.col(C_GSUB), 1.0 - LAMBDA_INIT, None, ALU.mult).then_inc(gain_ready, 1)
        dve.wait_ge(gain_ready, 1)
        dve.wait_ge(o_sum, HEADS)
        for a, b in zip(columns_of(rB[0:HEADS, :]), (psum[0:HEADS, 0, :], psum[0:HEADS, 1, 0:P])):
            nc.vector.tensor_scalar(a, b, 1.0 / P, EPS, ALU.mult, ALU.add).then_inc(o_var, 1)
        dve.wait_ge(y_sum, 1)
        for a, b in zip(columns_of(muB), (psum[:, 2, :], psum[:, 3, 0:P])):
            steps.did(nc.vector.tensor_scalar(a, b, 1.0 / D, None, ALU.mult))
        dve.wait_ge(o_std, 1)
        nc.vector.reciprocal(rB[0:HEADS, :], std[0:HEADS, :]).then_inc(o_rstd, 1)
        steps.settled()
        for j in range(DT):
            nc.vector.tensor_tensor(m.yT[:, j, :], m.yT[:, j, :], muB, ALU.subtract).then_inc(y_centred, 1)
        for h in range(HEADS):
            dve.wait_ge(o_spread, h + 1)
            parts = zip(columns_of(m.oT[:, h, :]), (psum[:, 4 + 2 * (h % 2), :], psum[:, 5 + 2 * (h % 2), 0:P]))
            for a, b in parts:
                last = nc.vector.scalar_tensor_tensor(a, a, m.lam[:, 7:8], b, ALU.mult, ALU.mult)
            last.then_inc(o_ready, 1)
        dve.wait_ge(y_sq_sum, DT)
        for a, b in zip(columns_of(bR), (psum[:, 0, :], psum[:, 1, 0:P])):
            nc.vector.tensor_scalar(a, b, 1.0 / D, EPS, ALU.mult, ALU.add).then_inc(y_var, 1)
        dve.wait_ge(y_std, 1)
        steps.did(nc.vector.reciprocal(bR, bstd))
        steps.settled()
        for j in range(DT):
            nc.vector.tensor_tensor(m.yT[:, j, :], m.yT[:, j, :], bR, ALU.mult).then_inc(y_norm, 1)
        steps.restart()
        with dve.Fori(0, DT // 2) as c:
            for q in range(4):
                t = sets[q % 2]
                if q % 2 == 0:
                    dve.wait_ge(gp_done, 4 * c + q)
                dve.wait_ge(gate_ready, 4 * c + (q + 1))
                dst = (first, other)[q % 2]
                for a, g, b in zip(columns_of(dst), columns_of(sg[q % 2]), (psum[:, t[1], :], psum[:, t[2], P:2 * P])):
                    last = nc.vector.tensor_tensor(a, b, g, ALU.mult)
                if q % 2 == 0:
                    last.then_inc(gp_done, 1)
                else:
                    steps.did(last)
                    steps.settled()
                    nc.vector.tensor_tensor(m.mT[:, bass.ds(2 * c + q // 2, 1), :].rearrange("p a t -> p (a t)"), first, other,
                                            ALU.add).then_inc(gp_done, 1)
            steps.restart()
        dve.wait_ge(x_in, 16)
        for i in range(TILES):
            b = 2 * (i % 2)
            dve.wait_ge(h_ps, i + 1)
            nc.vector.tensor_tensor(m.h[:, i, :].rearrange("p (s n) -> p s n", s=2), m.h[:, i, :].rearrange("p (s n) -> p s n", s=2),
                                    psum[:, b:b + 2, :], ALU.add).then_inc(h_done, 1)
            dve.wait_ge(h_sq, i + 1)
            nc.vector.tensor_scalar(var, ss, 1.0 / D, EPS, ALU.mult, ALU.add).then_inc(r_var, 1)
            dve.wait_ge(r_std, i + 1)
            steps.did(nc.vector.reciprocal(rstd, hstd))
            steps.settled()
            nc.vector.scalar_tensor_tensor(m.xn2[:, i, :], m.h[:, i, :], rstd, m.rows[:, R_GFFN:R_GFFN + D], ALU.mult,
                                           ALU.mult).then_inc(xn2_ready, 1)


def score(nc, ctx, m, w_pq, sk_T):
    def sem(name):
        return ctx.enter_context(nc.semaphore(name))

    landed = [sem("pair_landed0"), sem("pair_landed1")]
    q_ps, q_copied, s_ps, s_copied = sem("q_ps"), sem("q_copied"), sem("s_ps"), sem("s_copied")
    q_sb = [m.work[:, s * TOK:(s + 1) * TOK] for s in range(2)]
    psum = m.psum

    block = ctx.enter_context(nc.Block())

    @block.sync
    def _(sp):
        def load(s, g):
            sp.dma_start(m.wu[s], by_channels(w_pq, g * P, P)).then_inc(landed[s], 16)
            sp.dma_start(m.wu[2 + s][:, 0, :], sk_T[bass.ds(g, 1)].rearrange("a p n -> (a p) n")).then_inc(landed[s], 16)

        for s in range(2):
            load(s, s)
        with sp.Fori(1, PH) as c:
            for s in range(2):
                sp.wait_ge(s_ps, 2 * c + (s - 1))
                load(s, 2 * c + s)

    @block.tensor
    def _(pe):
        def queries(c, s):
            pe.wait_ge(landed[s], 32 * c + 32)
            pe.wait_ge(q_copied, 2 * c + s) if s else pe.wait_ge(q_copied, 2 * c)
            for k in range(DT):
                a, b = columns_of(m.mT[:, k, :])
                nc.tensor.matmul(psum[:, 2 * s, :], m.wu[s][:, k, :], a, start=(k == 0), stop=(k == DT - 1))
                last = nc.tensor.matmul(psum[:, 2 * s + 1, 0:P], m.wu[s][:, k, :], b, start=(k == 0), stop=(k == DT - 1))
            last.then_inc(q_ps, 1)

        def scores(c, s):
            pe.wait_ge(q_copied, 2 * c + (s + 1))
            if s == 0:
                pe.wait_ge(s_copied, 2 * c)
            for i in range(TILES):
                last = nc.tensor.matmul(psum[:, 4 + 2 * s + i // 4, (i % 4) * P:(i % 4 + 1) * P], q_sb[s][:, i * P:(i + 1) * P],
                                        m.wu[2 + s][:, 0, :], start=True, stop=True)
            last.then_inc(s_ps, 1)

        with pe.Fori(0, PH) as c:
            for s in range(2):
                queries(c, s)
                scores(c, s)

    @block.scalar
    def _(act):
        with act.Fori(0, PH) as c:
            for s in range(2):
                act.wait_ge(q_ps, 2 * c + (s + 1))
                a, b = columns_of(q_sb[s])
                nc.scalar.activation(a, psum[:, 2 * s, :], ACT.Copy)
                nc.scalar.activation(b, psum[:, 2 * s + 1, 0:P], ACT.Copy).then_inc(q_copied, 1)

    @block.vector
    def _(dve):
        with dve.Fori(0, PH) as c:
            for s in range(2):
                dve.wait_ge(s_ps, 2 * c + (s + 1))
                pair = m.scores_ig[:, :, bass.ds(2 * c + s, 1), :].rearrange("p i a k -> p i (a k)")
                nc.vector.tensor_copy(pair[:, 0:4, :], psum[:, 4 + 2 * s, :].rearrange("p (i k) -> p i k", i=4))
                nc.vector.tensor_copy(pair[:, 4, :], psum[:, 5 + 2 * s, 0:P]).then_inc(s_copied, 1)


def retrieve(nc, ctx, m, exp_u, exp_v, y_p, y_s):
    def sem(name):
        return ctx.enter_context(nc.semaphore(name))

    sc_copied, xs_copied = sem("sc_copied"), sem("xs_copied")
    idx_ready, best_ready, exp_ready = sem("idx_ready"), sem("best_ready"), sem("gate_exp_ready")
    u_landed = [sem(f"u_landed{s}") for s in range(U_RING)]
    v_landed = [sem(f"v_landed{s}") for s in range(V_RING)]
    dots, acted, w_ready, diag_ready, v_used = sem("dots"), sem("acted"), sem("w_ready"), sem("diag_ready"), sem("v_used")
    y_done, y_stored = sem("y_done"), sem("y_stored")
    dve_did = sem("dve_did6")

    work, psum, small = m.work, m.psum, m.small
    STEPS = TILES * PH
    urow = [m.slab_w[:, s * D:(s + 1) * D] for s in range(U_RING)]
    vrow = [m.slab_u[:, s * D:(s + 1) * D] for s in range(V_RING)]
    junk = [m.slab_u[:, (V_RING + k) * D:(V_RING + k + 1) * D] for k in range(2)]
    xs = m.slab_u[:, (V_RING + 2) * D:(V_RING + 3) * D]
    sc = [work[:, s * 256:(s + 1) * 256].rearrange("p (h k) -> p h k", h=2) for s in range(2)]
    sr = [work[:, 512:640], work[:, 2560:2688]]
    cand, cand2 = work[:, 640:896], work[:, 896:1152]
    eq = [work[:, 1152 + 256 * k:1408 + 256 * k].rearrange("p (k a) -> p k a", k=TOPK) for k in range(2)]
    diag = [work[:, 1664 + P * k:1664 + P * (k + 1)] for k in range(4)]
    tv = work[:, 2176:2208].rearrange("p (h a) -> p h a", h=2)
    bs = [work[:, 2208 + 16 * k:2224 + 16 * k] for k in range(2)]
    ex = [work[:, 2240 + 16 * k:2256 + 16 * k] for k in range(2)]
    ij = [work[:, 2272 + 16 * k:2288 + 16 * k] for k in range(2)]
    a_dot = [work[:, 2304 + 16 * k:2320 + 16 * k] for k in range(2)]
    a_act = [work[:, 2336 + 16 * k:2352 + 16 * k] for k in range(2)]
    wt = [work[:, 2368 + 16 * k:2384 + 16 * k] for k in range(2)]
    words = work[:, 2400:2400 + 160].bitcast(U32)
    ti = words[:, 0:32].rearrange("p (h a) -> p h a", h=2)
    bj, ab = words[:, 32:48], [words[:, 48:64], words[:, 64:80]]
    idx = [words[:, 80 + 16 * k:96 + 16 * k] for k in range(4)]
    nb, esum, er = [small[:, 16 + 4 * k:20 + 4 * k] for k in range(3)]
    iota16 = m.rows[:, R_IOTA:R_IOTA + TOPK]

    block = ctx.enter_context(nc.Block())

    @block.gpsimd
    def _(pool):
        passed = pool.alloc_register("passed")
        pool.reg_mov(passed, 0)

        def gather(dst, table, index, done):
            pool.reg_alu(passed, passed, 1, ALU.bitwise_xor)
            nc.gpsimd.indirect_dma_start(out=dst, out_offset=None, in_=table,
                                         in_offset=bass.IndirectOffsetOnAxis(ap=index, axis=0)).then_inc(done, 16)

        def step(c, h, last):
            for k in range(TOPK):
                if not (isinstance(c, int) and PH * TOPK * c + TOPK * h + k < V_RING):
                    pool.wait_ge(v_used, PH * TOPK * c + (TOPK * h + k - V_RING + 1))
                gather(vrow[k % V_RING], exp_v, idx[h % 4][:, k:k + 1], v_landed[k % V_RING])
                if not last:
                    if k == 0:
                        pool.wait_ge(idx_ready, PH * c + (h + 2))
                    pool.wait_ge(dots, PH * TOPK * c + (TOPK * (h + 1) + k - U_RING + 1))
                    gather(urow[k % U_RING], exp_u, idx[(h + 1) % 4][:, k:k + 1], u_landed[k % U_RING])

        pool.wait_ge(idx_ready, 1)
        for k in range(TOPK):
            if k >= U_RING:
                pool.wait_ge(dots, k - U_RING + 1)
            gather(urow[k % U_RING], exp_u, idx[0][:, k:k + 1], u_landed[k % U_RING])
        for h in range(PH):
            step(0, h, False)
        with pool.Fori(1, TILES - 1) as c:
            for h in range(PH):
                step(c, h, False)
        for h in range(PH):
            step(TILES - 1, h, h == PH - 1)
        pool.wait_ge(idx_ready, pool.snap(passed))

    @block.sync
    def _(sp):
        with sp.Fori(0, PT) as i:
            sp.wait_ge(y_done, i + 1)
            sp.dma_start(y_p[bass.ds(i * P, P), :], m.h[:, bass.ds(i, 1), :].rearrange("p a n -> p (a n)")).then_inc(y_stored, 16)
        sp.wait_ge(y_done, TILES)
        sp.dma_start(y_s, m.h[:, PT, :]).then_inc(y_stored, 16)
        sp.wait_ge(y_stored, 16 * TILES)

    def over_tiles(eng, step):
        for h in range(PH):
            step(0, h)
        with eng.Fori(1, TILES - 1) as c:
            for h in range(PH):
                step(c, h)
        for h in range(PH):
            step(TILES - 1, h)

    def exists(c, h, ahead):
        return not isinstance(c, int) or PH * c + h + ahead < STEPS

    @block.tensor
    def _(pe):
        def step(c, h):
            for k in range(TOPK):
                pe.wait_ge(diag_ready, PH * TOPK * c + (TOPK * h + k + 1))
                pe.wait_ge(v_landed[k % V_RING], 16 * PH * TOPK // V_RING * c + 16 * (TOPK // V_RING * h + k // V_RING + 1))
                if h == 0 and k == 0:
                    pe.wait_ge(y_done, c)
                for s in range(2):
                    last = nc.tensor.matmul(psum[:, s, :], diag[k % 4], vrow[k % V_RING][:, s * 512:(s + 1) * 512],
                                            start=(h == 0 and k == 0), stop=(h == PH - 1 and k == TOPK - 1))
                last.then_inc(v_used, 1)

        over_tiles(pe, step)

    @block.scalar
    def _(act):
        def copy_scores(n, s):
            nc.scalar.activation(sc[s], m.scores[:, bass.ds(n, 1), :].rearrange("p a (h k) -> p (a h) k", h=2),
                                 ACT.Copy).then_inc(sc_copied, 1)

        def exps(n, s):
            act.wait_ge(best_ready, n + 1)
            nc.scalar.activation(ex[s], bs[s], ACT.Exp, bias=nb[:, s:s + 1], accum_out=esum[:, s:s + 1]).then_inc(exp_ready, 1)

        def step(c, h):
            s = h % 2
            if exists(c, h, 2):
                copy_scores(PH * c + (h + 2), s)
            if exists(c, h, 1):
                exps(PH * c + (h + 1), 1 - s)
            act.wait_ge(dots, PH * TOPK * c + TOPK * (h + 1))
            nc.scalar.activation(a_act[s], a_dot[s], ACT.Gelu_apprx_tanh).then_inc(acted, 1)
            if h == PH - 1 and exists(c, h, 1):
                copy_rows(c + 1)
            act.wait_ge(w_ready, PH * c + (h + 1))
            for k in range(TOPK):
                if not (isinstance(c, int) and PH * TOPK * c + TOPK * h + k < 4):
                    act.wait_ge(v_used, PH * TOPK * c + (TOPK * h + k - 3))
                nc.scalar.activation(diag[k % 4], m.ident[:, :], ACT.Copy, scale=wt[s][:, k:k + 1]).then_inc(diag_ready, 1)

        def copy_rows(c):
            nc.scalar.activation(xs, m.xn2[:, bass.ds(c, 1), :].rearrange("p a n -> p (a n)"), ACT.Copy).then_inc(xs_copied, 1)

        copy_scores(0, 0)
        copy_scores(1, 1)
        exps(0, 0)
        copy_rows(0)
        over_tiles(act, step)

    @block.vector
    def _(dve):
        steps = Chain(dve, dve_did)

        def top(n, q):
            s = q % 2
            did, settled = steps.did, steps.settled
            dve.wait_ge(sc_copied, n + 1)
            nc.vector.memset(er[:, 2:3], 0.0)
            for k in range(2):
                did(nc.vector.max(tv[:, k, 0:8], sc[s][:, k, :]))
            settled()
            for k in range(2):
                did(nc.vector.max_index(ti[:, k, 0:8], tv[:, k, 0:8], sc[s][:, k, :]))
                did(nc.vector.match_replace(sr[k], tv[:, k, 0:8], sc[s][:, k, :], NEG))
            settled()
            for k in range(2):
                did(nc.vector.max(tv[:, k, 8:16], sr[k]))
            settled()
            for k in range(2):
                did(nc.vector.max_index(ti[:, k, 8:16], tv[:, k, 8:16], sr[k]))
            did(nc.vector.tensor_tensor(cand.rearrange("p (a b) -> p a b", a=TOPK), tv[:, 0, :, None].to_broadcast([P, TOPK, TOPK]),
                                        tv[:, 1:2, :].to_broadcast([P, TOPK, TOPK]), ALU.add))
            settled()
            did(nc.vector.max(bs[s][:, 0:8], cand))
            settled()
            did(nc.vector.max_index(bj[:, 0:8], bs[s][:, 0:8], cand))
            did(nc.vector.match_replace(cand2, bs[s][:, 0:8], cand, NEG))
            settled()
            did(nc.vector.max(bs[s][:, 8:16], cand2))
            settled()
            did(nc.vector.max_index(bj[:, 8:16], bs[s][:, 8:16], cand2))
            nc.vector.tensor_scalar(nb[:, s:s + 1], bs[s][:, 0:1], -1.0, None, ALU.mult).then_inc(best_ready, 1)
            settled()
            did(nc.vector.tensor_scalar(ab[0], bj, 4, None, ALU.logical_shift_right))
            did(nc.vector.tensor_scalar(ab[1], bj, TOPK - 1, None, ALU.bitwise_and))
            settled()
            for k in range(2):
                did(nc.vector.tensor_tensor(eq[k], ab[k][:, :, None].to_broadcast([P, TOPK, TOPK]),
                                            iota16[:, None, :].to_broadcast([P, TOPK, TOPK]), ALU.is_equal))
            settled()
            for k in range(2):
                did(nc.vector.tensor_tensor(eq[k], eq[k], ti[:, k:k + 1, :].to_broadcast([P, TOPK, TOPK]), ALU.mult))
            settled()
            for k in range(2):
                did(nc.vector.tensor_reduce(ij[k], eq[k], AX_X, ALU.add))
            settled()
            nc.vector.scalar_tensor_tensor(idx[q], ij[0], float(NKEYS), ij[1], ALU.mult, ALU.add).then_inc(idx_ready, 1)

        def result(c):
            tile = m.h[:, bass.ds(c, 1), :].rearrange("p a (s n) -> p (a s) n", s=2)
            nc.vector.tensor_tensor(tile, tile, psum[:, 0:2, :], ALU.add).then_inc(y_done, 1)

        def step(c, h):
            s = h % 2
            if exists(c, h, 1):
                top(PH * c + (h + 1), (h + 1) % 4)
            if h == 0:
                dve.wait_ge(xs_copied, c + 1)
            for k in range(TOPK):
                dve.wait_ge(u_landed[k % U_RING], 16 * PH * TOPK // U_RING * c + 16 * (TOPK // U_RING * h + k // U_RING + 1))
                if not (isinstance(c, int) and PH * TOPK * c + TOPK * h + k < 2):
                    dve.wait_ge(dots, PH * TOPK * c + (TOPK * h + k - 1))
                nc.vector.tensor_tensor_reduce(junk[k % 2], urow[k % U_RING], xs, 1.0, 0.0, ALU.mult, ALU.add,
                                               a_dot[s][:, k:k + 1]).then_inc(dots, 1)
            if h == 0 and not (isinstance(c, int) and c == 0):
                dve.wait_ge(v_used, PH * TOPK * c)
                result(c - 1)
            dve.wait_ge(exp_ready, PH * c + (h + 1))
            steps.did(nc.vector.reciprocal(er[:, s:s + 1], esum[:, s:s + 1]))
            steps.settled()
            dve.wait_ge(acted, PH * c + (h + 1))
            nc.vector.scalar_tensor_tensor(wt[s], ex[s], er[:, s:s + 1], a_act[s], ALU.mult, ALU.mult).then_inc(w_ready, 1)
            steps.restart()

        top(0, 0)
        steps.restart()
        over_tiles(dve, step)
        dve.wait_ge(v_used, STEPS * TOPK)
        result(TILES - 1)


def program(nc, x, xT, w_in, cols_d, rows_d, ident_d, ck_T, cv, cc_T, w_ao, w_co, w_out, w_pq, sk_T, exp_u, exp_v,
            y_p, y_s, k_p, v_p, c_p, k_s, v_s, c_s):
    with ExitStack() as memory:
        m = Memory(nc, memory)
        for stage, args in ((project, (xT, w_in, cols_d, rows_d, ident_d, cc_T, k_p, k_s, v_p, v_s, c_p, c_s)),
                            (attend, (ck_T, cv, v_s)),
                            (merge, (x, w_in, w_ao, w_co, w_out)),
                            (score, (w_pq, sk_T)),
                            (retrieve, (exp_u, exp_v, y_p, y_s))):
            with ExitStack() as ctx:
                stage(nc, ctx, m, *args)


def lay_out(inp):
    import numpy as np

    c = np.ascontiguousarray
    f = np.float32
    x = np.concatenate([inp["x_prompt"].reshape(PROMPT, D), inp["x_sample"].reshape(STREAMS * NEW, D)])
    by_column = lambda a: a.reshape(-1, P).T
    m = (np.arange(P) // NEW % 2).astype(f)[:, None]
    sel = np.zeros((P, 2 * HEADS - 1), f)
    sel[:, HEADS - 1] = 1
    cols = np.concatenate([by_column(inp[n][0]) for n in ("g_mix", "b_gate", "b_dw", "g_cln", "b_cln", "g_ffn", "g_sub")]
                          + [m, 1 - m, sel, inp["w_dw"][0].reshape(TAPS, DT, P).transpose(2, 1, 0).reshape(P, DT * TAPS)], axis=1)
    row = np.concatenate([inp[n][0] for n in ("g_qn", "g_kn", "lam_q1", "lam_k1", "lam_q2", "lam_k2")]
                         + [np.arange(TOPK, dtype=f), inp["g_ffn"][0]])
    return {
        "x": c(x), "xT": c(x.T), "w_in": c(inp["w_in"][0]), "cols": c(cols), "rows": c(np.broadcast_to(row, (P, row.size))),
        "ident": np.eye(P, dtype=f),
        "ck_T": c(inp["cache_k"][0].reshape(STREAMS, PAST, HEADS, P).transpose(0, 3, 2, 1).reshape(STREAMS, P, D)),
        "cv": c(inp["cache_v"][0].reshape(STREAMS, PAST, D)),
        "cc_T": c(inp["cache_conv"][0].reshape(STREAMS, HIST, DT, P).transpose(2, 3, 0, 1)),
        "w_ao": c(inp["w_attn_out"][0]), "w_co": c(inp["w_conv_out"][0]), "w_out": c(inp["w_out"][0]), "w_pq": c(inp["w_pq"][0]),
        "sk_T": c(inp["sub_keys"][0].reshape(2 * PH, NKEYS, P).transpose(0, 2, 1)),
        "exp_u": c(inp["expert_u"][0]), "exp_v": c(inp["expert_v"][0]),
    }


def kernel(**inputs):
    import numpy as np
    from concourse import bacc
    from concourse.bass_utils import run_bass_kernel_spmd

    nc = bacc.Bacc("TRN2", target_bir_lowering=False, num_devices=1)
    arrays = {f"in_{n}": a for n, a in lay_out({n: np.asarray(a) for n, a in inputs.items()}).items()}
    args = [nc.dram_tensor(n, a.shape, mybir.dt.from_np(a.dtype), kind="ExternalInput").ap() for n, a in arrays.items()]
    shapes = [(PROMPT, D), (STREAMS * NEW, D), (PROMPT, D), (PROMPT, D), (DT, P, HIST), (STREAMS * NEW, D), (STREAMS * NEW, D),
              (DT, P, STREAMS, HIST)]
    outs = [nc.dram_tensor(f"out_{i}_dram", s, F32, kind="ExternalOutput").ap() for i, s in enumerate(shapes)]
    program(nc, *args, *outs)
    r = run_bass_kernel_spmd(nc, [arrays], core_ids=[0]).results[0]
    y_p, y_s, k_p, v_p, c_p, k_s, v_s, c_s = [r[f"out_{i}_dram"] for i in range(len(shapes))]
    return (y_p.reshape(1, PROMPT, D), y_s.reshape(STREAMS, NEW, D),
            k_p.reshape(1, 1, PROMPT, HEADS, 2, DH), v_p.reshape(1, 1, PROMPT, HEADS, P),
            c_p.reshape(D, HIST).T.reshape(1, 1, HIST, D),
            k_s.reshape(1, STREAMS, NEW, HEADS, 2, DH), v_s.reshape(1, STREAMS, NEW, HEADS, P),
            c_s.reshape(D, STREAMS, HIST).transpose(1, 2, 0).reshape(1, STREAMS, HIST, D))
```

```python
import math
from contextlib import ExitStack

import concourse.bass as bass
from concourse import mybir

ALU = mybir.AluOpType
ACT = mybir.ActivationFunctionType
AX_X = mybir.AxisListType.X
F32 = mybir.dt.float32
U32 = mybir.dt.uint32

P = 128
D = 1024
DT = D // P
PROMPT = 512
TOK = 640
TILES = TOK // P
PT = PROMPT // P
CHUNK = 64
HEADS = 8
DH = 64
STREAMS = 8
NEW = 16
PAST = 128
TAPS = 31
HIST = TAPS - 1
EPS = 1e-6
NEG = -1e30
SCALE = DH ** -0.5
LAMBDA_INIT = 0.8 - 0.6 * math.exp(-0.3 * 0)
K_COL, V_COL, C_COL, G_COL = D, 2 * D, 3 * D, 5 * D
WCH = 256
PH = 8
TOPK = 16
NKEYS = 128
U_RING = 8
V_RING = 4
U_LEN = HIST + PROMPT + STREAMS * (HIST + NEW)
US = HIST + PROMPT

C_GMIX, C_BGATE, C_BDW, C_GCLN, C_BCLN, C_GFFN, C_GSUB = 0, 8, 24, 32, 40, 48, 56
C_M, C_NM, C_SEL, C_DW = 57, 58, 59, 59 + 2 * HEADS - 1
COLS = C_DW + DT * TAPS
R_GQ, R_GK, R_LAM, R_IOTA, R_GFFN = 0, DH, 2 * DH, 6 * DH, 6 * DH + TOPK
ROWS = R_GFFN + D


class Chain:

    def __init__(self, eng, sem):
        self.eng, self.sem, self.n = eng, sem, 0

    def did(self, instruction):
        self.n += 1
        instruction.then_inc(self.sem, 1)

    def settled(self):
        self.eng.wait_ge(self.sem, self.n)

    def restart(self):
        self.settled()
        self.eng.sem_clear(self.sem)
        self.n = 0




class Memory:

    def __init__(self, nc, ctx):
        def sb(name, shape, dt=F32):
            return ctx.enter_context(nc.sbuf_tensor(name, shape, dt))

        slab_a = sb("slab_a", [P, DT * TOK])
        slab_d = sb("slab_d", [P, DT * TOK])
        slab_e = sb("slab_e", [P, DT * TOK])
        slab_qk = sb("slab_qk", [P, 2 * DT * TOK])
        slab_u = sb("slab_u", [P, DT * U_LEN])
        self.slab_u = slab_u
        self.slab_w = slab_w = sb("slab_w", [P, 9216])
        self.work = sb("work", [P, 8192])
        self.cols = cols = sb("cols", [P, COLS])
        self.rows = sb("rows", [P, ROWS])
        self.ident = sb("ident", [P, P])
        self.ones = sb("ones", [P, P])
        self.lam = sb("lam", [P, 16])
        self.small = sb("small", [P, 64])
        self.psum = ctx.enter_context(nc.psum_tensor("psum", [P, 8, 512], F32))

        channels = lambda s: s[:, :].rearrange("p (c t) -> p c t", c=DT)
        tiles = lambda s: s[:, :].rearrange("p (i n) -> p i n", i=TILES)
        self.xnT, self.h = channels(slab_a), tiles(slab_a)
        self.v, self.mT = tiles(slab_d), channels(slab_d)
        self.oT, self.xn2 = channels(slab_e), tiles(slab_e)
        self.qkT = slab_qk[:, :].rearrange("p (g t) -> p g t", g=2 * HEADS)
        self.scores = slab_qk[:, :].rearrange("p (n k) -> p n k", k=2 * NKEYS)
        self.scores_ig = slab_qk[:, :].rearrange("p (i g k) -> p i g k", i=TILES, g=2 * PH)
        self.uT = slab_u[:, :].rearrange("p (c t) -> p c t", c=DT)
        self.yT = self.uT[:, :, 0:TOK]
        self.acc_s = self.work[:, 7168:8192].rearrange("p (c n q) -> p c n q", c=DT, n=STREAMS)
        self.wk = [slab_w[:, s * DT * WCH:(s + 1) * DT * WCH].rearrange("p (c n) -> p c n", c=DT) for s in range(2)]
        self.wu = [slab_w[:, s * D:(s + 1) * D].rearrange("p (c n) -> p c n", c=DT) for s in range(8)]
        self.wo = [slab_w[:, s * 4 * D:(s + 1) * 4 * D].rearrange("p (c n) -> p c n", c=DT) for s in range(2)]
        self.w_dw = cols[:, C_DW:C_DW + DT * TAPS].rearrange("p (c k) -> p c k", c=DT)

    def col(self, c, j=0):
        return self.cols[:, bass.ds(c + j, 1)]


def by_channels(w, c0, n):
    return w.rearrange("(c p) n -> p c n", p=P)[:, :, bass.ds(c0, n)]


def columns_of(t):
    return t[:, 0:PROMPT], t[:, PROMPT:TOK]


def tile_columns(place):
    i = (place - 1) % TILES
    return slice(i * P, (i + 1) * P)


def project(nc, ctx, m, xT, w_in, cols_d, rows_d, ident_d, cc_T, k_p, k_s, v_p, v_s, c_p, c_s):
    def sem(name):
        return ctx.enter_context(nc.semaphore(name))

    consts_in, xT_in, hist_in = sem("consts_in"), sem("xT_in"), sem("hist_in")
    w_landed = [sem("w_landed0"), sem("w_landed1")]
    ones_set, hist_zero = sem("ones_set"), sem("hist_zero")
    sq_ready, sq_used = sem("sq_ready"), sem("sq_used")
    var_ready, std_ready, xnT_ready = sem("var_ready"), sem("std_ready"), sem("xnT_ready")
    z_ps, z_sq, z_var, z_std, z_ready = [sem(n) for n in ("z_ps", "z_sq", "z_var", "z_std", "z_ready")]
    zT_ps, zT_free = sem("zT_ps"), sem("zT_free")
    k_stored = [sem("k_stored0"), sem("k_stored1")]
    v_stored, c_stored = sem("v_stored"), sem("c_stored")
    glu_ps, gate_ready, u_ready = sem("glu_ps"), sem("gate_ready"), sem("u_ready")
    s_tap, tap, acc_free = sem("s_tap"), sem("tap1"), sem("acc_free")
    dve_did = sem("dve_did1")

    work, psum, xnT, uT, wk = m.work, m.psum, m.xnT, m.uT, m.wk
    sq = [work[:, s * TOK:(s + 1) * TOK] for s in range(2)]
    rB, std = work[:, 1280:1920], work[:, 1920:2560]
    zq = [work[:, 2560 + s * WCH:2560 + (s + 1) * WCH] for s in range(2)]
    zs = [work[:, 3072 + s * WCH:3072 + (s + 1) * WCH] for s in range(2)]
    zg = work[:, 3584:3584 + WCH]
    acc = work[:, 5120:5120 + PROMPT]
    product = work[:, 5632:5632 + D].rearrange("p (c n q) -> p c n q", c=DT, n=STREAMS)
    sg = [work[:, 3840 + s * TOK:3840 + (s + 1) * TOK] for s in range(2)]
    zsum, zvar, zstd, zr = [m.small[:, 4 * k:4 * k + 4] for k in range(4)]
    NCH = 3 * D // WCH
    QK = 2 * D // WCH
    groups = lambda a: a.rearrange("p (g d) -> p g d", d=DH)
    glu = [(0, 1, 2), (3, 4, 7)]

    block = ctx.enter_context(nc.Block())

    @block.sync
    def _(sp):
        sp.dma_start(m.cols[:, :], cols_d).then_inc(consts_in, 16)
        sp.dma_start(m.rows[:, :], rows_d).then_inc(consts_in, 16)
        sp.dma_start(m.ident[:, :], ident_d).then_inc(consts_in, 16)
        sp.dma_start(xnT, xT.rearrange("(c p) t -> p c t", p=P)).then_inc(xT_in, 16)
        for s in range(2):
            for part in range(2):
                sp.dma_start(wk[s][:, :, part * P:(part + 1) * P],
                             by_channels(w_in, C_COL + part * D + s * P, P)).then_inc(w_landed[s], 16)
        for j in range(DT):
            sp.dma_start(uT[:, j, US:].rearrange("p (b t) -> p b t", b=STREAMS)[:, :, 0:HIST],
                         cc_T[j]).then_inc(hist_in, 16)
        with sp.Fori(1, DT // 2) as c:
            for s in range(2):
                sp.wait_ge(glu_ps, 2 * c + s - 1)
                for part in range(2):
                    sp.dma_start(wk[s][:, :, part * P:(part + 1) * P],
                                 by_channels(w_in, 2 * P * c + (C_COL + part * D + s * P), P)).then_inc(w_landed[s], 16)
        for s in range(2):
            sp.wait_ge(glu_ps, DT - 1 + s)
            sp.dma_start(wk[s], by_channels(w_in, s * WCH, WCH)).then_inc(w_landed[s], 16)
        with sp.Fori(1, NCH // 2) as c:
            for s in range(2):
                sp.wait_ge(z_ps, 2 * TILES * c + TILES * (s - 1))
                sp.dma_start(wk[s], by_channels(w_in, 2 * WCH * c + s * WCH, WCH)).then_inc(w_landed[s], 16)

    @block.gpsimd
    def _(pool):
        nc.gpsimd.memset(m.ones[:, :], 1.0).then_inc(ones_set, 1)
        nc.gpsimd.memset(uT[:, :, 0:HIST], 0.0).then_inc(hist_zero, 1)
        nc.gpsimd.memset(acc, 0.0).then_inc(acc_free, 1)
        pool.wait_ge(u_ready, DT)
        pool.wait_ge(hist_in, 16 * DT)
        for j in range(DT):
            pool.dma_start(c_p[j], uT[:, j, US - HIST:US]).then_inc(c_stored, 16)
            pool.dma_start(c_s[j], uT[:, j, US:].rearrange("p (b t) -> p b t", b=STREAMS)[:, :, NEW:]).then_inc(c_stored, 16)
        streams = uT[:, :, US:].rearrange("p c (n t) -> p c n t", n=STREAMS)
        for k in range(TAPS):
            w = m.w_dw[:, :, k:k + 1, None].to_broadcast([P, DT, STREAMS, NEW])
            if k == 0:
                nc.gpsimd.tensor_tensor(m.acc_s, streams[:, :, :, 0:NEW], w, ALU.mult).then_inc(s_tap, 1)
            else:
                nc.gpsimd.tensor_tensor(product, streams[:, :, :, k:k + NEW], w, ALU.mult).then_inc(s_tap, 1)
                pool.wait_ge(s_tap, 2 * k)
                nc.gpsimd.tensor_tensor(m.acc_s, m.acc_s, product, ALU.add).then_inc(s_tap, 1)
                pool.wait_ge(s_tap, 2 * k + 1)
        pool.wait_ge(z_ready, TILES * NCH)
        pool.dma_start(v_p.rearrange("(i p) n -> p i n", p=P), m.v[:, 0:PT, :]).then_inc(v_stored, 16)
        pool.dma_start(v_s, m.v[:, PT, :]).then_inc(v_stored, 16)
        pool.wait_ge(k_stored[0], 16 * TILES * QK // 4)
        pool.wait_ge(k_stored[1], 16 * TILES * QK // 4)
        pool.wait_ge(v_stored, 32)
        pool.wait_ge(c_stored, 32 * DT)

    @block.tensor
    def _(pe):
        pe.wait_ge(ones_set, 1)
        pe.wait_ge(consts_in, 48)
        for c in range(DT):
            pe.wait_ge(sq_ready, c + 1)
            a, b = columns_of(sq[c % 2])
            nc.tensor.matmul(psum[:, 0, :], m.ones[:, :], a, start=(c == 0), stop=(c == DT - 1))
            nc.tensor.matmul(psum[:, 1, 0:P], m.ones[:, :], b, start=(c == 0), stop=(c == DT - 1)).then_inc(sq_used, 1)
        pe.wait_ge(xnT_ready, DT)

        def products(s, i):
            for c in range(DT):
                last = nc.tensor.matmul(psum[:, i, 0:WCH], xnT[:, c, i * P:(i + 1) * P], wk[s][:, c, :],
                                        start=(c == 0), stop=(c == DT - 1))
            last.then_inc(z_ps, 1)

        def turn(c, n, first):
            pe.wait_ge(z_ready, 2 * TILES * c + (n + 1))
            if not first or n >= 2:
                pe.wait_ge(zT_free, 2 * TILES * c + (n - 1))
            for g in range(2):
                last = nc.tensor.transpose(psum[:, 5 + n % 2, g * P:(g + 1) * P], zq[n % 2][:, g * P:(g + 1) * P],
                                           m.ident[:, :])
            last.then_inc(zT_ps, 1)

        def qk_body(c, first):
            for n in range(2 * TILES):
                s, i = divmod(n, TILES)
                if i == 0:
                    pe.wait_ge(w_landed[s], 16 * c + (16 * DT + 16))
                if not first or n >= TILES:
                    pe.wait_ge(z_ready, 2 * TILES * c + (n - TILES + 1))
                products(s, i)
                if n >= 1:
                    turn(c, n - 1, first)
            turn(c, 2 * TILES - 1, first)

        def glu_body(c, first):
            for s in range(2):
                pe.wait_ge(w_landed[s], 32 * c + 32)
                if not first:
                    pe.wait_ge(u_ready, 2 * c + (s - 1))
                for part in range(2):
                    for k in range(DT):
                        w = wk[s][:, k, part * P:(part + 1) * P]
                        nc.tensor.matmul(psum[:, glu[s][part], :], w, xnT[:, k, 0:PROMPT],
                                         start=(k == 0), stop=(k == DT - 1))
                        last = nc.tensor.matmul(psum[:, glu[s][2], part * P:(part + 1) * P], w, xnT[:, k, PROMPT:TOK],
                                                start=(k == 0), stop=(k == DT - 1))
                last.then_inc(glu_ps, 1)

        glu_body(0, True)
        with pe.Fori(1, DT // 2) as c:
            glu_body(c, False)
        pe.wait_ge(u_ready, DT)
        qk_body(0, True)
        with pe.Fori(1, QK // 2) as c:
            qk_body(c, False)
        with pe.Fori(QK // 2, NCH // 2) as c:
            for n in range(2 * TILES):
                s, i = divmod(n, TILES)
                if i == 0:
                    pe.wait_ge(w_landed[s], 16 * c + (16 * DT + 16))
                pe.wait_ge(z_ready, 2 * TILES * c + (n - TILES + 1))
                products(s, i)

    @block.scalar
    def _(act):
        act.wait_ge(xT_in, 16)
        for c in range(DT):
            if c >= 2:
                act.wait_ge(sq_used, c - 1)
            nc.scalar.activation(sq[c % 2], xnT[:, c, :], ACT.Square).then_inc(sq_ready, 1)
        act.wait_ge(var_ready, 2)
        nc.scalar.activation(std, rB, ACT.Sqrt).then_inc(std_ready, 1)

        def gates(c, s, first):
            act.wait_ge(glu_ps, 2 * c + (s + 1))
            if not first:
                act.wait_ge(u_ready, 2 * c + (s - 1))
            nc.scalar.activation(sg[s][:, 0:PROMPT], psum[:, glu[s][1], :], ACT.Sigmoid)
            nc.scalar.activation(sg[s][:, PROMPT:TOK], psum[:, glu[s][2], P:2 * P], ACT.Sigmoid).then_inc(gate_ready, 1)

        for s in range(2):
            gates(0, s, True)
        with act.Fori(1, DT // 2) as c:
            for s in range(2):
                gates(c, s, False)

        def conv_out(j):
            act.wait_ge(tap, TAPS * j + TAPS)
            nc.scalar.activation(m.yT[:, bass.ds(j, 1), 0:PROMPT].rearrange("p a t -> p (a t)"), acc, ACT.Identity,
                                 bias=m.col(C_BDW, j)).then_inc(acc_free, 1)

        def turned(c, n):
            s, i = divmod(n, TILES)
            act.wait_ge(zT_ps, 2 * TILES * c + (n + 1))
            nc.scalar.activation(m.qkT[:, bass.ds(4 * c + 2 * s, 2), i * P:(i + 1) * P],
                                 psum[:, 5 + n % 2, 0:WCH].rearrange("p (g t) -> p g t", g=2), ACT.Copy).then_inc(zT_free, 1)

        def store(c, n):
            s, i = divmod(n, TILES)
            act.wait_ge(z_ready, 2 * TILES * c + (n + 1))
            col = bass.ds(2 * WCH * c + (s * WCH - D), WCH)
            dst = k_p[i * P:(i + 1) * P, col] if i < PT else k_s[:, col]
            act.dma_start(dst, zq[n % 2]).then_inc(k_stored[n % 2], 16)

        for kind in range(2):
            with act.Fori(kind * QK // 4, (kind + 1) * QK // 4) as c:
                for n in range(2 * TILES):
                    i = n % TILES
                    act.wait_ge(z_ps, 2 * TILES * c + (n + 1))
                    if n >= 2:
                        act.wait_ge(z_ready, 2 * TILES * c + (n - 1))
                    nc.scalar.activation(zs[n % 2], psum[:, i, 0:WCH], ACT.Square).then_inc(z_sq, 1)
                    act.wait_ge(z_var, 2 * TILES * c + (n + 1))
                    nc.scalar.activation(zstd, zvar, ACT.Sqrt).then_inc(z_std, 1)
                    if n >= 1:
                        if kind == 1:
                            store(c, n - 1)
                        turned(c, n - 1)
                if kind == 1:
                    store(c, 2 * TILES - 1)
                turned(c, 2 * TILES - 1)
                conv_out(c)

    @block.vector
    def _(dve):
        steps = Chain(dve, dve_did)
        dve.wait_ge(consts_in, 48)
        lam = m.lam
        for k in range(2):
            a = m.rows[:, R_LAM + 2 * k * DH:R_LAM + (2 * k + 1) * DH]
            b = m.rows[:, R_LAM + (2 * k + 1) * DH:R_LAM + (2 * k + 2) * DH]
            steps.did(nc.vector.tensor_tensor(zg[:, k * DH:(k + 1) * DH], a, b, ALU.mult))
        steps.settled()
        steps.did(nc.vector.tensor_reduce(lam[:, 0:2], zg[:, 0:2 * DH].rearrange("p (k d) -> p k d", k=2), AX_X, ALU.add))
        steps.settled()
        dve.wait_ge(sq_used, DT)
        for (a, b) in zip(columns_of(rB), (psum[:, 0, :], psum[:, 1, 0:P])):
            nc.vector.tensor_scalar(a, b, 1.0 / D, EPS, ALU.mult, ALU.add).then_inc(var_ready, 1)
        dve.wait_ge(std_ready, 1)
        steps.did(nc.vector.reciprocal(rB, std))
        steps.settled()
        for c in range(DT):
            nc.vector.scalar_tensor_tensor(xnT[:, c, :], xnT[:, c, :], m.col(C_GMIX + c), rB, ALU.mult, ALU.mult).then_inc(xnT_ready, 1)
        with dve.Fori(0, DT // 2) as c:
            for s in range(2):
                dve.wait_ge(gate_ready, 2 * c + (s + 1))
                nc.vector.tensor_tensor(uT[:, bass.ds(2 * c + s, 1), HIST:US].rearrange("p a t -> p (a t)"),
                                        psum[:, glu[s][0], :], sg[s][:, 0:PROMPT], ALU.mult)
                streams = uT[:, bass.ds(2 * c + s, 1), US:].rearrange("p a (b t) -> p (a b) t", b=STREAMS)[:, :, HIST:]
                nc.vector.tensor_tensor(streams, psum[:, glu[s][2], 0:P].rearrange("p (b t) -> p b t", b=STREAMS),
                                        sg[s][:, PROMPT:TOK].rearrange("p (b t) -> p b t", b=STREAMS),
                                        ALU.mult).then_inc(u_ready, 1)

        dve.wait_ge(hist_zero, 1)

        def taps(c, n):
            for k in range(n * TAPS // (2 * TILES), (n + 1) * TAPS // (2 * TILES)):
                w = m.w_dw[:, bass.ds(c, 1), k:k + 1].rearrange("p a k -> p (a k)")
                u = uT[:, bass.ds(c, 1), k:k + PROMPT].rearrange("p a t -> p (a t)")
                if k == 0:
                    dve.wait_ge(acc_free, c + 1)
                    nc.vector.tensor_scalar(acc, u, w, None, ALU.mult).then_inc(tap, 1)
                else:
                    dve.wait_ge(tap, TAPS * c + k)
                    nc.vector.scalar_tensor_tensor(acc, u, w, acc, ALU.mult, ALU.add).then_inc(tap, 1)

        for kind in range(2):
            gain = m.rows[:, R_GQ + kind * DH:R_GQ + (kind + 1) * DH]
            steps.restart()
            with dve.Fori(kind * QK // 4, (kind + 1) * QK // 4) as c:
                for n in range(2 * TILES):
                    i = n % TILES
                    dve.wait_ge(z_sq, 2 * TILES * c + (n + 1))
                    steps.did(nc.vector.tensor_reduce(zsum, groups(zs[n % 2]), AX_X, ALU.add))
                    steps.settled()
                    nc.vector.tensor_scalar(zvar, zsum, 1.0 / DH, EPS, ALU.mult, ALU.add).then_inc(z_var, 1)
                    steps.did(nc.vector.tensor_tensor(groups(zg), groups(psum[:, i, 0:WCH]),
                                                      gain[:, None, :].to_broadcast([P, 4, DH]), ALU.mult))
                    dve.wait_ge(z_std, 2 * TILES * c + (n + 1))
                    steps.did(nc.vector.reciprocal(zr, zstd))
                    steps.settled()
                    if n >= 2:
                        dve.wait_ge(zT_ps, 2 * TILES * c + (n - 1))
                    if kind == 1:
                        dve.wait_ge(k_stored[n % 2], 16 * TILES * c + 16 * (n // 2) - 16 * TILES * QK // 4)
                    nc.vector.tensor_tensor(groups(zq[n % 2]), groups(zg),
                                            zr[:, :, None].to_broadcast([P, 4, DH]), ALU.mult).then_inc(z_ready, 1)
                    taps(c, n)
                steps.restart()
        with dve.Fori(QK // 2, NCH // 2) as c:
            for n in range(2 * TILES):
                s, i = divmod(n, TILES)
                dve.wait_ge(z_ps, 2 * TILES * c + (n + 1))
                nc.vector.tensor_copy(m.v[:, i, bass.ds(2 * WCH * c + (s * WCH - 2 * D), WCH)],
                                      psum[:, i, 0:WCH]).then_inc(z_ready, 1)


def attend(nc, ctx, m, ck_T, cv, v_s):
    def sem(name):
        return ctx.enter_context(nc.semaphore(name))

    cache_in = [sem("cache_in0"), sem("cache_in1")]
    laid = sem("laid")
    bd_zero, bd_ready, lam_exp, lam_ready = sem("bd_zero"), sem("bd_ready"), sem("lam_exp"), sem("lam_ready")
    names = ("logits", "max_ready", "exp_ready", "probs", "probsT_ps", "probsT", "out_ps", "out_done")
    s_ps, s_max, s_exp, s_prob, s_pT, s_pTs, s_out, s_done = [sem("s_" + n) for n in names]
    p_ps, p_max, p_exp, p_prob, p_pT, p_pTs, p_out, p_done = [sem("p_" + n) for n in names]
    masked, head_ready = sem("masked"), sem("head_ready")
    tap, acc_free = sem("tap"), sem("acc_free2")
    dve_did = sem("dve_did2")

    work, psum, slab_w, small = m.work, m.psum, m.slab_w, m.small
    T = PAST + NEW
    UNIT = HEADS // 2
    ckT = [slab_w[:, s * 3072:s * 3072 + 1024].rearrange("p (h t) -> p h t", h=HEADS) for s in range(2)]
    cvv = [slab_w[:, s * 3072 + 1024:s * 3072 + 2048].rearrange("p (h e) -> p h e", h=HEADS) for s in range(2)]
    vnew = [slab_w[0:NEW, s * 3072 + 2048:s * 3072 + 3072].rearrange("p (h e) -> p h e", h=HEADS) for s in range(2)]
    HB = 6144
    qh = [slab_w[:, HB + s * 1536:HB + s * 1536 + 512] for s in range(2)]
    kh = [slab_w[:, HB + s * 1536 + 512:HB + s * 1536 + 1024] for s in range(2)]
    vh = [slab_w[:, HB + s * 1536 + 1024:HB + s * 1536 + 1536].rearrange("p (i e) -> p i e", i=PT) for s in range(2)]
    probs = [work[:, s * 1024:(s + 1) * 1024].rearrange("p (m k) -> p m k", m=2) for s in range(2)]
    diff = [work[:, 2048 + s * 512:2560 + s * 512] for s in range(2)]
    second = work[:, 3072:3584]
    diffT = [work[:, 3584 + s * 512:4096 + s * 512] for s in range(2)]
    acc = work[:, 4608:4608 + PROMPT]
    sp_probs = [work[:, 5248 + s * T:5248 + (s + 1) * T] for s in range(2)]
    bd = [work[:, 5536 + s * 256:5792 + s * 256] for s in range(2)]
    kn = [work[:, 6048 + s * P:6176 + s * P].rearrange("p (h q) -> p h q", h=HEADS) for s in range(2)]
    sprobsT = [work[:, 6304 + s * 256:6560 + s * 256] for s in range(2)]
    mx = [small[:, 16 + 4 * s:18 + 4 * s] for s in range(2)]
    nmx = [small[:, 24 + 4 * s:26 + 4 * s] for s in range(2)]
    den = [small[:, 32 + 4 * s:34 + 4 * s] for s in range(2)]
    rden = [small[:, 40 + 4 * s:42 + 4 * s] for s in range(2)]
    minus_lam, row_sign = m.lam[:, 4:5], m.lam[:, 5:6]
    LU = 4
    U = 2 * PT
    s_mx, s_nmx, s_den = [[small[:, 48 + 2 * k + s:49 + 2 * k + s] for s in range(2)] for k in range(3)]
    s_rden = [small[:, 54 + 2 * s:56 + 2 * s] for s in range(2)]
    s_lg, s_T, s_Tn, s_o = psum[:, 7, 0:T], psum[:, 7, 144:272], psum[0:NEW, 7, 272:400], psum[:, 7, 400:464]
    bdv = lambda s: bd[s].rearrange("p (h m q) -> p h m q", h=HEADS, m=2)

    ROUNDS = HEADS // 2

    def exists(c, u, per_round=U):
        return not isinstance(c, int) or 0 <= per_round * c + u < per_round * ROUNDS

    def over_rounds(eng, step):
        for u in range(U):
            step(0, u)
        with eng.Fori(1, ROUNDS - 1) as c:
            for u in range(U):
                step(c, u)
        for u in range(U + 3):
            step(ROUNDS - 1, u)

    block = ctx.enter_context(nc.Block())

    @block.sync
    def _(sp):
        def load(s, b):
            sp.dma_start(slab_w[:, s * 3072:s * 3072 + 1024], ck_T[bass.ds(b, 1)].rearrange("a p n -> (a p) n")).then_inc(cache_in[s], 16)
            sp.dma_start(slab_w[:, s * 3072 + 1024:s * 3072 + 2048], cv[bass.ds(b, 1)].rearrange("a p n -> (a p) n")).then_inc(cache_in[s], 16)
            sp.dma_start(slab_w[0:NEW, s * 3072 + 2048:s * 3072 + 3072], v_s[bass.ds(b * NEW, NEW), :]).then_inc(cache_in[s], 16)

        for s in range(2):
            load(s, s)
        with sp.Fori(1, STREAMS // 2) as c:
            for s in range(2):
                sp.wait_ge(s_out, LU * c + (2 * s - 2))
                load(s, 2 * c + s)

    @block.gpsimd
    def _(pool):
        nc.gpsimd.memset(acc, 0.0).then_inc(acc_free, 1)
        for s in range(2):
            nc.gpsimd.memset(bd[s], 0.0).then_inc(bd_zero, 1)
        pool.wait_ge(bd_zero, 2)

        def lay(s, b):
            new = bass.ds(b * NEW + PROMPT, NEW)
            for k in range(2):
                rows = slice(k * DH, (k + 1) * DH)
                nc.gpsimd.tensor_copy(bdv(s)[rows, :, k, :], m.qkT[rows, 0:HEADS, new]).then_inc(laid, 1)
                pool.wait_ge(laid, 2 * b + (k + 1))
            nc.gpsimd.tensor_copy(kn[s], m.qkT[:, HEADS:, new]).then_inc(bd_ready, 1)

        def head(s, h):
            nc.gpsimd.tensor_copy(qh[s], m.qkT[:, bass.ds(h, 1), 0:PROMPT].rearrange("p a t -> p (a t)"))
            nc.gpsimd.tensor_copy(kh[s], m.qkT[:, bass.ds(h + HEADS, 1), 0:PROMPT].rearrange("p a t -> p (a t)"))
            nc.gpsimd.tensor_copy(vh[s], m.v[:, 0:PT, bass.ds(h * P, P)]).then_inc(head_ready, 1)

        for s in range(2):
            lay(s, s)
            head(s, s)
        with pool.Fori(1, HEADS // 2) as c:
            for s in range(2):
                pool.wait_ge(s_ps, LU * c + (2 * s - 2))
                lay(s, 2 * c + s)
                pool.wait_ge(p_out, U * c + PT * (s - 1))
                head(s, 2 * c + s)

    @block.tensor
    def _(pe):
        def stream_logits(c, v):
            s, g = v // 2 % 2, v % 2
            if g == 0:
                pe.wait_ge(cache_in[s], 48 * c + 48 * (v // LU + 1))
                pe.wait_ge(bd_ready, 2 * c + (v // 2 + 1))
            if exists(c, v - 1, LU):
                pe.wait_ge(s_done, LU * c + v)
            for k in range(UNIT):
                h = g * UNIT + k
                out = s_lg[32 * k:32 * k + 32, :]
                lhsT = bd[s][:, 32 * h:32 * h + 32]
                nc.tensor.matmul(out[:, 0:PAST], lhsT, ckT[s][:, h, :], start=True, stop=True)
                last = nc.tensor.matmul(out[:, PAST:T], lhsT, kn[s][:, h, :], start=True, stop=True)
            last.then_inc(s_ps, 1)

        def stream_turn(c, v):
            pe.wait_ge(s_prob, LU * c + (v + 1))
            nc.tensor.transpose(s_T, sp_probs[v % 2][:, 0:PAST], m.ident[:, :])
            nc.tensor.transpose(s_Tn, sp_probs[v % 2][:, PAST:T], m.ident[:, :]).then_inc(s_pT, 1)

        def stream_values(c, v):
            s, g = v // 2 % 2, v % 2
            pe.wait_ge(s_pTs, LU * c + (v + 1))
            for k in range(UNIT):
                h = g * UNIT + k
                out = s_o[:, k * NEW:(k + 1) * NEW]
                for j in range(2):
                    a = 32 * k + NEW * j
                    nc.tensor.matmul(out, cvv[s][:, h, :], sprobsT[v % 2][:, a:a + NEW], start=(j == 0), stop=False)
                    last = nc.tensor.matmul(out, vnew[s][:, h, :], sprobsT[v % 2][0:NEW, P + a:P + a + NEW],
                                            start=False, stop=(j == 1))
            last.then_inc(s_out, 1)

        def logits(c, u):
            s, i = u // PT % 2, u % PT
            n = (i + 1) * P
            if i == 0:
                pe.wait_ge(head_ready, 2 * c + (u // PT + 1))
            if exists(c, u - 2):
                pe.wait_ge(p_exp, U * c + (u - 1))
            for j in range(2):
                rows = slice(j * DH, (j + 1) * DH)
                last = nc.tensor.matmul(psum[:, 2 * (u % 2) + j, 0:n], qh[s][rows, i * P:(i + 1) * P], kh[s][rows, 0:n],
                                        start=True, stop=True)
            last.then_inc(p_ps, 1)

        def turn(c, u):
            pe.wait_ge(p_prob, U * c + (u + 1))
            if exists(c, u - 2):
                pe.wait_ge(p_pTs, U * c + (u - 1))
            for k in range(u % PT + 1):
                last = nc.tensor.transpose(psum[:, 4 + u % 2, k * P:(k + 1) * P], diff[u % 2][:, k * P:(k + 1) * P], m.ident[:, :])
            last.then_inc(p_pT, 1)

        def values(c, u):
            s, i = u // PT % 2, u % PT
            pe.wait_ge(p_pTs, U * c + (u + 1))
            if i == 0 and exists(c, u - 1):
                pe.wait_ge(p_done, 2 * c + u // PT)
            for k in range(i + 1):
                last = nc.tensor.matmul(psum[:, 6, i * P:(i + 1) * P], vh[s][:, k, :], diffT[u % 2][:, k * P:(k + 1) * P],
                                        start=(k == 0), stop=(k == i))
            last.then_inc(p_out, 1)

        def step(c, u):
            v = u // 2
            if exists(c, u):
                logits(c, u)
            if exists(c, u - 2):
                turn(c, u - 2)
            if u % 2 == 0 and exists(c, v - 1, LU):
                stream_values(c, v - 1)
            if exists(c, u - 3):
                values(c, u - 3)
            if exists(c, u):
                (stream_turn if u % 2 else stream_logits)(c, v)

        over_rounds(pe, step)

    @block.scalar
    def _(act):
        nc.scalar.activation(m.lam[:, 2:4], m.lam[:, 0:2], ACT.Exp).then_inc(lam_exp, 1)

        def stream_exp(c, v):
            act.wait_ge(s_max, LU * c + (v + 1))
            if exists(c, v - 2, LU):
                act.wait_ge(s_pT, LU * c + (v - 1))
            nc.scalar.activation(sp_probs[v % 2], s_lg, ACT.Exp, bias=s_nmx[v % 2], scale=SCALE,
                                 accum_out=s_den[v % 2]).then_inc(s_exp, 1)

        def stream_copy(c, v):
            act.wait_ge(s_pT, LU * c + (v + 1))
            if exists(c, v - 2, LU):
                act.wait_ge(s_out, LU * c + (v - 1))
            nc.scalar.activation(sprobsT[v % 2][:, 0:P], s_T, ACT.Copy)
            nc.scalar.activation(sprobsT[v % 2][0:NEW, P:2 * P], s_Tn, ACT.Copy).then_inc(s_pTs, 1)

        def stream_out(c, v):
            g = v % 2
            act.wait_ge(s_out, LU * c + (v + 1))
            nc.scalar.activation(m.oT[:, g * UNIT:(g + 1) * UNIT, bass.ds(2 * NEW * c + (PROMPT + NEW * (v // 2)), NEW)],
                                 s_o.rearrange("p (h q) -> p h q", h=UNIT), ACT.Copy).then_inc(s_done, 1)

        def exps(c, u):
            n = (u % PT + 1) * P
            act.wait_ge(p_max, U * c + (u + 1))
            if exists(c, u - 2):
                act.wait_ge(p_prob, U * c + (u - 1))
            for j in range(2):
                last = nc.scalar.activation(probs[u % 2][:, j, 0:n], psum[:, 2 * (u % 2) + j, 0:n], ACT.Exp,
                                            bias=nmx[u % 2][:, j:j + 1], scale=SCALE, accum_out=den[u % 2][:, j:j + 1])
            last.then_inc(p_exp, 1)

        def copy(c, u):
            n = (u % PT + 1) * P
            act.wait_ge(p_pT, U * c + (u + 1))
            if exists(c, u - 2):
                act.wait_ge(p_out, U * c + (u - 1))
            nc.scalar.activation(diffT[u % 2][:, 0:n], psum[:, 4 + u % 2, 0:n], ACT.Copy).then_inc(p_pTs, 1)

        def out(c, u):
            act.wait_ge(p_out, U * c + (u + 1))
            nc.scalar.activation(m.oT[:, bass.ds(2 * c + u // PT, 1), 0:PROMPT].rearrange("p a t -> p (a t)"), psum[:, 6, :],
                                 ACT.Copy).then_inc(p_done, 1)

        def streams_out(j):
            nc.scalar.activation(m.yT[:, bass.ds(j, 1), PROMPT:TOK].rearrange("p a (n q) -> p (a n) q", n=STREAMS),
                                 m.acc_s[:, bass.ds(j, 1)].rearrange("p a n q -> p (a n) q"), ACT.Identity, bias=m.col(C_BDW, j))

        def conv_out(c):
            act.wait_ge(tap, TAPS * c + TAPS)
            nc.scalar.activation(m.yT[:, bass.ds(c + DT // 2, 1), 0:PROMPT].rearrange("p a t -> p (a t)"), acc, ACT.Identity,
                                 bias=m.col(C_BDW, c + DT // 2)).then_inc(acc_free, 1)
            streams_out(c + DT // 2)

        def step(c, u):
            v = u // 2
            if exists(c, u):
                exps(c, u)
            if exists(c, u - 2):
                copy(c, u - 2)
            if u % 2 == 0 and exists(c, v - 1, LU):
                stream_out(c, v - 1)
            if exists(c, u):
                (stream_copy if u % 2 else stream_exp)(c, v)
            if u % PT == PT - 2 and exists(c, u - 3):
                out(c, u - 3)
            if u == PT:
                streams_out(c)
            if u == U - 1:
                conv_out(c)

        over_rounds(act, step)

    @block.vector
    def _(dve):
        steps = Chain(dve, dve_did)
        lam = m.lam
        dve.wait_ge(lam_exp, 1)
        steps.did(nc.vector.tensor_scalar(lam[:, 6:7], lam[:, 3:4], -LAMBDA_INIT, None, ALU.add))
        steps.settled()
        steps.did(nc.vector.tensor_tensor(minus_lam, lam[:, 6:7], lam[:, 2:3], ALU.subtract))
        steps.settled()
        steps.did(nc.vector.scalar_tensor_tensor(row_sign, m.col(C_M), minus_lam, m.col(C_NM), ALU.mult, ALU.add))
        steps.restart()

        def stream_max(c, u):
            dve.wait_ge(s_ps, LU * c + (u + 1))
            steps.did(nc.vector.reduce_max(s_mx[u % 2], s_lg, AX_X))
            steps.settled()
            nc.vector.tensor_scalar(s_nmx[u % 2], s_mx[u % 2], -SCALE, None, ALU.mult).then_inc(s_max, 1)

        def stream_scale(c, u):
            dve.wait_ge(s_exp, LU * c + (u + 1))
            steps.did(nc.vector.reciprocal(s_rden[u % 2][:, 0:1], s_den[u % 2]))
            steps.settled()
            steps.did(nc.vector.tensor_scalar(s_rden[u % 2][:, 1:2], s_rden[u % 2][:, 0:1], row_sign, None, ALU.mult))
            steps.settled()
            nc.vector.tensor_scalar(sp_probs[u % 2], sp_probs[u % 2], s_rden[u % 2][:, 1:2], None, ALU.mult).then_inc(s_prob, 1)

        def maxima(c, u):
            n = (u % PT + 1) * P
            b = 2 * (u % 2)
            dve.wait_ge(p_ps, U * c + (u + 1))
            nc.vector.memset(psum[0:CHUNK, b:b + 2, n - CHUNK:n], NEG).then_inc(masked, 1)
            dve.wait_ge(masked, U * c + (u + 1))
            steps.did(nc.vector.reduce_max(mx[u % 2], psum[:, b:b + 2, 0:n], AX_X))
            steps.settled()
            nc.vector.tensor_scalar(nmx[u % 2], mx[u % 2], -SCALE, None, ALU.mult).then_inc(p_max, 1)

        def combine(c, u):
            n = (u % PT + 1) * P
            dve.wait_ge(p_exp, U * c + (u + 1))
            steps.did(nc.vector.reciprocal(rden[u % 2], den[u % 2]))
            steps.settled()
            steps.did(nc.vector.tensor_scalar(second[:, 0:n], probs[u % 2][:, 1, 0:n], rden[u % 2][:, 1:2], minus_lam,
                                              ALU.mult, ALU.mult))
            steps.settled()
            if exists(c, u - 2):
                dve.wait_ge(p_pT, U * c + (u - 1))
            nc.vector.scalar_tensor_tensor(diff[u % 2][:, 0:n], probs[u % 2][:, 0, 0:n], rden[u % 2][:, 0:1], second[:, 0:n],
                                           ALU.mult, ALU.add).then_inc(p_prob, 1)

        def taps(c, u):
            for k in range(u * TAPS // U, (u + 1) * TAPS // U):
                w = m.w_dw[:, bass.ds(c + DT // 2, 1), k:k + 1].rearrange("p a k -> p (a k)")
                row = m.uT[:, bass.ds(c + DT // 2, 1), k:k + PROMPT].rearrange("p a t -> p (a t)")
                if k == 0:
                    dve.wait_ge(acc_free, c + 1)
                    nc.vector.tensor_scalar(acc, row, w, None, ALU.mult).then_inc(tap, 1)
                else:
                    dve.wait_ge(tap, TAPS * c + k)
                    nc.vector.scalar_tensor_tensor(acc, row, w, acc, ALU.mult, ALU.add).then_inc(tap, 1)

        def step(c, u):
            if exists(c, u):
                maxima(c, u)
            if exists(c, u - 1):
                combine(c, u - 1)
            if exists(c, u):
                if u % 2 == 1:
                    stream_scale(c, u // 2)
                taps(c, u)
                if u % 2 == 0:
                    stream_max(c, u // 2)
                if u == U - 1:
                    steps.restart()

        over_rounds(dve, step)
        steps.settled()


def merge(nc, ctx, m, x, w_in, w_ao, w_co, w_out):
    def sem(name):
        return ctx.enter_context(nc.semaphore(name))

    w_landed = [sem(f"unit_landed{s}") for s in range(4)]
    wo_landed, x_in = [sem("wo_landed0"), sem("wo_landed1")], sem("x_in")
    o_sq, o_sum, o_var, o_std, o_rstd, o_spread, o_ready = [sem("o_" + n) for n in ("sq", "sum", "var", "std", "rstd", "spread", "ready")]
    y_sum, y_centred, y_sq, y_sq_sum, y_var, y_std, y_norm, y_ready = [
        sem("y_" + n) for n in ("sum", "centred", "sq", "sq_sum", "var", "std", "norm", "ready")]
    gp_ps, gate_ready, gp_done = sem("gp_ps"), sem("mgate_ready"), sem("gp_done")
    h_ps, h_done, h_sq, r_std, xn2_ready, x2T_ps, x2T_done = [sem(n) for n in ("h_ps", "h_done", "h_sq", "r_std", "xn2_ready", "x2T_ps", "x2T_done")]
    r_var, gain_ready = sem("r_var"), sem("gain_ready")
    dve_did = sem("dve_did3")

    work, psum = m.work, m.psum
    sq = [work[:, s * TOK:(s + 1) * TOK] for s in range(2)]
    rB, std, muB, bR, bstd = [work[:, (2 + k) * TOK:(3 + k) * TOK] for k in range(5)]
    sg = [work[:, (7 + k) * TOK:(8 + k) * TOK] for k in range(2)]
    first = work[:, 9 * TOK:10 * TOK]
    other = work[:, 10 * TOK:11 * TOK]
    hsq = work[:, 0:D]
    ss, var, hstd, rstd = [m.small[:, 16 + 2 * k:17 + 2 * k] for k in range(4)]
    sets = [(0, 1, 2), (3, 4, 5)]

    block = ctx.enter_context(nc.Block())

    @block.sync
    def _(sp):
        def unit(q, j):
            br = q % 2
            sp.dma_start(m.wu[2 * q], by_channels(w_in, j * P + (G_COL + br * D), P)).then_inc(w_landed[q], 16)
            sp.dma_start(m.wu[2 * q + 1], by_channels((w_ao, w_co)[br], j * P, P)).then_inc(w_landed[q], 16)

        for q in range(4):
            unit(q, q // 2)
        with sp.Fori(1, DT // 2) as c:
            for q in range(4):
                sp.wait_ge(gp_ps, 4 * c + (q - 3))
                unit(q, 2 * c + q // 2)
        sp.wait_ge(gp_ps, 2 * DT)
        for s in range(2):
            sp.dma_start(m.wo[s], by_channels(w_out, s * 512, 512)).then_inc(wo_landed[s], 16)
        sp.dma_start(m.h[:, 0, :], x[PROMPT:TOK, :]).then_inc(x_in, 16)
        sp.dma_start(m.h[:, 1:, :], x[0:PROMPT, :].rearrange("(i p) n -> p i n", p=P)).then_inc(x_in, 16)

    @block.tensor
    def _(pe):
        for h in range(HEADS):
            pe.wait_ge(o_sq, h + 1)
            sel = m.cols[:, C_SEL + HEADS - 1 - h:C_SEL + 2 * HEADS - 1 - h]
            a, b = columns_of(sq[h % 2])
            nc.tensor.matmul(psum[0:HEADS, 0, :], sel, a, start=(h == 0), stop=(h == HEADS - 1))
            nc.tensor.matmul(psum[0:HEADS, 1, 0:P], sel, b, start=(h == 0), stop=(h == HEADS - 1)).then_inc(o_sum, 1)
        for j in range(DT):
            a, b = columns_of(m.yT[:, j, :])
            nc.tensor.matmul(psum[:, 2, :], m.ones[:, :], a, start=(j == 0), stop=(j == DT - 1))
            last = nc.tensor.matmul(psum[:, 3, 0:P], m.ones[:, :], b, start=(j == 0), stop=(j == DT - 1))
        last.then_inc(y_sum, 1)
        pe.wait_ge(o_rstd, 1)
        for h in range(HEADS):
            if h >= 2:
                pe.wait_ge(o_ready, h - 1)
            sel = m.ident[0:HEADS, h:h + 1].to_broadcast([HEADS, P])
            a, b = columns_of(rB[0:HEADS, :])
            nc.tensor.matmul(psum[:, 4 + 2 * (h % 2), :], sel, a, start=True, stop=True)
            nc.tensor.matmul(psum[:, 5 + 2 * (h % 2), 0:P], sel, b, start=True, stop=True).then_inc(o_spread, 1)
        pe.wait_ge(o_var, 2)
        for j in range(DT):
            pe.wait_ge(y_sq, j + 1)
            a, b = columns_of(sq[j % 2])
            nc.tensor.matmul(psum[:, 0, :], m.ones[:, :], a, start=(j == 0), stop=(j == DT - 1))
            nc.tensor.matmul(psum[:, 1, 0:P], m.ones[:, :], b, start=(j == 0), stop=(j == DT - 1)).then_inc(y_sq_sum, 1)
        pe.wait_ge(y_ready, DT)
        pe.wait_ge(o_ready, HEADS)
        with pe.Fori(0, DT // 2) as c:
            for q in range(4):
                t = sets[q % 2]
                pe.wait_ge(w_landed[q], 32 * c + 32)
                if q >= 2:
                    pe.wait_ge(gp_done, 4 * c + (q - 1))
                elif q == 0:
                    pe.wait_ge(gp_done, 4 * c)
                for part, rhs in enumerate((m.xnT, (m.oT, m.yT)[q % 2])):
                    for k in range(DT):
                        a, b = columns_of(rhs[:, k, :])
                        w = m.wu[2 * q + part][:, k, :]
                        nc.tensor.matmul(psum[:, t[part], :], w, a, start=(k == 0), stop=(k == DT - 1))
                        last = nc.tensor.matmul(psum[:, t[2], part * P:(part + 1) * P], w, b, start=(k == 0), stop=(k == DT - 1))
                last.then_inc(gp_ps, 1)
        pe.wait_ge(gp_done, 2 * DT)

        def turn(i):
            pe.wait_ge(xn2_ready, i + 1)
            if i >= 1:
                pe.wait_ge(x2T_done, i)
            for k in range(DT):
                last = nc.tensor.transpose(psum[:, 4 + k // 4, (k % 4) * P:(k % 4 + 1) * P], m.xn2[:, i, k * P:(k + 1) * P], m.ident[:, :])
            last.then_inc(x2T_ps, 1)

        for i in range(TILES):
            b = 2 * (i % 2)
            if i >= 2:
                pe.wait_ge(h_done, i - 1)
            for s in range(2):
                pe.wait_ge(wo_landed[s], 16)
                for k in range(DT):
                    last = nc.tensor.matmul(psum[:, b + s, :], m.mT[:, k, tile_columns(i)], m.wo[s][:, k, :],
                                            start=(k == 0), stop=(k == DT - 1))
            last.then_inc(h_ps, 1)
            if i >= 1:
                turn(i - 1)
        turn(TILES - 1)

    @block.scalar
    def _(act):
        for h in range(HEADS):
            if h >= 2:
                act.wait_ge(o_sum, h - 1)
            nc.scalar.activation(sq[h % 2], m.oT[:, h, :], ACT.Square).then_inc(o_sq, 1)
        act.wait_ge(o_var, 2)
        nc.scalar.activation(std[0:HEADS, :], rB[0:HEADS, :], ACT.Sqrt).then_inc(o_std, 1)
        act.wait_ge(o_sum, HEADS)
        for j in range(DT):
            act.wait_ge(y_centred, j + 1)
            if j >= 2:
                act.wait_ge(y_sq_sum, j - 1)
            nc.scalar.activation(sq[j % 2], m.yT[:, j, :], ACT.Square).then_inc(y_sq, 1)
        act.wait_ge(y_var, 2)
        nc.scalar.activation(bstd, bR, ACT.Sqrt).then_inc(y_std, 1)
        for j in range(DT):
            act.wait_ge(y_norm, j + 1)
            nc.scalar.activation(m.yT[:, j, :], m.yT[:, j, :], ACT.Silu, bias=m.col(C_BCLN + j), scale=m.col(C_GCLN + j)).then_inc(y_ready, 1)
        with act.Fori(0, DT // 2) as c:
            for q in range(4):
                t = sets[q % 2]
                act.wait_ge(gp_ps, 4 * c + (q + 1))
                if q >= 2:
                    act.wait_ge(gp_done, 4 * c + (q - 1))
                bias = m.col(C_BGATE + DT * (q % 2) + q // 2, 2 * c)
                a, b = columns_of(sg[q % 2])
                nc.scalar.activation(a, psum[:, t[0], :], ACT.Sigmoid, bias=bias)
                nc.scalar.activation(b, psum[:, t[2], 0:P], ACT.Sigmoid, bias=bias).then_inc(gate_ready, 1)
        for i in range(TILES):
            act.wait_ge(h_done, i + 1)
            nc.scalar.activation(hsq, m.h[:, i, :], ACT.Square, accum_out=ss).then_inc(h_sq, 1)
            act.wait_ge(r_var, i + 1)
            nc.scalar.activation(hstd, var, ACT.Sqrt).then_inc(r_std, 1)
            act.wait_ge(x2T_ps, i + 1)
            for k in range(2):
                last = nc.scalar.activation(m.mT[:, 4 * k:4 * k + 4, tile_columns(i)],
                                            psum[:, 4 + k, :].rearrange("p (c t) -> p c t", c=4), ACT.Copy)
            last.then_inc(x2T_done, 1)

    @block.vector
    def _(dve):
        steps = Chain(dve, dve_did)
        nc.vector.tensor_scalar(m.lam[:, 7:8], m.col(C_GSUB), 1.0 - LAMBDA_INIT, None, ALU.mult).then_inc(gain_ready, 1)
        dve.wait_ge(gain_ready, 1)
        dve.wait_ge(o_sum, HEADS)
        for a, b in zip(columns_of(rB[0:HEADS, :]), (psum[0:HEADS, 0, :], psum[0:HEADS, 1, 0:P])):
            nc.vector.tensor_scalar(a, b, 1.0 / P, EPS, ALU.mult, ALU.add).then_inc(o_var, 1)
        dve.wait_ge(y_sum, 1)
        for a, b in zip(columns_of(muB), (psum[:, 2, :], psum[:, 3, 0:P])):
            steps.did(nc.vector.tensor_scalar(a, b, 1.0 / D, None, ALU.mult))
        dve.wait_ge(o_std, 1)
        nc.vector.reciprocal(rB[0:HEADS, :], std[0:HEADS, :]).then_inc(o_rstd, 1)
        steps.settled()
        for j in range(DT):
            nc.vector.tensor_tensor(m.yT[:, j, :], m.yT[:, j, :], muB, ALU.subtract).then_inc(y_centred, 1)
        for h in range(HEADS):
            dve.wait_ge(o_spread, h + 1)
            parts = zip(columns_of(m.oT[:, h, :]), (psum[:, 4 + 2 * (h % 2), :], psum[:, 5 + 2 * (h % 2), 0:P]))
            for a, b in parts:
                last = nc.vector.scalar_tensor_tensor(a, a, m.lam[:, 7:8], b, ALU.mult, ALU.mult)
            last.then_inc(o_ready, 1)
        dve.wait_ge(y_sq_sum, DT)
        for a, b in zip(columns_of(bR), (psum[:, 0, :], psum[:, 1, 0:P])):
            nc.vector.tensor_scalar(a, b, 1.0 / D, EPS, ALU.mult, ALU.add).then_inc(y_var, 1)
        dve.wait_ge(y_std, 1)
        steps.did(nc.vector.reciprocal(bR, bstd))
        steps.settled()
        for j in range(DT):
            nc.vector.tensor_tensor(m.yT[:, j, :], m.yT[:, j, :], bR, ALU.mult).then_inc(y_norm, 1)
        steps.restart()
        with dve.Fori(0, DT // 2) as c:
            for q in range(4):
                t = sets[q % 2]
                if q % 2 == 0:
                    dve.wait_ge(gp_done, 4 * c + q)
                dve.wait_ge(gate_ready, 4 * c + (q + 1))
                dst = (first, other)[q % 2]
                for a, g, b in zip(columns_of(dst), columns_of(sg[q % 2]), (psum[:, t[1], :], psum[:, t[2], P:2 * P])):
                    last = nc.vector.tensor_tensor(a, b, g, ALU.mult)
                if q % 2 == 0:
                    last.then_inc(gp_done, 1)
                else:
                    steps.did(last)
                    steps.settled()
                    nc.vector.tensor_tensor(m.mT[:, bass.ds(2 * c + q // 2, 1), :].rearrange("p a t -> p (a t)"), first, other,
                                            ALU.add).then_inc(gp_done, 1)
            steps.restart()
        dve.wait_ge(x_in, 32)
        for i in range(TILES):
            b = 2 * (i % 2)
            dve.wait_ge(h_ps, i + 1)
            nc.vector.tensor_tensor(m.h[:, i, :].rearrange("p (s n) -> p s n", s=2), m.h[:, i, :].rearrange("p (s n) -> p s n", s=2),
                                    psum[:, b:b + 2, :], ALU.add).then_inc(h_done, 1)
            dve.wait_ge(h_sq, i + 1)
            nc.vector.tensor_scalar(var, ss, 1.0 / D, EPS, ALU.mult, ALU.add).then_inc(r_var, 1)
            dve.wait_ge(r_std, i + 1)
            steps.did(nc.vector.reciprocal(rstd, hstd))
            steps.settled()
            nc.vector.scalar_tensor_tensor(m.xn2[:, i, :], m.h[:, i, :], rstd, m.rows[:, R_GFFN:R_GFFN + D], ALU.mult,
                                           ALU.mult).then_inc(xn2_ready, 1)


def load_pair(sp, m, w_pq, sk_T, weights, keys, g, done):
    sp.dma_start(weights, by_channels(w_pq, g * P, P)).then_inc(done, 16)
    sp.dma_start(keys, sk_T[bass.ds(g, 1)].rearrange("a p n -> (a p) n")).then_inc(done, 16)


def score(nc, ctx, m, w_pq, sk_T):
    def sem(name):
        return ctx.enter_context(nc.semaphore(name))

    landed = [sem(f"pair_landed{s}") for s in range(4)]
    q_ps, q_copied, s_ps, s_copied = sem("q_ps"), sem("q_copied"), sem("s_ps"), sem("s_copied")
    q_sb = [m.work[:, s * P:(s + 1) * P] for s in range(4)]
    keys = [m.work[:, (4 + s) * P:(5 + s) * P] for s in range(4)]
    psum = m.psum

    block = ctx.enter_context(nc.Block())

    @block.sync
    def _(sp):
        for s in range(4):
            load_pair(sp, m, w_pq, sk_T, m.wu[s], keys[s], s, landed[s])
        with sp.Fori(1, PH // 2) as c:
            for s in range(4):
                sp.wait_ge(s_ps, 4 * c + (s - 3))
                load_pair(sp, m, w_pq, sk_T, m.wu[s], keys[s], 4 * c + s, landed[s])

    @block.tensor
    def _(pe):
        def queries(c, s, first):
            pe.wait_ge(landed[s], 32 * c + 32)
            if not first:
                pe.wait_ge(q_copied, 4 * c + (s - 3))
            for k in range(DT):
                last = nc.tensor.matmul(psum[:, s, 0:P], m.wu[s][:, k, :], m.mT[:, k, PROMPT:TOK], start=(k == 0), stop=(k == DT - 1))
            last.then_inc(q_ps, 1)

        def scores(c, s, first):
            pe.wait_ge(q_copied, 4 * c + (s + 1))
            if not first:
                pe.wait_ge(s_copied, 4 * c + (s - 3))
            nc.tensor.matmul(psum[:, 4 + s, 0:P], q_sb[s], keys[s], start=True, stop=True).then_inc(s_ps, 1)

        def four(c, first):
            for s in range(4):
                queries(c, s, first)
                if s >= 1:
                    scores(c, s - 1, first)
            scores(c, 3, first)

        four(0, True)
        with pe.Fori(1, PH // 2) as c:
            four(c, False)

    @block.scalar
    def _(act):
        with act.Fori(0, PH // 2) as c:
            for s in range(4):
                act.wait_ge(q_ps, 4 * c + (s + 1))
                nc.scalar.activation(q_sb[s], psum[:, s, 0:P], ACT.Copy).then_inc(q_copied, 1)

    @block.vector
    def _(dve):
        with dve.Fori(0, PH // 2) as c:
            for s in range(4):
                dve.wait_ge(s_ps, 4 * c + (s + 1))
                nc.vector.tensor_copy(m.scores_ig[:, 0, bass.ds(4 * c + s, 1), :].rearrange("p a k -> p (a k)"),
                                      psum[:, 4 + s, 0:P]).then_inc(s_copied, 1)


def retrieve(nc, ctx, m, w_pq, sk_T, exp_u, exp_v, y_p, y_s):
    def sem(name):
        return ctx.enter_context(nc.semaphore(name))

    sc_copied, xs_copied = sem("sc_copied"), sem("xs_copied")
    idx_ready, best_ready, exp_ready = sem("idx_ready"), sem("best_ready"), sem("gate_exp_ready")
    u_landed = [sem(f"u_landed{s}") for s in range(U_RING)]
    v_landed = [sem(f"v_landed{s}") for s in range(V_RING)]
    dots, acted, w_ready, diag_ready, v_used = sem("dots"), sem("acted"), sem("w_ready"), sem("diag_ready"), sem("v_used")
    y_done, y_stored = sem("y_done"), sem("y_stored")
    landed = [sem("pair_landed_p0"), sem("pair_landed_p1")]
    q_ps, q_copied, s_ps, s_copied = [sem(n) for n in ("pq_ps", "pq_copied", "ps_ps", "ps_copied")]
    dve_did = sem("dve_did6")

    work, psum, small = m.work, m.psum, m.small
    STEPS = TILES * PH
    urow = [m.slab_w[:, s * D:(s + 1) * D] for s in range(U_RING)]
    vrow = [m.slab_u[:, s * D:(s + 1) * D] for s in range(V_RING)]
    junk = [m.slab_u[:, (V_RING + k) * D:(V_RING + k + 1) * D] for k in range(2)]
    xs = m.slab_u[:, (V_RING + 2) * D:(V_RING + 3) * D]
    sc = [work[:, s * 256:(s + 1) * 256].rearrange("p (h k) -> p h k", h=2) for s in range(2)]
    sr = [work[:, 512:640], work[:, 2560:2688]]
    cand, cand2 = work[:, 640:896], work[:, 896:1152]
    eq = [work[:, 1152 + 256 * k:1408 + 256 * k].rearrange("p (k a) -> p k a", k=TOPK) for k in range(2)]
    diag = [work[:, 1664 + P * k:1664 + P * (k + 1)] for k in range(4)]
    tv = work[:, 2176:2208].rearrange("p (h a) -> p h a", h=2)
    bs = [work[:, 2208 + 16 * k:2224 + 16 * k] for k in range(2)]
    ex = [work[:, 2240 + 16 * k:2256 + 16 * k] for k in range(2)]
    ij = [work[:, 2272 + 16 * k:2288 + 16 * k] for k in range(2)]
    a_dot = [work[:, 2304 + 16 * k:2320 + 16 * k] for k in range(2)]
    a_act = [work[:, 2336 + 16 * k:2352 + 16 * k] for k in range(2)]
    wt = [work[:, 2368 + 16 * k:2384 + 16 * k] for k in range(2)]
    words = work[:, 2400:2400 + 160].bitcast(U32)
    ti = words[:, 0:32].rearrange("p (h a) -> p h a", h=2)
    bj, ab = words[:, 32:48], [words[:, 48:64], words[:, 64:80]]
    idx = [words[:, 80 + 16 * k:96 + 16 * k] for k in range(4)]
    nb, esum, er = [small[:, 16 + 4 * k:20 + 4 * k] for k in range(3)]
    iota16 = m.rows[:, R_IOTA:R_IOTA + TOPK]
    w_pair = [work[:, 2688 + s * D:2688 + (s + 1) * D].rearrange("p (c n) -> p c n", c=DT) for s in range(2)]
    keys = [work[:, 4736 + s * P:4864 + s * P] for s in range(2)]
    q_sb = [work[:, 4992 + s * PROMPT:4992 + (s + 1) * PROMPT] for s in range(2)]

    Q_AT = (DT + 2, 1)

    block = ctx.enter_context(nc.Block())

    @block.gpsimd
    def _(pool):
        passed = pool.alloc_register("passed")
        pool.reg_mov(passed, 0)

        def gather(dst, table, index, done):
            pool.reg_alu(passed, passed, 1, ALU.bitwise_xor)
            nc.gpsimd.indirect_dma_start(out=dst, out_offset=None, in_=table,
                                         in_offset=bass.IndirectOffsetOnAxis(ap=index, axis=0)).then_inc(done, 16)

        def step(c, h, last):
            for k in range(TOPK):
                if not (isinstance(c, int) and PH * TOPK * c + TOPK * h + k < V_RING):
                    pool.wait_ge(v_used, PH * TOPK * c + (TOPK * h + k - V_RING + 1))
                gather(vrow[k % V_RING], exp_v, idx[h % 4][:, k:k + 1], v_landed[k % V_RING])
                if not last:
                    if k == 0:
                        pool.wait_ge(idx_ready, PH * c + (h + 2))
                    pool.wait_ge(dots, PH * TOPK * c + (TOPK * (h + 1) + k - U_RING + 1))
                    gather(urow[k % U_RING], exp_u, idx[(h + 1) % 4][:, k:k + 1], u_landed[k % U_RING])

        pool.wait_ge(idx_ready, 1)
        for k in range(TOPK):
            if k >= U_RING:
                pool.wait_ge(dots, k - U_RING + 1)
            gather(urow[k % U_RING], exp_u, idx[0][:, k:k + 1], u_landed[k % U_RING])
        for h in range(PH):
            step(0, h, False)
        with pool.Fori(1, TILES - 1) as c:
            for h in range(PH):
                step(c, h, False)
        for h in range(PH):
            step(TILES - 1, h, h == PH - 1)
        pool.wait_ge(idx_ready, pool.snap(passed))

    @block.sync
    def _(sp):
        for s in range(2):
            load_pair(sp, m, w_pq, sk_T, w_pair[s], keys[s], s, landed[s])
        with sp.Fori(1, PH) as c:
            for s in range(2):
                sp.wait_ge(s_ps, 2 * c + (s - 1))
                load_pair(sp, m, w_pq, sk_T, w_pair[s], keys[s], 2 * c + s, landed[s])
        sp.wait_ge(y_done, 1)
        sp.dma_start(y_s, m.h[:, 0, :]).then_inc(y_stored, 16)
        with sp.Fori(1, TILES) as c:
            sp.wait_ge(y_done, c + 1)
            sp.dma_start(y_p[bass.ds(c * P - P, P), :], m.h[:, bass.ds(c, 1), :].rearrange("p a n -> p (a n)")).then_inc(y_stored, 16)
        sp.wait_ge(y_stored, 16 * TILES)

    def over_tiles(eng, step):
        for h in range(PH):
            step(0, h)
        with eng.Fori(1, TILES - 1) as c:
            for h in range(PH):
                step(c, h)
        for h in range(PH):
            step(TILES - 1, h)

    def exists(c, h, ahead):
        return not isinstance(c, int) or PH * c + h + ahead < STEPS

    @block.tensor
    def _(pe):
        def prompt_queries(h, s, k):
            if k == 0:
                pe.wait_ge(landed[s], 32 * h + 32)
                if h >= 1:
                    pe.wait_ge(q_copied, 2 * h + s - 1)
            made = nc.tensor.matmul(psum[:, 2 + s, :], w_pair[s][:, k, :], m.mT[:, k, 0:PROMPT], start=(k == 0), stop=(k == DT - 1))
            if k == DT - 1:
                made.then_inc(q_ps, 1)

        def prompt_scores(h, s):
            pe.wait_ge(q_copied, 2 * h + s + 1)
            if h >= 1:
                pe.wait_ge(s_copied, 2 * h + s - 1)
            for i in range(PT):
                last = nc.tensor.matmul(psum[:, 4 + s, i * P:(i + 1) * P], q_sb[s][:, i * P:(i + 1) * P], keys[s],
                                        start=True, stop=True)
            last.then_inc(s_ps, 1)

        def step(c, h):
            streams = isinstance(c, int) and c == 0
            for k in range(TOPK):
                pe.wait_ge(diag_ready, PH * TOPK * c + (TOPK * h + k + 1))
                pe.wait_ge(v_landed[k % V_RING], 16 * PH * TOPK // V_RING * c + 16 * (TOPK // V_RING * h + k // V_RING + 1))
                if h == 0 and k == 0 and not (isinstance(c, int) and c == 0):
                    pe.wait_ge(y_done, c)
                for s in range(2):
                    last = nc.tensor.matmul(psum[:, s, :], diag[k % 4], vrow[k % V_RING][:, s * 512:(s + 1) * 512],
                                            start=(h == 0 and k == 0), stop=(h == PH - 1 and k == TOPK - 1))
                last.then_inc(v_used, 1)
                if streams:
                    prompt_queries(h, k // DT, k % DT)
                    if k == Q_AT[0] + 1:
                        prompt_scores(h, 0)
                    if k == Q_AT[1] + 1 and h >= 1:
                        prompt_scores(h - 1, 1)
            if streams and h == PH - 1:
                prompt_scores(h, 1)

        over_tiles(pe, step)

    @block.scalar
    def _(act):
        def copy_scores(n, s):
            nc.scalar.activation(sc[s], m.scores[:, bass.ds(n, 1), :].rearrange("p a (h k) -> p (a h) k", h=2),
                                 ACT.Copy).then_inc(sc_copied, 1)

        def exps(n, s):
            act.wait_ge(best_ready, n + 1)
            nc.scalar.activation(ex[s], bs[s], ACT.Exp, bias=nb[:, s:s + 1], accum_out=esum[:, s:s + 1]).then_inc(exp_ready, 1)

        def copy_queries(h, j):
            act.wait_ge(q_ps, 2 * h + j + 1)
            nc.scalar.activation(q_sb[j], psum[:, 2 + j, :], ACT.Copy).then_inc(q_copied, 1)

        def keep_scores(h, j):
            act.wait_ge(s_ps, 2 * h + j + 1)
            nc.scalar.activation(m.scores_ig[:, 1:, 2 * h + j, :], psum[:, 4 + j, :].rearrange("p (i k) -> p i k", i=PT),
                                 ACT.Copy).then_inc(s_copied, 1)

        def step(c, h):
            s = h % 2
            streams = isinstance(c, int) and c == 0
            if streams and h >= PH - 2:
                act.wait_ge(s_copied, 2 * (h + 2 - PH) + 2)
            elif h == 0 and not streams:
                act.wait_ge(s_copied, 2 * PH)
            if exists(c, h, 2):
                copy_scores(PH * c + (h + 2), s)
            if exists(c, h, 1):
                exps(PH * c + (h + 1), 1 - s)
            act.wait_ge(dots, PH * TOPK * c + TOPK * (h + 1))
            nc.scalar.activation(a_act[s], a_dot[s], ACT.Gelu_apprx_tanh).then_inc(acted, 1)
            if h == PH - 1 and exists(c, h, 1):
                copy_rows(c + 1)
            act.wait_ge(w_ready, PH * c + (h + 1))
            for k in range(TOPK):
                if not (isinstance(c, int) and PH * TOPK * c + TOPK * h + k < 4):
                    act.wait_ge(v_used, PH * TOPK * c + (TOPK * h + k - 3))
                nc.scalar.activation(diag[k % 4], m.ident[:, :], ACT.Copy, scale=wt[s][:, k:k + 1]).then_inc(diag_ready, 1)
                if streams:
                    for j in range(2):
                        if (j == 0 or h >= 1) and k == Q_AT[j]:
                            copy_queries(h - j, j)
                        if (j == 0 or h >= 1) and k == Q_AT[j] + 3:
                            keep_scores(h - j, j)
            if streams and h == PH - 1:
                copy_queries(h, 1)
                keep_scores(h, 1)

        def copy_rows(c):
            nc.scalar.activation(xs, m.xn2[:, bass.ds(c, 1), :].rearrange("p a n -> p (a n)"), ACT.Copy).then_inc(xs_copied, 1)

        copy_scores(0, 0)
        copy_scores(1, 1)
        exps(0, 0)
        copy_rows(0)
        over_tiles(act, step)

    @block.vector
    def _(dve):
        steps = Chain(dve, dve_did)

        def top(n, q):
            s = q % 2
            did, settled = steps.did, steps.settled
            dve.wait_ge(sc_copied, n + 1)
            nc.vector.memset(er[:, 2:3], 0.0)
            for k in range(2):
                did(nc.vector.max(tv[:, k, 0:8], sc[s][:, k, :]))
            settled()
            for k in range(2):
                did(nc.vector.max_index(ti[:, k, 0:8], tv[:, k, 0:8], sc[s][:, k, :]))
                did(nc.vector.match_replace(sr[k], tv[:, k, 0:8], sc[s][:, k, :], NEG))
            settled()
            for k in range(2):
                did(nc.vector.max(tv[:, k, 8:16], sr[k]))
            settled()
            for k in range(2):
                did(nc.vector.max_index(ti[:, k, 8:16], tv[:, k, 8:16], sr[k]))
            did(nc.vector.tensor_tensor(cand.rearrange("p (a b) -> p a b", a=TOPK), tv[:, 0, :, None].to_broadcast([P, TOPK, TOPK]),
                                        tv[:, 1:2, :].to_broadcast([P, TOPK, TOPK]), ALU.add))
            settled()
            did(nc.vector.max(bs[s][:, 0:8], cand))
            settled()
            did(nc.vector.max_index(bj[:, 0:8], bs[s][:, 0:8], cand))
            did(nc.vector.match_replace(cand2, bs[s][:, 0:8], cand, NEG))
            settled()
            did(nc.vector.max(bs[s][:, 8:16], cand2))
            settled()
            did(nc.vector.max_index(bj[:, 8:16], bs[s][:, 8:16], cand2))
            nc.vector.tensor_scalar(nb[:, s:s + 1], bs[s][:, 0:1], -1.0, None, ALU.mult).then_inc(best_ready, 1)
            settled()
            did(nc.vector.tensor_scalar(ab[0], bj, 4, None, ALU.logical_shift_right))
            did(nc.vector.tensor_scalar(ab[1], bj, TOPK - 1, None, ALU.bitwise_and))
            settled()
            for k in range(2):
                did(nc.vector.tensor_tensor(eq[k], ab[k][:, :, None].to_broadcast([P, TOPK, TOPK]),
                                            iota16[:, None, :].to_broadcast([P, TOPK, TOPK]), ALU.is_equal))
            settled()
            for k in range(2):
                did(nc.vector.tensor_tensor(eq[k], eq[k], ti[:, k:k + 1, :].to_broadcast([P, TOPK, TOPK]), ALU.mult))
            settled()
            for k in range(2):
                did(nc.vector.tensor_reduce(ij[k], eq[k], AX_X, ALU.add))
            settled()
            nc.vector.scalar_tensor_tensor(idx[q], ij[0], float(NKEYS), ij[1], ALU.mult, ALU.add).then_inc(idx_ready, 1)

        def result(c):
            tile = m.h[:, bass.ds(c, 1), :].rearrange("p a (s n) -> p (a s) n", s=2)
            nc.vector.tensor_tensor(tile, tile, psum[:, 0:2, :], ALU.add).then_inc(y_done, 1)

        def step(c, h):
            s = h % 2
            if exists(c, h, 1):
                top(PH * c + (h + 1), (h + 1) % 4)
            if h == 0:
                dve.wait_ge(xs_copied, c + 1)
            for k in range(TOPK):
                dve.wait_ge(u_landed[k % U_RING], 16 * PH * TOPK // U_RING * c + 16 * (TOPK // U_RING * h + k // U_RING + 1))
                if not (isinstance(c, int) and PH * TOPK * c + TOPK * h + k < 2):
                    dve.wait_ge(dots, PH * TOPK * c + (TOPK * h + k - 1))
                nc.vector.tensor_tensor_reduce(junk[k % 2], urow[k % U_RING], xs, 1.0, 0.0, ALU.mult, ALU.add,
                                               a_dot[s][:, k:k + 1]).then_inc(dots, 1)
            if h == 0 and not (isinstance(c, int) and c == 0):
                dve.wait_ge(v_used, PH * TOPK * c)
                result(c - 1)
            dve.wait_ge(exp_ready, PH * c + (h + 1))
            steps.did(nc.vector.reciprocal(er[:, s:s + 1], esum[:, s:s + 1]))
            steps.settled()
            dve.wait_ge(acted, PH * c + (h + 1))
            nc.vector.scalar_tensor_tensor(wt[s], ex[s], er[:, s:s + 1], a_act[s], ALU.mult, ALU.mult).then_inc(w_ready, 1)
            steps.restart()

        top(0, 0)
        steps.restart()
        over_tiles(dve, step)
        dve.wait_ge(v_used, STEPS * TOPK)
        result(TILES - 1)


def program(nc, x, xT, w_in, cols_d, rows_d, ident_d, ck_T, cv, cc_T, w_ao, w_co, w_out, w_pq, sk_T, exp_u, exp_v,
            y_p, y_s, k_p, v_p, c_p, k_s, v_s, c_s):
    with ExitStack() as memory:
        m = Memory(nc, memory)
        for stage, args in ((project, (xT, w_in, cols_d, rows_d, ident_d, cc_T, k_p, k_s, v_p, v_s, c_p, c_s)),
                            (attend, (ck_T, cv, v_s)),
                            (merge, (x, w_in, w_ao, w_co, w_out)),
                            (score, (w_pq, sk_T)),
                            (retrieve, (w_pq, sk_T, exp_u, exp_v, y_p, y_s))):
            with ExitStack() as ctx:
                stage(nc, ctx, m, *args)


def lay_out(inp):
    import numpy as np

    c = np.ascontiguousarray
    f = np.float32
    x = np.concatenate([inp["x_prompt"].reshape(PROMPT, D), inp["x_sample"].reshape(STREAMS * NEW, D)])
    by_column = lambda a: a.reshape(-1, P).T
    m = (np.arange(P) // NEW % 2).astype(f)[:, None]
    sel = np.zeros((P, 2 * HEADS - 1), f)
    sel[:, HEADS - 1] = 1
    cols = np.concatenate([by_column(inp[n][0]) for n in ("g_mix", "b_gate", "b_dw", "g_cln", "b_cln", "g_ffn", "g_sub")]
                          + [m, 1 - m, sel, inp["w_dw"][0].reshape(TAPS, DT, P).transpose(2, 1, 0).reshape(P, DT * TAPS)], axis=1)
    row = np.concatenate([inp[n][0] for n in ("g_qn", "g_kn", "lam_q1", "lam_k1", "lam_q2", "lam_k2")]
                         + [np.arange(TOPK, dtype=f), inp["g_ffn"][0]])
    return {
        "x": c(x), "xT": c(x.T), "w_in": c(inp["w_in"][0]), "cols": c(cols), "rows": c(np.broadcast_to(row, (P, row.size))),
        "ident": np.eye(P, dtype=f),
        "ck_T": c(inp["cache_k"][0].reshape(STREAMS, PAST, HEADS, P).transpose(0, 3, 2, 1).reshape(STREAMS, P, D)),
        "cv": c(inp["cache_v"][0].reshape(STREAMS, PAST, D)),
        "cc_T": c(inp["cache_conv"][0].reshape(STREAMS, HIST, DT, P).transpose(2, 3, 0, 1)),
        "w_ao": c(inp["w_attn_out"][0]), "w_co": c(inp["w_conv_out"][0]), "w_out": c(inp["w_out"][0]), "w_pq": c(inp["w_pq"][0]),
        "sk_T": c(inp["sub_keys"][0].reshape(2 * PH, NKEYS, P).transpose(0, 2, 1)),
        "exp_u": c(inp["expert_u"][0]), "exp_v": c(inp["expert_v"][0]),
    }


def kernel(**inputs):
    import numpy as np
    from concourse import bacc
    from concourse.bass_utils import run_bass_kernel_spmd

    nc = bacc.Bacc("TRN2", target_bir_lowering=False, num_devices=1)
    arrays = {f"in_{n}": a for n, a in lay_out({n: np.asarray(a) for n, a in inputs.items()}).items()}
    args = [nc.dram_tensor(n, a.shape, mybir.dt.from_np(a.dtype), kind="ExternalInput").ap() for n, a in arrays.items()]
    shapes = [(PROMPT, D), (STREAMS * NEW, D), (PROMPT, D), (PROMPT, D), (DT, P, HIST), (STREAMS * NEW, D), (STREAMS * NEW, D),
              (DT, P, STREAMS, HIST)]
    outs = [nc.dram_tensor(f"out_{i}_dram", s, F32, kind="ExternalOutput").ap() for i, s in enumerate(shapes)]
    program(nc, *args, *outs)
    r = run_bass_kernel_spmd(nc, [arrays], core_ids=[0]).results[0]
    y_p, y_s, k_p, v_p, c_p, k_s, v_s, c_s = [r[f"out_{i}_dram"] for i in range(len(shapes))]
    return (y_p.reshape(1, PROMPT, D), y_s.reshape(STREAMS, NEW, D),
            k_p.reshape(1, 1, PROMPT, HEADS, 2, DH), v_p.reshape(1, 1, PROMPT, HEADS, P),
            c_p.reshape(D, HIST).T.reshape(1, 1, HIST, D),
            k_s.reshape(1, STREAMS, NEW, HEADS, 2, DH), v_s.reshape(1, STREAMS, NEW, HEADS, P),
            c_s.reshape(D, STREAMS, HIST).transpose(1, 2, 0).reshape(1, STREAMS, HIST, D))
```

```python
import math
from contextlib import ExitStack

import concourse.bass as bass
from concourse import mybir

ALU = mybir.AluOpType
ACT = mybir.ActivationFunctionType
AX_X = mybir.AxisListType.X
F32 = mybir.dt.float32
U32 = mybir.dt.uint32

P = 128
D = 1024
DT = D // P
PROMPT = 512
TOK = 640
TILES = TOK // P
PT = PROMPT // P
CHUNK = 64
HEADS = 8
DH = 64
STREAMS = 8
NEW = 16
PAST = 128
TAPS = 31
HIST = TAPS - 1
EPS = 1e-6
NEG = -1e30
SCALE = DH ** -0.5
LAMBDA_INIT = 0.8 - 0.6 * math.exp(-0.3 * 0)
K_COL, V_COL, C_COL, G_COL = D, 2 * D, 3 * D, 5 * D
WCH = 256
PH = 8
TOPK = 16
NKEYS = 128
U_RING = 8
V_RING = 4
U_LEN = HIST + PROMPT + STREAMS * (HIST + NEW)
US = HIST + PROMPT

C_GMIX, C_BGATE, C_BDW, C_GCLN, C_BCLN, C_GFFN, C_GSUB = 0, 8, 24, 32, 40, 48, 56
C_M, C_NM, C_SEL, C_DW = 57, 58, 59, 59 + 2 * HEADS - 1
COLS = C_DW + DT * TAPS
R_GQ, R_GK, R_LAM, R_IOTA, R_GFFN = 0, DH, 2 * DH, 6 * DH, 6 * DH + TOPK
ROWS = R_GFFN + D


class Chain:

    def __init__(self, eng, sem):
        self.eng, self.sem, self.n = eng, sem, 0

    def did(self, instruction):
        self.n += 1
        instruction.then_inc(self.sem, 1)

    def settled(self):
        self.eng.wait_ge(self.sem, self.n)

    def restart(self):
        self.settled()
        self.eng.sem_clear(self.sem)
        self.n = 0




class Memory:

    def __init__(self, nc, ctx):
        def sb(name, shape, dt=F32):
            return ctx.enter_context(nc.sbuf_tensor(name, shape, dt))

        slab_a = sb("slab_a", [P, DT * TOK])
        slab_d = sb("slab_d", [P, DT * TOK])
        slab_e = sb("slab_e", [P, DT * TOK])
        slab_qk = sb("slab_qk", [P, 2 * DT * TOK])
        slab_u = sb("slab_u", [P, DT * U_LEN])
        self.slab_u = slab_u
        self.slab_w = slab_w = sb("slab_w", [P, 9216])
        self.work = sb("work", [P, 8192])
        self.cols = cols = sb("cols", [P, COLS])
        self.rows = sb("rows", [P, ROWS])
        self.ident = sb("ident", [P, P])
        self.ones = sb("ones", [P, P])
        self.lam = sb("lam", [P, 16])
        self.small = sb("small", [P, 64])
        self.psum = ctx.enter_context(nc.psum_tensor("psum", [P, 8, 512], F32))
        self.v_stored = ctx.enter_context(nc.semaphore("v_stored"))
        self.cache_in = [ctx.enter_context(nc.semaphore(f"cache_in{s}")) for s in range(2)]
        self.pair_landed = [ctx.enter_context(nc.semaphore(f"pair_landed{s}")) for s in range(4)]

        channels = lambda s: s[:, :].rearrange("p (c t) -> p c t", c=DT)
        tiles = lambda s: s[:, :].rearrange("p (i n) -> p i n", i=TILES)
        self.xnT, self.h = channels(slab_a), tiles(slab_a)
        self.v, self.mT = tiles(slab_d), channels(slab_d)
        self.oT, self.xn2 = channels(slab_e), tiles(slab_e)
        self.qkT = slab_qk[:, :].rearrange("p (g t) -> p g t", g=2 * HEADS)
        self.scores = slab_qk[:, :].rearrange("p (n k) -> p n k", k=2 * NKEYS)
        self.scores_ig = slab_qk[:, :].rearrange("p (i g k) -> p i g k", i=TILES, g=2 * PH)
        self.uT = slab_u[:, :].rearrange("p (c t) -> p c t", c=DT)
        self.yT = self.uT[:, :, 0:TOK]
        self.acc_p = slab_e[:, 0:PROMPT]
        self.acc_s = self.work[:, 7168:8192].rearrange("p (c n q) -> p c n q", c=DT, n=STREAMS)
        self.wk = [slab_w[:, s * DT * WCH:(s + 1) * DT * WCH].rearrange("p (c n) -> p c n", c=DT) for s in range(2)]
        self.wu = [slab_w[:, s * D:(s + 1) * D].rearrange("p (c n) -> p c n", c=DT) for s in range(8)]
        self.wo = [slab_w[:, s * 4 * D:(s + 1) * 4 * D].rearrange("p (c n) -> p c n", c=DT) for s in range(2)]
        self.cache = [slab_w[:, b:b + 3072] for b in (6144, 3072)]
        self.w_pair = [self.work[:, 2688 + s * D:2688 + (s + 1) * D].rearrange("p (c n) -> p c n", c=DT) for s in range(4)]
        self.pair_keys = [self.work[:, 6784 + s * P:6912 + s * P] for s in range(4)]
        self.w_dw = cols[:, C_DW:C_DW + DT * TAPS].rearrange("p (c k) -> p c k", c=DT)

    def col(self, c, j=0):
        return self.cols[:, bass.ds(c + j, 1)]


def by_channels(w, c0, n):
    return w.rearrange("(c p) n -> p c n", p=P)[:, :, bass.ds(c0, n)]


def columns_of(t):
    return t[:, 0:PROMPT], t[:, PROMPT:TOK]


def tile_columns(place):
    i = (place - 1) % TILES
    return slice(i * P, (i + 1) * P)


def project(nc, ctx, m, xT, w_in, cols_d, rows_d, ident_d, ck_T, cv, cc_T, k_p, k_s, v_p, v_s, c_p, c_s):
    def sem(name):
        return ctx.enter_context(nc.semaphore(name))

    consts_in, hist_in = sem("consts_in"), sem("hist_in")
    xT_in = [sem(f"xT_in{k}") for k in range(DT // 2)]
    w_landed = [sem("w_landed0"), sem("w_landed1")]
    ones_set, hist_zero = sem("ones_set"), sem("hist_zero")
    sq_ready, sq_used = sem("sq_ready"), sem("sq_used")
    var_ready, std_ready, xnT_ready = sem("var_ready"), sem("std_ready"), sem("xnT_ready")
    z_ps, z_sq, z_var, z_std, z_ready = [sem(n) for n in ("z_ps", "z_sq", "z_var", "z_std", "z_ready")]
    zT_ps, zT_free = sem("zT_ps"), sem("zT_free")
    k_stored = [sem("k_stored0"), sem("k_stored1")]
    v_stored, c_stored = m.v_stored, sem("c_stored")
    glu_ps, gate_ready, u_ready = sem("glu_ps"), sem("gate_ready"), sem("u_ready")
    s_tap, tap, acc_free = sem("s_tap"), sem("tap1"), sem("acc_free")
    dve_did = sem("dve_did1")

    work, psum, xnT, uT, wk = m.work, m.psum, m.xnT, m.uT, m.wk
    sq = [work[:, s * TOK:(s + 1) * TOK] for s in range(2)]
    rB, std = work[:, 1280:1920], work[:, 1920:2560]
    zq = [work[:, 2560 + s * WCH:2560 + (s + 1) * WCH] for s in range(2)]
    zs = [work[:, 3072 + s * WCH:3072 + (s + 1) * WCH] for s in range(2)]
    zg = work[:, 3584:3584 + WCH]
    acc = work[:, 5120:5120 + PROMPT]
    product = work[:, 5632:5632 + D].rearrange("p (c n q) -> p c n q", c=DT, n=STREAMS)
    product_p = work[:, 5632:5632 + PROMPT]
    sg = [work[:, 3840 + s * TOK:3840 + (s + 1) * TOK] for s in range(2)]
    zsum, zvar, zstd, zr = [m.small[:, 4 * k:4 * k + 4] for k in range(4)]
    NCH = 3 * D // WCH
    QK = 2 * D // WCH
    groups = lambda a: a.rearrange("p (g d) -> p g d", d=DH)
    glu = [(0, 1, 2), (3, 4, 7)]

    block = ctx.enter_context(nc.Block())

    @block.sync
    def _(sp):
        for c in range(0, DT, 2):
            sp.dma_start(xnT[:, c:c + 2, :], xT[c * P:(c + 2) * P, :].rearrange("(c p) t -> p c t", p=P)).then_inc(xT_in[c // 2], 16)
        sp.dma_start(m.cols[:, :], cols_d).then_inc(consts_in, 16)
        sp.dma_start(m.rows[:, :], rows_d).then_inc(consts_in, 16)
        sp.dma_start(m.ident[:, :], ident_d).then_inc(consts_in, 16)
        for s in range(2):
            for part in range(2):
                sp.dma_start(wk[s][:, :, part * P:(part + 1) * P],
                             by_channels(w_in, C_COL + part * D + s * P, P)).then_inc(w_landed[s], 16)
        for j in range(DT):
            sp.dma_start(uT[:, j, US:].rearrange("p (b t) -> p b t", b=STREAMS)[:, :, 0:HIST],
                         cc_T[j]).then_inc(hist_in, 16)
        with sp.Fori(1, DT // 2) as c:
            for s in range(2):
                sp.wait_ge(glu_ps, 2 * c + s - 1)
                for part in range(2):
                    sp.dma_start(wk[s][:, :, part * P:(part + 1) * P],
                                 by_channels(w_in, 2 * P * c + (C_COL + part * D + s * P), P)).then_inc(w_landed[s], 16)
        for s in range(2):
            sp.wait_ge(glu_ps, DT - 1 + s)
            sp.dma_start(wk[s], by_channels(w_in, s * WCH, WCH)).then_inc(w_landed[s], 16)
        with sp.Fori(1, NCH // 2) as c:
            for s in range(2):
                sp.wait_ge(z_ps, 2 * TILES * c + TILES * (s - 1))
                sp.dma_start(wk[s], by_channels(w_in, 2 * WCH * c + s * WCH, WCH)).then_inc(w_landed[s], 16)
        sp.dma_start(m.cache[0][:, 0:D], ck_T[0]).then_inc(m.cache_in[0], 16)
        sp.dma_start(m.cache[0][:, D:2 * D], cv[0]).then_inc(m.cache_in[0], 16)

    @block.gpsimd
    def _(pool):
        def add_tap(k, n, u, w, total, product):
            if k == 0:
                nc.gpsimd.tensor_tensor(total, u, w, ALU.mult).then_inc(s_tap, 1)
                return n + 1
            nc.gpsimd.tensor_tensor(product, u, w, ALU.mult).then_inc(s_tap, 1)
            pool.wait_ge(s_tap, n + 1)
            nc.gpsimd.tensor_tensor(total, total, product, ALU.add).then_inc(s_tap, 1)
            pool.wait_ge(s_tap, n + 2)
            return n + 2

        nc.gpsimd.memset(m.ones[:, :], 1.0).then_inc(ones_set, 1)
        nc.gpsimd.memset(uT[:, :, 0:HIST], 0.0).then_inc(hist_zero, 1)
        for s in range(2):
            nc.gpsimd.memset(m.small[:, 62 + s:63 + s], 0.0).then_inc(k_stored[s], 16)
        nc.gpsimd.memset(acc, 0.0).then_inc(acc_free, 1)
        pool.wait_ge(u_ready, DT)
        pool.wait_ge(hist_in, 16 * DT)
        for j in range(DT):
            pool.dma_start(c_p[j], uT[:, j, US - HIST:US]).then_inc(c_stored, 16)
            pool.dma_start(c_s[j], uT[:, j, US:].rearrange("p (b t) -> p b t", b=STREAMS)[:, :, NEW:]).then_inc(c_stored, 16)
        streams = uT[:, :, US:].rearrange("p c (n t) -> p c n t", n=STREAMS)
        n = 0
        for k in range(TAPS):
            w = m.w_dw[:, :, k:k + 1, None].to_broadcast([P, DT, STREAMS, NEW])
            n = add_tap(k, n, streams[:, :, :, k:k + NEW], w, m.acc_s, product)
        for k in range(TAPS):
            n = add_tap(k, n, uT[:, DT - 1, k:k + PROMPT], m.w_dw[:, DT - 1, k:k + 1].to_broadcast([P, PROMPT]), m.acc_p, product_p)
        for part in range(2):
            pool.wait_ge(z_ready, TILES * (QK + 2 * part + 2))
            n = slice(part * D // 2, (part + 1) * D // 2)
            pool.dma_start(v_s[:, n], m.v[:, PT, n]).then_inc(v_stored, 16)
            pool.dma_start(v_p.rearrange("(i p) n -> p i n", p=P)[:, :, n], m.v[:, 0:PT, n]).then_inc(v_stored, 16)
        pool.wait_ge(k_stored[0], 16 * TILES * QK // 4 + 16)
        pool.wait_ge(k_stored[1], 16 * TILES * QK // 4 + 16)
        pool.wait_ge(c_stored, 32 * DT)

    @block.tensor
    def _(pe):
        pe.wait_ge(ones_set, 1)
        for c in range(DT):
            pe.wait_ge(sq_ready, c + 1)
            a, b = columns_of(sq[c % 2])
            nc.tensor.matmul(psum[:, 0, :], m.ones[:, :], a, start=(c == 0), stop=(c == DT - 1))
            nc.tensor.matmul(psum[:, 1, 0:P], m.ones[:, :], b, start=(c == 0), stop=(c == DT - 1)).then_inc(sq_used, 1)
        pe.wait_ge(consts_in, 48)

        def products(s, i):
            for c in range(DT):
                last = nc.tensor.matmul(psum[:, i, 0:WCH], xnT[:, c, i * P:(i + 1) * P], wk[s][:, c, :],
                                        start=(c == 0), stop=(c == DT - 1))
            last.then_inc(z_ps, 1)

        def turn(c, n, first):
            pe.wait_ge(z_ready, 2 * TILES * c + (n + 1))
            if not first or n >= 2:
                pe.wait_ge(zT_free, 2 * TILES * c + (n - 1))
            for g in range(2):
                last = nc.tensor.transpose(psum[:, 5 + n % 2, g * P:(g + 1) * P], zq[n % 2][:, g * P:(g + 1) * P],
                                           m.ident[:, :])
            last.then_inc(zT_ps, 1)

        def qk_body(c, first):
            for n in range(2 * TILES):
                s, i = divmod(n, TILES)
                if i == 0:
                    pe.wait_ge(w_landed[s], 16 * c + (16 * DT + 16))
                if not first or n >= TILES:
                    pe.wait_ge(z_ready, 2 * TILES * c + (n - TILES + 1))
                products(s, i)
                if n >= 1:
                    turn(c, n - 1, first)
            turn(c, 2 * TILES - 1, first)

        def glu_body(c, first):
            for s in range(2):
                pe.wait_ge(w_landed[s], 32 * c + 32)
                if not first:
                    pe.wait_ge(u_ready, 2 * c + (s - 1))
                for part in range(2):
                    for k in range(DT):
                        if first and s == 0 and part == 0:
                            pe.wait_ge(xnT_ready, k + 1)
                        w = wk[s][:, k, part * P:(part + 1) * P]
                        nc.tensor.matmul(psum[:, glu[s][part], :], w, xnT[:, k, 0:PROMPT],
                                         start=(k == 0), stop=(k == DT - 1))
                        last = nc.tensor.matmul(psum[:, glu[s][2], part * P:(part + 1) * P], w, xnT[:, k, PROMPT:TOK],
                                                start=(k == 0), stop=(k == DT - 1))
                last.then_inc(glu_ps, 1)

        glu_body(0, True)
        with pe.Fori(1, DT // 2) as c:
            glu_body(c, False)
        pe.wait_ge(u_ready, DT)
        qk_body(0, True)
        with pe.Fori(1, QK // 2) as c:
            qk_body(c, False)
        with pe.Fori(QK // 2, NCH // 2) as c:
            for n in range(2 * TILES):
                s, i = divmod(n, TILES)
                if i == 0:
                    pe.wait_ge(w_landed[s], 16 * c + (16 * DT + 16))
                pe.wait_ge(z_ready, 2 * TILES * c + (n - TILES + 1))
                products(s, i)

    @block.scalar
    def _(act):
        for c in range(DT):
            act.wait_ge(xT_in[c // 2], 16)
            if c >= 2:
                act.wait_ge(sq_used, c - 1)
            nc.scalar.activation(sq[c % 2], xnT[:, c, :], ACT.Square).then_inc(sq_ready, 1)
        act.wait_ge(var_ready, 2)
        nc.scalar.activation(std, rB, ACT.Sqrt).then_inc(std_ready, 1)

        def gates(c, s, first):
            act.wait_ge(glu_ps, 2 * c + (s + 1))
            if not first:
                act.wait_ge(u_ready, 2 * c + (s - 1))
            nc.scalar.activation(sg[s][:, 0:PROMPT], psum[:, glu[s][1], :], ACT.Sigmoid)
            nc.scalar.activation(sg[s][:, PROMPT:TOK], psum[:, glu[s][2], P:2 * P], ACT.Sigmoid).then_inc(gate_ready, 1)

        for s in range(2):
            gates(0, s, True)
        with act.Fori(1, DT // 2) as c:
            for s in range(2):
                gates(c, s, False)

        def conv_out(j):
            act.wait_ge(tap, TAPS * j + TAPS)
            nc.scalar.activation(m.yT[:, bass.ds(j, 1), 0:PROMPT].rearrange("p a t -> p (a t)"), acc, ACT.Identity,
                                 bias=m.col(C_BDW, j)).then_inc(acc_free, 1)

        def turned(c, n):
            s, i = divmod(n, TILES)
            act.wait_ge(zT_ps, 2 * TILES * c + (n + 1))
            nc.scalar.activation(m.qkT[:, bass.ds(4 * c + 2 * s, 2), i * P:(i + 1) * P],
                                 psum[:, 5 + n % 2, 0:WCH].rearrange("p (g t) -> p g t", g=2), ACT.Copy).then_inc(zT_free, 1)

        def store(c, n):
            s, i = divmod(n, TILES)
            act.wait_ge(z_ready, 2 * TILES * c + (n + 1))
            col = bass.ds(2 * WCH * c + (s * WCH - D), WCH)
            dst = k_p[i * P:(i + 1) * P, col] if i < PT else k_s[:, col]
            act.dma_start(dst, zq[n % 2]).then_inc(k_stored[n % 2], 16)

        for kind in range(2):
            with act.Fori(kind * QK // 4, (kind + 1) * QK // 4) as c:
                for n in range(2 * TILES):
                    i = n % TILES
                    act.wait_ge(z_ps, 2 * TILES * c + (n + 1))
                    if n >= 2:
                        act.wait_ge(z_ready, 2 * TILES * c + (n - 1))
                    nc.scalar.activation(zs[n % 2], psum[:, i, 0:WCH], ACT.Square).then_inc(z_sq, 1)
                    act.wait_ge(z_var, 2 * TILES * c + (n + 1))
                    nc.scalar.activation(zstd, zvar, ACT.Sqrt).then_inc(z_std, 1)
                    if n >= 1:
                        if kind == 1:
                            store(c, n - 1)
                        turned(c, n - 1)
                if kind == 1:
                    store(c, 2 * TILES - 1)
                turned(c, 2 * TILES - 1)
                if kind == 1:
                    conv_out(c - QK // 4)
        with act.Fori(QK // 2, NCH // 2) as c:
            conv_out(c - QK // 4)

    @block.vector
    def _(dve):
        steps = Chain(dve, dve_did)
        dve.wait_ge(consts_in, 48)
        lam = m.lam
        for k in range(2):
            a = m.rows[:, R_LAM + 2 * k * DH:R_LAM + (2 * k + 1) * DH]
            b = m.rows[:, R_LAM + (2 * k + 1) * DH:R_LAM + (2 * k + 2) * DH]
            steps.did(nc.vector.tensor_tensor(zg[:, k * DH:(k + 1) * DH], a, b, ALU.mult))
        steps.settled()
        steps.did(nc.vector.tensor_reduce(lam[:, 0:2], zg[:, 0:2 * DH].rearrange("p (k d) -> p k d", k=2), AX_X, ALU.add))
        steps.settled()
        dve.wait_ge(sq_used, DT)
        for (a, b) in zip(columns_of(rB), (psum[:, 0, :], psum[:, 1, 0:P])):
            nc.vector.tensor_scalar(a, b, 1.0 / D, EPS, ALU.mult, ALU.add).then_inc(var_ready, 1)
        dve.wait_ge(std_ready, 1)
        steps.did(nc.vector.reciprocal(rB, std))
        steps.settled()
        for c in range(DT):
            nc.vector.scalar_tensor_tensor(xnT[:, c, :], xnT[:, c, :], m.col(C_GMIX + c), rB, ALU.mult, ALU.mult).then_inc(xnT_ready, 1)
        with dve.Fori(0, DT // 2) as c:
            for s in range(2):
                dve.wait_ge(gate_ready, 2 * c + (s + 1))
                nc.vector.tensor_tensor(uT[:, bass.ds(2 * c + s, 1), HIST:US].rearrange("p a t -> p (a t)"),
                                        psum[:, glu[s][0], :], sg[s][:, 0:PROMPT], ALU.mult)
                streams = uT[:, bass.ds(2 * c + s, 1), US:].rearrange("p a (b t) -> p (a b) t", b=STREAMS)[:, :, HIST:]
                nc.vector.tensor_tensor(streams, psum[:, glu[s][2], 0:P].rearrange("p (b t) -> p b t", b=STREAMS),
                                        sg[s][:, PROMPT:TOK].rearrange("p (b t) -> p b t", b=STREAMS),
                                        ALU.mult).then_inc(u_ready, 1)

        dve.wait_ge(hist_zero, 1)

        def taps(c, n):
            j = c - QK // 4
            for k in range(n * TAPS // (2 * TILES), (n + 1) * TAPS // (2 * TILES)):
                w = m.w_dw[:, bass.ds(j, 1), k:k + 1].rearrange("p a k -> p (a k)")
                u = uT[:, bass.ds(j, 1), k:k + PROMPT].rearrange("p a t -> p (a t)")
                if k == 0:
                    dve.wait_ge(acc_free, j + 1)
                    nc.vector.tensor_scalar(acc, u, w, None, ALU.mult).then_inc(tap, 1)
                else:
                    dve.wait_ge(tap, TAPS * j + k)
                    nc.vector.scalar_tensor_tensor(acc, u, w, acc, ALU.mult, ALU.add).then_inc(tap, 1)

        for kind in range(2):
            gain = m.rows[:, R_GQ + kind * DH:R_GQ + (kind + 1) * DH]
            steps.restart()
            with dve.Fori(kind * QK // 4, (kind + 1) * QK // 4) as c:
                for n in range(2 * TILES):
                    i = n % TILES
                    dve.wait_ge(z_sq, 2 * TILES * c + (n + 1))
                    steps.did(nc.vector.tensor_reduce(zsum, groups(zs[n % 2]), AX_X, ALU.add))
                    steps.settled()
                    nc.vector.tensor_scalar(zvar, zsum, 1.0 / DH, EPS, ALU.mult, ALU.add).then_inc(z_var, 1)
                    steps.did(nc.vector.tensor_tensor(groups(zg), groups(psum[:, i, 0:WCH]),
                                                      gain[:, None, :].to_broadcast([P, 4, DH]), ALU.mult))
                    dve.wait_ge(z_std, 2 * TILES * c + (n + 1))
                    steps.did(nc.vector.reciprocal(zr, zstd))
                    steps.settled()
                    if n >= 2:
                        dve.wait_ge(zT_ps, 2 * TILES * c + (n - 1))
                    if kind == 1:
                        dve.wait_ge(k_stored[n % 2], 16 * TILES * c + 16 * (n // 2 + 1) - 16 * TILES * QK // 4)
                    nc.vector.tensor_tensor(groups(zq[n % 2]), groups(zg),
                                            zr[:, :, None].to_broadcast([P, 4, DH]), ALU.mult).then_inc(z_ready, 1)
                    if kind == 1:
                        taps(c, n)
                steps.restart()
        with dve.Fori(QK // 2, NCH // 2) as c:
            for n in range(2 * TILES):
                s, i = divmod(n, TILES)
                dve.wait_ge(z_ps, 2 * TILES * c + (n + 1))
                nc.vector.tensor_copy(m.v[:, i, bass.ds(2 * WCH * c + (s * WCH - 2 * D), WCH)],
                                      psum[:, i, 0:WCH]).then_inc(z_ready, 1)
                taps(c, n)


def attend(nc, ctx, m, ck_T, cv, v_s):
    def sem(name):
        return ctx.enter_context(nc.semaphore(name))

    cache_in = m.cache_in
    laid = sem("laid")
    bd_zero, bd_ready, lam_exp, lam_ready = sem("bd_zero"), sem("bd_ready"), sem("lam_exp"), sem("lam_ready")
    names = ("logits", "max_ready", "exp_ready", "probs", "probsT_ps", "probsT", "out_ps", "out_done")
    s_ps, s_max, s_exp, s_prob, s_pT, s_pTs, s_out, s_done = [sem("s_" + n) for n in names]
    p_ps, p_max, p_exp, p_prob, p_pT, p_pTs, p_out, p_done = [sem("p_" + n) for n in names]
    masked, head_ready = sem("masked"), sem("head_ready")
    tap, acc_free, last_copied = sem("tap"), sem("acc_free2"), sem("last_copied")
    dve_did = sem("dve_did2")

    work, psum, slab_w, small = m.work, m.psum, m.slab_w, m.small
    T = PAST + NEW
    UNIT = HEADS // 2
    ckT = [m.cache[s][:, 0:1024].rearrange("p (h t) -> p h t", h=HEADS) for s in range(2)]
    cvv = [m.cache[s][:, 1024:2048].rearrange("p (h e) -> p h e", h=HEADS) for s in range(2)]
    vnew = [m.cache[s][0:NEW, 2048:3072].rearrange("p (h e) -> p h e", h=HEADS) for s in range(2)]
    qh = [slab_w[:, s * 1536:s * 1536 + 512] for s in range(2)]
    kh = [slab_w[:, s * 1536 + 512:s * 1536 + 1024] for s in range(2)]
    vh = [slab_w[:, s * 1536 + 1024:s * 1536 + 1536].rearrange("p (i e) -> p i e", i=PT) for s in range(2)]
    probs = [work[:, s * 1024:(s + 1) * 1024].rearrange("p (m k) -> p m k", m=2) for s in range(2)]
    diff = [work[:, 2048 + s * 512:2560 + s * 512] for s in range(2)]
    second = work[:, 3072:3584]
    diffT = [work[:, 3584 + s * 512:4096 + s * 512] for s in range(2)]
    acc = work[:, 4608:4608 + PROMPT]
    sp_probs = [work[:, 5248 + s * T:5248 + (s + 1) * T] for s in range(2)]
    bd = [work[:, 5536 + s * 256:5792 + s * 256] for s in range(2)]
    kn = [work[:, 6048 + s * P:6176 + s * P].rearrange("p (h q) -> p h q", h=HEADS) for s in range(2)]
    sprobsT = [work[:, 6304 + s * 256:6560 + s * 256] for s in range(2)]
    mx = [small[:, 16 + 4 * s:18 + 4 * s] for s in range(2)]
    nmx = [small[:, 24 + 4 * s:26 + 4 * s] for s in range(2)]
    den = [small[:, 32 + 4 * s:34 + 4 * s] for s in range(2)]
    rden = [small[:, 40 + 4 * s:42 + 4 * s] for s in range(2)]
    minus_lam, row_sign = m.lam[:, 4:5], m.lam[:, 5:6]
    LU = 4
    U = 2 * PT
    s_mx, s_nmx, s_den = [[small[:, 48 + 2 * k + s:49 + 2 * k + s] for s in range(2)] for k in range(3)]
    s_rden = [small[:, 54 + 2 * s:56 + 2 * s] for s in range(2)]
    s_lg, s_T = [psum[:, b, 0:T] for b in (7, 5)], [psum[:, b, T:T + P] for b in (7, 5)]
    s_Tn, s_o = [psum[0:NEW, b, T + P:T + 2 * P] for b in (7, 5)], [psum[:, b, 400:400 + UNIT * NEW] for b in (7, 5)]
    bdv = lambda s: bd[s].rearrange("p (h m q) -> p h m q", h=HEADS, m=2)

    ROUNDS = HEADS // 2

    def exists(c, u, per_round=U):
        return not isinstance(c, int) or 0 <= per_round * c + u < per_round * ROUNDS

    def over_rounds(eng, step):
        for u in range(U):
            step(0, u)
        with eng.Fori(1, ROUNDS - 1) as c:
            for u in range(U):
                step(c, u)
        for u in range(U + 3):
            step(ROUNDS - 1, u)

    block = ctx.enter_context(nc.Block())

    @block.sync
    def _(sp):
        def load_cache(s, b):
            sp.dma_start(m.cache[s][:, 0:1024], ck_T[bass.ds(b, 1)].rearrange("a p n -> (a p) n")).then_inc(cache_in[s], 16)
            sp.dma_start(m.cache[s][:, 1024:2048], cv[bass.ds(b, 1)].rearrange("a p n -> (a p) n")).then_inc(cache_in[s], 16)

        def load_new(s, b):
            sp.dma_start(m.cache[s][0:NEW, 2048:3072], v_s[bass.ds(b * NEW, NEW), :]).then_inc(cache_in[s], 16)

        load_cache(1, 1)
        sp.wait_ge(m.v_stored, 64)
        for s in range(2):
            load_new(s, s)
        with sp.Fori(1, STREAMS // 2) as c:
            for s in range(2):
                sp.wait_ge(s_out, LU * c + (2 * s - 2))
                load_cache(s, 2 * c + s)
                load_new(s, 2 * c + s)

    @block.gpsimd
    def _(pool):
        nc.gpsimd.memset(acc, 0.0).then_inc(acc_free, 1)
        def lay(s, b):
            new = bass.ds(b * NEW + PROMPT, NEW)
            for k in range(2):
                rows = slice(k * DH, (k + 1) * DH)
                nc.gpsimd.tensor_copy(bdv(s)[rows, :, k, :], m.qkT[rows, 0:HEADS, new]).then_inc(laid, 1)
                pool.wait_ge(laid, 2 * b + (k + 1))
            nc.gpsimd.tensor_copy(kn[s], m.qkT[:, HEADS:, new]).then_inc(bd_ready, 1)

        def head(s, h):
            nc.gpsimd.tensor_copy(qh[s], m.qkT[:, bass.ds(h, 1), 0:PROMPT].rearrange("p a t -> p (a t)"))
            nc.gpsimd.tensor_copy(kh[s], m.qkT[:, bass.ds(h + HEADS, 1), 0:PROMPT].rearrange("p a t -> p (a t)"))
            nc.gpsimd.tensor_copy(vh[s], m.v[:, 0:PT, bass.ds(h * P, P)]).then_inc(head_ready, 1)

        for s in range(2):
            nc.gpsimd.memset(bd[s], 0.0).then_inc(bd_zero, 1)
        pool.wait_ge(bd_zero, 2)
        for s in range(2):
            lay(s, s)
            head(s, s)
        with pool.Fori(1, HEADS // 2) as c:
            for s in range(2):
                pool.wait_ge(s_ps, LU * c + (2 * s - 2))
                lay(s, 2 * c + s)
                pool.wait_ge(p_out, U * c + PT * (s - 1))
                head(s, 2 * c + s)

    @block.tensor
    def _(pe):
        def stream_logits(c, v):
            s, g = v // 2 % 2, v % 2
            if g == 0:
                pe.wait_ge(cache_in[s], 48 * c + 48 * (v // LU + 1))
                pe.wait_ge(bd_ready, 2 * c + (v // 2 + 1))
            if exists(c, v - 2, LU):
                pe.wait_ge(s_done, LU * c + (v - 1))
            for k in range(UNIT):
                h = g * UNIT + k
                out = s_lg[v % 2][32 * k:32 * k + 32, :]
                lhsT = bd[s][:, 32 * h:32 * h + 32]
                nc.tensor.matmul(out[:, 0:PAST], lhsT, ckT[s][:, h, :], start=True, stop=True)
                last = nc.tensor.matmul(out[:, PAST:T], lhsT, kn[s][:, h, :], start=True, stop=True)
            last.then_inc(s_ps, 1)

        def stream_turn(c, v):
            pe.wait_ge(s_prob, LU * c + (v + 1))
            nc.tensor.transpose(s_T[v % 2], sp_probs[v % 2][:, 0:PAST], m.ident[:, :])
            nc.tensor.transpose(s_Tn[v % 2], sp_probs[v % 2][:, PAST:T], m.ident[:, :]).then_inc(s_pT, 1)

        def stream_values(c, v):
            s, g = v // 2 % 2, v % 2
            pe.wait_ge(s_pTs, LU * c + (v + 1))
            for k in range(UNIT):
                h = g * UNIT + k
                out = s_o[v % 2][:, k * NEW:(k + 1) * NEW]
                for j in range(2):
                    a = 32 * k + NEW * j
                    nc.tensor.matmul(out, cvv[s][:, h, :], sprobsT[v % 2][:, a:a + NEW], start=(j == 0), stop=False)
                    last = nc.tensor.matmul(out, vnew[s][:, h, :], sprobsT[v % 2][0:NEW, P + a:P + a + NEW],
                                            start=False, stop=(j == 1))
            last.then_inc(s_out, 1)

        def logits(c, u):
            s, i = u // PT % 2, u % PT
            n = (i + 1) * P
            if i == 0:
                pe.wait_ge(head_ready, 2 * c + (u // PT + 1))
            if exists(c, u - 2):
                pe.wait_ge(p_exp, U * c + (u - 1))
            for j in range(2):
                rows = slice(j * DH, (j + 1) * DH)
                last = nc.tensor.matmul(psum[:, 2 * (u % 2) + j, 0:n], qh[s][rows, i * P:(i + 1) * P], kh[s][rows, 0:n],
                                        start=True, stop=True)
            last.then_inc(p_ps, 1)

        def turn(c, u):
            pe.wait_ge(p_prob, U * c + (u + 1))
            if exists(c, u - 1):
                pe.wait_ge(p_pTs, U * c + u)
            for k in range(u % PT + 1):
                last = nc.tensor.transpose(psum[:, 4, k * P:(k + 1) * P], diff[u % 2][:, k * P:(k + 1) * P], m.ident[:, :])
            last.then_inc(p_pT, 1)

        def values(c, u):
            s, i = u // PT % 2, u % PT
            pe.wait_ge(p_pTs, U * c + (u + 1))
            if i == 0 and exists(c, u - 1):
                pe.wait_ge(p_done, 2 * c + u // PT)
            for k in range(i + 1):
                last = nc.tensor.matmul(psum[:, 6, i * P:(i + 1) * P], vh[s][:, k, :], diffT[u % 2][:, k * P:(k + 1) * P],
                                        start=(k == 0), stop=(k == i))
            last.then_inc(p_out, 1)

        def step(c, u):
            v = u // 2
            if exists(c, u):
                logits(c, u)
            if exists(c, u - 3):
                values(c, u - 3)
            if exists(c, u - 2):
                turn(c, u - 2)
            if exists(c, v - 1, LU):
                (stream_values if u % 2 else stream_turn)(c, v - 1)
            if u % 2 == 0 and exists(c, u):
                stream_logits(c, v)

        over_rounds(pe, step)

    @block.scalar
    def _(act):
        nc.scalar.activation(m.lam[:, 2:4], m.lam[:, 0:2], ACT.Exp).then_inc(lam_exp, 1)
        nc.scalar.activation(m.yT[:, DT - 1, 0:PROMPT], m.acc_p, ACT.Identity, bias=m.col(C_BDW + DT - 1)).then_inc(last_copied, 1)
        act.wait_ge(last_copied, 1)

        def stream_exp(c, v):
            act.wait_ge(s_max, LU * c + (v + 1))
            if exists(c, v - 2, LU):
                act.wait_ge(s_pT, LU * c + (v - 1))
            nc.scalar.activation(sp_probs[v % 2], s_lg[v % 2], ACT.Exp, bias=s_nmx[v % 2], scale=SCALE,
                                 accum_out=s_den[v % 2]).then_inc(s_exp, 1)

        def stream_copy(c, v):
            act.wait_ge(s_pT, LU * c + (v + 1))
            if exists(c, v - 2, LU):
                act.wait_ge(s_out, LU * c + (v - 1))
            nc.scalar.activation(sprobsT[v % 2][:, 0:P], s_T[v % 2], ACT.Copy)
            nc.scalar.activation(sprobsT[v % 2][0:NEW, P:2 * P], s_Tn[v % 2], ACT.Copy).then_inc(s_pTs, 1)

        def stream_out(c, v):
            g = v % 2
            act.wait_ge(s_out, LU * c + (v + 1))
            nc.scalar.activation(m.oT[:, g * UNIT:(g + 1) * UNIT, bass.ds(2 * NEW * c + (PROMPT + NEW * (v // 2)), NEW)],
                                 s_o[g].rearrange("p (h q) -> p h q", h=UNIT), ACT.Copy).then_inc(s_done, 1)

        def exps(c, u):
            n = (u % PT + 1) * P
            act.wait_ge(p_max, U * c + (u + 1))
            if exists(c, u - 2):
                act.wait_ge(p_prob, U * c + (u - 1))
            for j in range(2):
                last = nc.scalar.activation(probs[u % 2][:, j, 0:n], psum[:, 2 * (u % 2) + j, 0:n], ACT.Exp,
                                            bias=nmx[u % 2][:, j:j + 1], scale=SCALE, accum_out=den[u % 2][:, j:j + 1])
            last.then_inc(p_exp, 1)

        def copy(c, u):
            n = (u % PT + 1) * P
            act.wait_ge(p_pT, U * c + (u + 1))
            if exists(c, u - 2):
                act.wait_ge(p_out, U * c + (u - 1))
            nc.scalar.activation(diffT[u % 2][:, 0:n], psum[:, 4, 0:n], ACT.Copy).then_inc(p_pTs, 1)

        def out(c, u):
            act.wait_ge(p_out, U * c + (u + 1))
            nc.scalar.activation(m.oT[:, bass.ds(2 * c + u // PT, 1), 0:PROMPT].rearrange("p a t -> p (a t)"), psum[:, 6, :],
                                 ACT.Copy).then_inc(p_done, 1)

        def streams_out(j):
            nc.scalar.activation(m.yT[:, bass.ds(j, 1), PROMPT:TOK].rearrange("p a (n q) -> p (a n) q", n=STREAMS),
                                 m.acc_s[:, bass.ds(j, 1)].rearrange("p a n q -> p (a n) q"), ACT.Identity, bias=m.col(C_BDW, j))

        def conv_out(c):
            act.wait_ge(tap, TAPS * c + TAPS)
            nc.scalar.activation(m.yT[:, bass.ds(c + DT // 2, 1), 0:PROMPT].rearrange("p a t -> p (a t)"), acc, ACT.Identity,
                                 bias=m.col(C_BDW, c + DT // 2)).then_inc(acc_free, 1)
            streams_out(c + DT // 2)

        def step(c, u):
            v = u // 2
            if exists(c, u):
                exps(c, u)
            if exists(c, u - 2):
                copy(c, u - 2)
            if exists(c, v - 1, LU):
                (stream_out if u % 2 else stream_copy)(c, v - 1)
            if u % 2 == 1 and exists(c, u):
                stream_exp(c, v)
            if u % PT == PT - 2 and exists(c, u - 3):
                out(c, u - 3)
            if u == PT:
                streams_out(c)
            if u == U - 1:
                if isinstance(c, int) and c == ROUNDS - 1:
                    streams_out(DT - 1)
                else:
                    conv_out(c)

        over_rounds(act, step)

    @block.vector
    def _(dve):
        steps = Chain(dve, dve_did)
        lam = m.lam
        dve.wait_ge(lam_exp, 1)
        steps.did(nc.vector.tensor_scalar(lam[:, 6:7], lam[:, 3:4], -LAMBDA_INIT, None, ALU.add))
        steps.settled()
        steps.did(nc.vector.tensor_tensor(minus_lam, lam[:, 6:7], lam[:, 2:3], ALU.subtract))
        steps.settled()
        steps.did(nc.vector.scalar_tensor_tensor(row_sign, m.col(C_M), minus_lam, m.col(C_NM), ALU.mult, ALU.add))
        steps.restart()

        def stream_max(c, u):
            dve.wait_ge(s_ps, LU * c + (u + 1))
            steps.did(nc.vector.reduce_max(s_mx[u % 2], s_lg[u % 2], AX_X))
            steps.settled()
            nc.vector.tensor_scalar(s_nmx[u % 2], s_mx[u % 2], -SCALE, None, ALU.mult).then_inc(s_max, 1)

        def stream_scale(c, u):
            dve.wait_ge(s_exp, LU * c + (u + 1))
            steps.did(nc.vector.reciprocal(s_rden[u % 2][:, 0:1], s_den[u % 2]))
            steps.settled()
            steps.did(nc.vector.tensor_scalar(s_rden[u % 2][:, 1:2], s_rden[u % 2][:, 0:1], row_sign, None, ALU.mult))
            steps.settled()
            nc.vector.tensor_scalar(sp_probs[u % 2], sp_probs[u % 2], s_rden[u % 2][:, 1:2], None, ALU.mult).then_inc(s_prob, 1)

        def maxima(c, u):
            n = (u % PT + 1) * P
            b = 2 * (u % 2)
            dve.wait_ge(p_ps, U * c + (u + 1))
            nc.vector.memset(psum[0:CHUNK, b:b + 2, n - CHUNK:n], NEG).then_inc(masked, 1)
            tap_of(c, u, 0)
            dve.wait_ge(masked, U * c + (u + 1))
            steps.did(nc.vector.reduce_max(mx[u % 2], psum[:, b:b + 2, 0:n], AX_X))
            tap_of(c, u, 1)
            steps.settled()
            nc.vector.tensor_scalar(nmx[u % 2], mx[u % 2], -SCALE, None, ALU.mult).then_inc(p_max, 1)

        def combine(c, u):
            n = (u % PT + 1) * P
            dve.wait_ge(p_exp, U * c + (u + 1))
            steps.did(nc.vector.reciprocal(rden[u % 2], den[u % 2]))
            tap_of(c, u + 1, 2)
            steps.settled()
            steps.did(nc.vector.tensor_scalar(second[:, 0:n], probs[u % 2][:, 1, 0:n], rden[u % 2][:, 1:2], minus_lam,
                                              ALU.mult, ALU.mult))
            tap_of(c, u + 1, 3)
            steps.settled()
            if exists(c, u - 2):
                dve.wait_ge(p_pT, U * c + (u - 1))
            nc.vector.scalar_tensor_tensor(diff[u % 2][:, 0:n], probs[u % 2][:, 0, 0:n], rden[u % 2][:, 0:1], second[:, 0:n],
                                           ALU.mult, ALU.add).then_inc(p_prob, 1)

        def tap_of(c, u, number):
            k = u * TAPS // U + number
            if k < (u + 1) * TAPS // U and u < U and not (isinstance(c, int) and c == ROUNDS - 1):
                w = m.w_dw[:, bass.ds(c + DT // 2, 1), k:k + 1].rearrange("p a k -> p (a k)")
                row = m.uT[:, bass.ds(c + DT // 2, 1), k:k + PROMPT].rearrange("p a t -> p (a t)")
                if k == 0:
                    dve.wait_ge(acc_free, c + 1)
                    nc.vector.tensor_scalar(acc, row, w, None, ALU.mult).then_inc(tap, 1)
                else:
                    dve.wait_ge(tap, TAPS * c + k)
                    nc.vector.scalar_tensor_tensor(acc, row, w, acc, ALU.mult, ALU.add).then_inc(tap, 1)

        def step(c, u):
            if exists(c, u):
                maxima(c, u)
            if exists(c, u - 1):
                combine(c, u - 1)
            if exists(c, u):
                if not exists(c, u - 1):
                    tap_of(c, u, 2)
                    tap_of(c, u, 3)
                (stream_scale if u % 2 else stream_max)(c, u // 2)
                if u == U - 1:
                    steps.restart()

        over_rounds(dve, step)
        steps.settled()


def load_pair(sp, m, w_pq, sk_T, slot, g):
    sp.dma_start(m.w_pair[slot], by_channels(w_pq, g * P, P)).then_inc(m.pair_landed[slot], 16)
    sp.dma_start(m.pair_keys[slot], sk_T[bass.ds(g, 1)].rearrange("a p n -> (a p) n")).then_inc(m.pair_landed[slot], 16)


def merge(nc, ctx, m, x, w_in, w_ao, w_co, w_out, w_pq, sk_T):
    def sem(name):
        return ctx.enter_context(nc.semaphore(name))

    w_landed = [sem(f"unit_landed{s}") for s in range(4)]
    wo_landed, x_in = [sem("wo_landed0"), sem("wo_landed1")], sem("x_in")
    o_sq, o_sum, o_var, o_std, o_rstd, o_spread, o_ready = [sem("o_" + n) for n in ("sq", "sum", "var", "std", "rstd", "spread", "ready")]
    y_sum, y_centred, y_sq, y_sq_sum, y_var, y_std, y_norm, y_ready = [
        sem("y_" + n) for n in ("sum", "centred", "sq", "sq_sum", "var", "std", "norm", "ready")]
    gp_ps, gate_ready, gp_done = sem("gp_ps"), sem("mgate_ready"), sem("gp_done")
    h_ps, h_done, h_sq, r_std, xn2_ready, x2T_ps, x2T_done = [sem(n) for n in ("h_ps", "h_done", "h_sq", "r_std", "xn2_ready", "x2T_ps", "x2T_done")]
    r_var, gain_ready = sem("r_var"), sem("gain_ready")
    dve_did = sem("dve_did3")

    work, psum = m.work, m.psum
    sq = [work[:, s * TOK:(s + 1) * TOK] for s in range(2)]
    rB, std, muB, bR, bstd = [work[:, (2 + k) * TOK:(3 + k) * TOK] for k in range(5)]
    sg = [work[:, (7 + k) * TOK:(8 + k) * TOK] for k in range(2)]
    first_branch = work[:, 9 * TOK:10 * TOK]
    other = work[:, 10 * TOK:11 * TOK]
    hsq = work[:, 0:D]
    ss, var, hstd, rstd = [m.small[:, 16 + 2 * k:17 + 2 * k] for k in range(4)]
    sets = [(0, 1, 2), (3, 4, 5)]
    spread = [(6, 7), (3, 5)]

    block = ctx.enter_context(nc.Block())

    @block.sync
    def _(sp):
        def unit(q, j):
            br = q % 2
            sp.dma_start(m.wu[2 * q], by_channels(w_in, j * P + (G_COL + br * D), P)).then_inc(w_landed[q], 16)
            sp.dma_start(m.wu[2 * q + 1], by_channels((w_ao, w_co)[br], j * P, P)).then_inc(w_landed[q], 16)

        for q in range(4):
            unit(q, q // 2)
        with sp.Fori(1, DT // 2) as c:
            for q in range(4):
                sp.wait_ge(gp_ps, 4 * c + (q - 3))
                unit(q, 2 * c + q // 2)
        for s in range(2):
            sp.wait_ge(gp_ps, 2 * DT - 2 + 2 * s)
            sp.dma_start(m.wo[s], by_channels(w_out, s * 512, 512)).then_inc(wo_landed[s], 16)
        sp.dma_start(m.h[:, 0, :], x[PROMPT:TOK, :]).then_inc(x_in, 16)
        sp.dma_start(m.h[:, 1:, :], x[0:PROMPT, :].rearrange("(i p) n -> p i n", p=P)).then_inc(x_in, 16)
        sp.wait_ge(gp_done, 2 * DT)
        for s in range(4):
            load_pair(sp, m, w_pq, sk_T, s, s)

    @block.tensor
    def _(pe):
        for j in range(DT):
            a, b = columns_of(m.yT[:, j, :])
            nc.tensor.matmul(psum[:, 6, :], m.ones[:, :], a, start=(j == 0), stop=(j == DT - 1))
            last = nc.tensor.matmul(psum[:, 7, 0:P], m.ones[:, :], b, start=(j == 0), stop=(j == DT - 1))
        last.then_inc(y_sum, 1)
        for h in range(HEADS):
            pe.wait_ge(o_sq, h + 1)
            sel = m.cols[:, C_SEL + HEADS - 1 - h:C_SEL + 2 * HEADS - 1 - h]
            a, b = columns_of(sq[h % 2])
            nc.tensor.matmul(psum[0:HEADS, 1, :], sel, a, start=(h == 0), stop=(h == HEADS - 1))
            nc.tensor.matmul(psum[0:HEADS, 4, 0:P], sel, b, start=(h == 0), stop=(h == HEADS - 1)).then_inc(o_sum, 1)

        def part_of(q, part):
            t = sets[q % 2]
            rhs = (m.xnT, (m.oT, m.yT)[q % 2])[part]
            for k in range(DT):
                a, b = columns_of(rhs[:, k, :])
                w = m.wu[2 * q + part][:, k, :]
                nc.tensor.matmul(psum[:, t[part], :], w, a, start=(k == 0), stop=(k == DT - 1))
                last = nc.tensor.matmul(psum[:, t[2], part * P:(part + 1) * P], w, b, start=(k == 0), stop=(k == DT - 1))
            return last

        def units(c, numbers, first):
            for q in numbers:
                pe.wait_ge(w_landed[q], 32 * c + 32)
                if not first or q >= 2:
                    pe.wait_ge(gp_done, 4 * c + (q - 1))
                part_of(q, 0)
                part_of(q, 1).then_inc(gp_ps, 1)

        pe.wait_ge(w_landed[0], 32)
        part_of(0, 0)
        pe.wait_ge(o_var, 2)
        for j in range(DT):
            pe.wait_ge(y_sq, j + 1)
            a, b = columns_of(sq[j % 2])
            nc.tensor.matmul(psum[:, 1, :], m.ones[:, :], a, start=(j == 0), stop=(j == DT - 1))
            nc.tensor.matmul(psum[:, 4, 0:P], m.ones[:, :], b, start=(j == 0), stop=(j == DT - 1)).then_inc(y_sq_sum, 1)
        pe.wait_ge(o_rstd, 1)
        for h in range(HEADS):
            if h >= 2:
                pe.wait_ge(o_ready, h - 1)
            sel = m.ident[0:HEADS, h:h + 1].to_broadcast([HEADS, P])
            a, b = columns_of(rB[0:HEADS, :])
            nc.tensor.matmul(psum[:, spread[h % 2][0], :], sel, a, start=True, stop=True)
            nc.tensor.matmul(psum[:, spread[h % 2][1], 0:P], sel, b, start=True, stop=True).then_inc(o_spread, 1)
        pe.wait_ge(y_var, 2)
        pe.wait_ge(o_ready, HEADS)
        part_of(0, 1).then_inc(gp_ps, 1)
        pe.wait_ge(w_landed[1], 32)
        part_of(1, 0)
        pe.wait_ge(y_ready, DT)
        part_of(1, 1).then_inc(gp_ps, 1)
        units(0, (2, 3), True)
        with pe.Fori(1, DT // 2) as c:
            units(c, range(4), False)
        pe.wait_ge(gp_done, 2 * DT)

        def turn(i):
            pe.wait_ge(xn2_ready, i + 1)
            if i >= 1:
                pe.wait_ge(x2T_done, i)
            for k in range(DT):
                last = nc.tensor.transpose(psum[:, 4 + k // 4, (k % 4) * P:(k % 4 + 1) * P], m.xn2[:, i, k * P:(k + 1) * P], m.ident[:, :])
            last.then_inc(x2T_ps, 1)

        def half(i, s):
            pe.wait_ge(wo_landed[s], 16)
            for k in range(DT):
                last = nc.tensor.matmul(psum[:, 2 * (i % 2) + s, :], m.mT[:, k, tile_columns(i)], m.wo[s][:, k, :],
                                        start=(k == 0), stop=(k == DT - 1))
            return last

        for i in range(2):
            half(i, 0)
        for i in range(TILES):
            if i >= 2:
                pe.wait_ge(h_done, i - 1)
                half(i, 0)
            half(i, 1).then_inc(h_ps, 1)
            if i >= 1:
                turn(i - 1)
        turn(TILES - 1)

    @block.scalar
    def _(act):
        for h in range(HEADS):
            if h >= 2:
                act.wait_ge(o_sum, h - 1)
            nc.scalar.activation(sq[h % 2], m.oT[:, h, :], ACT.Square).then_inc(o_sq, 1)
        act.wait_ge(o_var, 2)
        nc.scalar.activation(std[0:HEADS, :], rB[0:HEADS, :], ACT.Sqrt).then_inc(o_std, 1)
        act.wait_ge(o_sum, HEADS)
        for j in range(DT):
            act.wait_ge(y_centred, j + 1)
            if j >= 2:
                act.wait_ge(y_sq_sum, j - 1)
            nc.scalar.activation(sq[j % 2], m.yT[:, j, :], ACT.Square).then_inc(y_sq, 1)
        act.wait_ge(y_var, 2)
        nc.scalar.activation(bstd, bR, ACT.Sqrt).then_inc(y_std, 1)
        for j in range(DT):
            act.wait_ge(y_norm, j + 1)
            nc.scalar.activation(m.yT[:, j, :], m.yT[:, j, :], ACT.Silu, bias=m.col(C_BCLN + j), scale=m.col(C_GCLN + j)).then_inc(y_ready, 1)
        with act.Fori(0, DT // 2) as c:
            for q in range(4):
                t = sets[q % 2]
                act.wait_ge(gp_ps, 4 * c + (q + 1))
                if q >= 2:
                    act.wait_ge(gp_done, 4 * c + (q - 1))
                bias = m.col(C_BGATE + DT * (q % 2) + q // 2, 2 * c)
                a, b = columns_of(sg[q % 2])
                nc.scalar.activation(a, psum[:, t[0], :], ACT.Sigmoid, bias=bias)
                nc.scalar.activation(b, psum[:, t[2], 0:P], ACT.Sigmoid, bias=bias).then_inc(gate_ready, 1)
        for i in range(TILES):
            act.wait_ge(h_done, i + 1)
            nc.scalar.activation(hsq, m.h[:, i, :], ACT.Square, accum_out=ss).then_inc(h_sq, 1)
            act.wait_ge(r_var, i + 1)
            nc.scalar.activation(hstd, var, ACT.Sqrt).then_inc(r_std, 1)
            act.wait_ge(x2T_ps, i + 1)
            for k in range(2):
                last = nc.scalar.activation(m.mT[:, 4 * k:4 * k + 4, tile_columns(i)],
                                            psum[:, 4 + k, :].rearrange("p (c t) -> p c t", c=4), ACT.Copy)
            last.then_inc(x2T_done, 1)

    @block.vector
    def _(dve):
        steps = Chain(dve, dve_did)
        nc.vector.tensor_scalar(m.lam[:, 7:8], m.col(C_GSUB), 1.0 - LAMBDA_INIT, None, ALU.mult).then_inc(gain_ready, 1)
        dve.wait_ge(gain_ready, 1)
        dve.wait_ge(y_sum, 1)
        for a, b in zip(columns_of(muB), (psum[:, 6, :], psum[:, 7, 0:P])):
            steps.did(nc.vector.tensor_scalar(a, b, 1.0 / D, None, ALU.mult))
        dve.wait_ge(o_sum, HEADS)
        for a, b in zip(columns_of(rB[0:HEADS, :]), (psum[0:HEADS, 1, :], psum[0:HEADS, 4, 0:P])):
            nc.vector.tensor_scalar(a, b, 1.0 / P, EPS, ALU.mult, ALU.add).then_inc(o_var, 1)
        steps.settled()
        for j in range(DT):
            nc.vector.tensor_tensor(m.yT[:, j, :], m.yT[:, j, :], muB, ALU.subtract).then_inc(y_centred, 1)
        dve.wait_ge(o_std, 1)
        nc.vector.reciprocal(rB[0:HEADS, :], std[0:HEADS, :]).then_inc(o_rstd, 1)
        dve.wait_ge(y_sq_sum, DT)
        for a, b in zip(columns_of(bR), (psum[:, 1, :], psum[:, 4, 0:P])):
            nc.vector.tensor_scalar(a, b, 1.0 / D, EPS, ALU.mult, ALU.add).then_inc(y_var, 1)
        for h in range(HEADS):
            dve.wait_ge(o_spread, h + 1)
            parts = zip(columns_of(m.oT[:, h, :]), (psum[:, spread[h % 2][0], :], psum[:, spread[h % 2][1], 0:P]))
            for a, b in parts:
                last = nc.vector.scalar_tensor_tensor(a, a, m.lam[:, 7:8], b, ALU.mult, ALU.mult)
            last.then_inc(o_ready, 1)
        dve.wait_ge(y_std, 1)
        steps.did(nc.vector.reciprocal(bR, bstd))
        steps.settled()
        for j in range(DT):
            nc.vector.tensor_tensor(m.yT[:, j, :], m.yT[:, j, :], bR, ALU.mult).then_inc(y_norm, 1)
        steps.restart()

        def branches(c, first):
            for q in range(4):
                t = sets[q % 2]
                if q % 2 == 0 and not (first and q == 0):
                    dve.wait_ge(gp_done, 4 * c + q)
                dve.wait_ge(gate_ready, 4 * c + (q + 1))
                dst = (first_branch, other)[q % 2]
                for a, g, b in zip(columns_of(dst), columns_of(sg[q % 2]), (psum[:, t[1], :], psum[:, t[2], P:2 * P])):
                    last = nc.vector.tensor_tensor(a, b, g, ALU.mult)
                if q % 2 == 0:
                    last.then_inc(gp_done, 1)
                else:
                    steps.did(last)
                    steps.settled()
                    nc.vector.tensor_tensor(m.mT[:, bass.ds(2 * c + q // 2, 1), :].rearrange("p a t -> p (a t)"), first_branch, other,
                                            ALU.add).then_inc(gp_done, 1)
            steps.restart()

        branches(0, True)
        with dve.Fori(1, DT // 2) as c:
            branches(c, False)
        dve.wait_ge(x_in, 32)
        for i in range(TILES):
            b = 2 * (i % 2)
            dve.wait_ge(h_ps, i + 1)
            nc.vector.tensor_tensor(m.h[:, i, :].rearrange("p (s n) -> p s n", s=2), m.h[:, i, :].rearrange("p (s n) -> p s n", s=2),
                                    psum[:, b:b + 2, :], ALU.add).then_inc(h_done, 1)
            dve.wait_ge(h_sq, i + 1)
            nc.vector.tensor_scalar(var, ss, 1.0 / D, EPS, ALU.mult, ALU.add).then_inc(r_var, 1)
            dve.wait_ge(r_std, i + 1)
            steps.did(nc.vector.reciprocal(rstd, hstd))
            steps.settled()
            nc.vector.scalar_tensor_tensor(m.xn2[:, i, :], m.h[:, i, :], rstd, m.rows[:, R_GFFN:R_GFFN + D], ALU.mult,
                                           ALU.mult).then_inc(xn2_ready, 1)


def retrieve(nc, ctx, m, w_pq, sk_T, exp_u, exp_v, y_p, y_s):
    def sem(name):
        return ctx.enter_context(nc.semaphore(name))

    sc_copied, xs_copied = sem("sc_copied"), sem("xs_copied")
    idx_ready, best_ready, exp_ready = sem("idx_ready"), sem("best_ready"), sem("gate_exp_ready")
    u_landed = [sem(f"u_landed{s}") for s in range(U_RING)]
    v_landed = [sem(f"v_landed{s}") for s in range(V_RING)]
    dots, acted, w_ready, diag_ready, v_used = sem("dots"), sem("acted"), sem("w_ready"), sem("diag_ready"), sem("v_used")
    y_done, y_stored = sem("y_done"), sem("y_stored")
    landed = m.pair_landed
    sq_ps, sq_copied, ss_ps, ss_copied = [sem(n) for n in ("sq_ps", "sq_copied", "ss_ps", "ss_copied")]
    q_ps, q_copied, s_ps, s_copied = [sem(n) for n in ("pq_ps", "pq_copied", "ps_ps", "ps_copied")]
    dve_did = sem("dve_did6")

    work, psum, small = m.work, m.psum, m.small
    STEPS = TILES * PH
    urow = [m.slab_w[:, s * D:(s + 1) * D] for s in range(U_RING)]
    vrow = [m.slab_u[:, s * D:(s + 1) * D] for s in range(V_RING)]
    junk = [m.slab_u[:, (V_RING + k) * D:(V_RING + k + 1) * D] for k in range(2)]
    xs = m.slab_u[:, (V_RING + 2) * D:(V_RING + 3) * D]
    sc = [work[:, s * 256:(s + 1) * 256].rearrange("p (h k) -> p h k", h=2) for s in range(2)]
    sr = [work[:, 512:640], work[:, 2560:2688]]
    cand, cand2 = work[:, 640:896], work[:, 896:1152]
    eq = [work[:, 1152 + 256 * k:1408 + 256 * k].rearrange("p (k a) -> p k a", k=TOPK) for k in range(2)]
    diag = [work[:, 1664 + P * k:1664 + P * (k + 1)] for k in range(4)]
    tv = work[:, 2176:2208].rearrange("p (h a) -> p h a", h=2)
    bs = [work[:, 2208 + 16 * k:2224 + 16 * k] for k in range(2)]
    ex = [work[:, 2240 + 16 * k:2256 + 16 * k] for k in range(2)]
    ij = [work[:, 2272 + 16 * k:2288 + 16 * k] for k in range(2)]
    a_dot = [work[:, 2304 + 16 * k:2320 + 16 * k] for k in range(2)]
    a_act = [work[:, 2336 + 16 * k:2352 + 16 * k] for k in range(2)]
    wt = [work[:, 2368 + 16 * k:2384 + 16 * k] for k in range(2)]
    words = work[:, 2400:2400 + 160].bitcast(U32)
    ti = words[:, 0:32].rearrange("p (h a) -> p h a", h=2)
    bj, ab = words[:, 32:48], [words[:, 48:64], words[:, 64:80]]
    idx = [words[:, 80 + 16 * k:96 + 16 * k] for k in range(4)]
    nb, esum, er = [small[:, 16 + 4 * k:20 + 4 * k] for k in range(3)]
    iota16 = m.rows[:, R_IOTA:R_IOTA + TOPK]
    w_pair, keys = m.w_pair, m.pair_keys
    q_sb = [m.slab_w[:, 8192 + s * PROMPT:8192 + (s + 1) * PROMPT] for s in range(2)]
    q_st = [work[:, 7296 + s * P:7424 + s * P] for s in range(4)]

    Q_AT = (DT + 2, 1)

    block = ctx.enter_context(nc.Block())

    @block.gpsimd
    def _(pool):
        passed = pool.alloc_register("passed")
        pool.reg_mov(passed, 0)

        def gather(dst, table, index, done):
            pool.reg_alu(passed, passed, 1, ALU.bitwise_xor)
            nc.gpsimd.indirect_dma_start(out=dst, out_offset=None, in_=table,
                                         in_offset=bass.IndirectOffsetOnAxis(ap=index, axis=0)).then_inc(done, 16)

        def step(c, h, last):
            for k in range(TOPK):
                if not (isinstance(c, int) and PH * TOPK * c + TOPK * h + k < V_RING):
                    pool.wait_ge(v_used, PH * TOPK * c + (TOPK * h + k - V_RING + 1))
                gather(vrow[k % V_RING], exp_v, idx[h % 4][:, k:k + 1], v_landed[k % V_RING])
                if not last:
                    if k == 0:
                        pool.wait_ge(idx_ready, PH * c + (h + 2))
                    pool.wait_ge(dots, PH * TOPK * c + (TOPK * (h + 1) + k - U_RING + 1))
                    gather(urow[k % U_RING], exp_u, idx[(h + 1) % 4][:, k:k + 1], u_landed[k % U_RING])

        pool.wait_ge(idx_ready, 1)
        for k in range(TOPK):
            if k >= U_RING:
                pool.wait_ge(dots, k - U_RING + 1)
            gather(urow[k % U_RING], exp_u, idx[0][:, k:k + 1], u_landed[k % U_RING])
        for h in range(PH):
            step(0, h, False)
        with pool.Fori(1, TILES - 1) as c:
            for h in range(PH):
                step(c, h, False)
        for h in range(PH):
            step(TILES - 1, h, h == PH - 1)
        pool.wait_ge(idx_ready, pool.snap(passed))

    @block.sync
    def _(sp):
        with sp.Fori(1, PH // 2) as c:
            for s in range(4):
                sp.wait_ge(ss_ps, 4 * c + (s - 3))
                load_pair(sp, m, w_pq, sk_T, s, 4 * c + s)
        for s in range(4):
            sp.wait_ge(ss_ps, 2 * PH + s - 3)
            load_pair(sp, m, w_pq, sk_T, s, s)
        with sp.Fori(1, PH // 2) as c:
            for s in range(4):
                sp.wait_ge(s_ps, 4 * c + (s - 3))
                load_pair(sp, m, w_pq, sk_T, s, 4 * c + s)
        sp.wait_ge(y_done, 1)
        sp.dma_start(y_s, m.h[:, 0, :]).then_inc(y_stored, 16)
        with sp.Fori(1, TILES) as c:
            sp.wait_ge(y_done, c + 1)
            sp.dma_start(y_p[bass.ds(c * P - P, P), :], m.h[:, bass.ds(c, 1), :].rearrange("p a n -> p (a n)")).then_inc(y_stored, 16)
        sp.wait_ge(y_stored, 16 * TILES)

    def over_tiles(eng, step):
        for h in range(PH):
            step(0, h)
        with eng.Fori(1, TILES - 1) as c:
            for h in range(PH):
                step(c, h)
        for h in range(PH):
            step(TILES - 1, h)

    def exists(c, h, ahead):
        return not isinstance(c, int) or PH * c + h + ahead < STEPS

    @block.tensor
    def _(pe):
        def stream_queries(c, s, first):
            pe.wait_ge(landed[s], 32 * c + 32)
            if not first:
                pe.wait_ge(sq_copied, 4 * c + (s - 3))
            for k in range(DT):
                last = nc.tensor.matmul(psum[:, s, 0:P], w_pair[s][:, k, :], m.mT[:, k, PROMPT:TOK], start=(k == 0), stop=(k == DT - 1))
            last.then_inc(sq_ps, 1)

        def stream_scores(c, s, first):
            pe.wait_ge(sq_copied, 4 * c + (s + 1))
            if not first:
                pe.wait_ge(ss_copied, 4 * c + (s - 3))
            nc.tensor.matmul(psum[:, 4 + s, 0:P], q_st[s], keys[s], start=True, stop=True).then_inc(ss_ps, 1)

        def four_pairs(c, first):
            for s in range(4):
                stream_queries(c, s, first)
                if s >= 1:
                    stream_scores(c, s - 1, first)
            stream_scores(c, 3, first)

        four_pairs(0, True)
        with pe.Fori(1, PH // 2) as c:
            four_pairs(c, False)
        pe.wait_ge(ss_copied, 2 * PH)

        def prompt_queries(h, s, k):
            slot = (2 * h + s) % 4
            if k == 0:
                pe.wait_ge(landed[slot], 32 * PH // 2 + 32 * (h // 2 + 1))
                if h >= 1:
                    pe.wait_ge(q_copied, 2 * h + s - 1)
            made = nc.tensor.matmul(psum[:, 2 + s, :], w_pair[slot][:, k, :], m.mT[:, k, 0:PROMPT], start=(k == 0), stop=(k == DT - 1))
            if k == DT - 1:
                made.then_inc(q_ps, 1)

        def prompt_scores(h, s):
            pe.wait_ge(q_copied, 2 * h + s + 1)
            if h >= 1:
                pe.wait_ge(s_copied, 2 * h + s - 1)
            for i in range(PT):
                last = nc.tensor.matmul(psum[:, 4 + s, i * P:(i + 1) * P], q_sb[s][:, i * P:(i + 1) * P],
                                        keys[(2 * h + s) % 4], start=True, stop=True)
            last.then_inc(s_ps, 1)

        def step(c, h):
            streams = isinstance(c, int) and c == 0
            for k in range(TOPK):
                pe.wait_ge(diag_ready, PH * TOPK * c + (TOPK * h + k + 1))
                pe.wait_ge(v_landed[k % V_RING], 16 * PH * TOPK // V_RING * c + 16 * (TOPK // V_RING * h + k // V_RING + 1))
                if h == 0 and k == 0 and not (isinstance(c, int) and c == 0):
                    pe.wait_ge(y_done, c)
                for s in range(2):
                    last = nc.tensor.matmul(psum[:, s, :], diag[k % 4], vrow[k % V_RING][:, s * 512:(s + 1) * 512],
                                            start=(h == 0 and k == 0), stop=(h == PH - 1 and k == TOPK - 1))
                last.then_inc(v_used, 1)
                if streams:
                    prompt_queries(h, k // DT, k % DT)
                    if k == Q_AT[0] + 1:
                        prompt_scores(h, 0)
                    if k == Q_AT[1] + 1 and h >= 1:
                        prompt_scores(h - 1, 1)
            if streams and h == PH - 1:
                prompt_scores(h, 1)

        over_tiles(pe, step)

    @block.scalar
    def _(act):
        def copy_scores(n, s):
            nc.scalar.activation(sc[s], m.scores[:, bass.ds(n, 1), :].rearrange("p a (h k) -> p (a h) k", h=2),
                                 ACT.Copy).then_inc(sc_copied, 1)

        def exps(n, s):
            act.wait_ge(best_ready, n + 1)
            nc.scalar.activation(ex[s], bs[s], ACT.Exp, bias=nb[:, s:s + 1], accum_out=esum[:, s:s + 1]).then_inc(exp_ready, 1)

        def copy_queries(h, j):
            act.wait_ge(q_ps, 2 * h + j + 1)
            nc.scalar.activation(q_sb[j], psum[:, 2 + j, :], ACT.Copy).then_inc(q_copied, 1)

        def keep_scores(h, j):
            act.wait_ge(s_ps, 2 * h + j + 1)
            nc.scalar.activation(m.scores_ig[:, 1:, 2 * h + j, :], psum[:, 4 + j, :].rearrange("p (i k) -> p i k", i=PT),
                                 ACT.Copy).then_inc(s_copied, 1)

        def step(c, h):
            s = h % 2
            streams = isinstance(c, int) and c == 0
            if streams and h >= PH - 2:
                act.wait_ge(s_copied, 2 * (h + 2 - PH) + 2)
            elif h == 0 and not streams:
                act.wait_ge(s_copied, 2 * PH)
            if exists(c, h, 2):
                copy_scores(PH * c + (h + 2), s)
            if exists(c, h, 1):
                exps(PH * c + (h + 1), 1 - s)
            act.wait_ge(dots, PH * TOPK * c + TOPK * (h + 1))
            nc.scalar.activation(a_act[s], a_dot[s], ACT.Gelu_apprx_tanh).then_inc(acted, 1)
            if h == PH - 1 and exists(c, h, 1):
                copy_rows(c + 1)
            act.wait_ge(w_ready, PH * c + (h + 1))
            for k in range(TOPK):
                if not (isinstance(c, int) and PH * TOPK * c + TOPK * h + k < 4):
                    act.wait_ge(v_used, PH * TOPK * c + (TOPK * h + k - 3))
                nc.scalar.activation(diag[k % 4], m.ident[:, :], ACT.Copy, scale=wt[s][:, k:k + 1]).then_inc(diag_ready, 1)
                if streams:
                    for j in range(2):
                        if (j == 0 or h >= 1) and k == Q_AT[j]:
                            copy_queries(h - j, j)
                        if (j == 0 or h >= 1) and k == Q_AT[j] + 3:
                            keep_scores(h - j, j)
            if streams and h == PH - 1:
                copy_queries(h, 1)
                keep_scores(h, 1)

        def copy_rows(c):
            nc.scalar.activation(xs, m.xn2[:, bass.ds(c, 1), :].rearrange("p a n -> p (a n)"), ACT.Copy).then_inc(xs_copied, 1)

        def stream_pairs(c):
            for s in range(5):
                if s < 4:
                    act.wait_ge(sq_ps, 4 * c + (s + 1))
                    nc.scalar.activation(q_st[s], psum[:, s, 0:P], ACT.Copy).then_inc(sq_copied, 1)
                if s >= 1:
                    act.wait_ge(ss_ps, 4 * c + s)
                    nc.scalar.activation(m.scores_ig[:, 0, bass.ds(4 * c + (s - 1), 1), :].rearrange("p a k -> p (a k)"),
                                         psum[:, 3 + s, 0:P], ACT.Copy).then_inc(ss_copied, 1)

        stream_pairs(0)
        act.wait_ge(ss_copied, 4)
        copy_scores(0, 0)
        copy_scores(1, 1)
        with act.Fori(1, PH // 2) as c:
            stream_pairs(c)
        act.wait_ge(ss_copied, 2 * PH)
        exps(0, 0)
        copy_rows(0)
        over_tiles(act, step)

    @block.vector
    def _(dve):
        steps = Chain(dve, dve_did)

        def top(n, q):
            s = q % 2
            did, settled = steps.did, steps.settled
            dve.wait_ge(sc_copied, n + 1)
            nc.vector.memset(er[:, 2:3], 0.0)
            for k in range(2):
                did(nc.vector.max(tv[:, k, 0:8], sc[s][:, k, :]))
            settled()
            for k in range(2):
                did(nc.vector.max_index(ti[:, k, 0:8], tv[:, k, 0:8], sc[s][:, k, :]))
                did(nc.vector.match_replace(sr[k], tv[:, k, 0:8], sc[s][:, k, :], NEG))
            settled()
            for k in range(2):
                did(nc.vector.max(tv[:, k, 8:16], sr[k]))
            settled()
            for k in range(2):
                did(nc.vector.max_index(ti[:, k, 8:16], tv[:, k, 8:16], sr[k]))
            did(nc.vector.tensor_tensor(cand.rearrange("p (a b) -> p a b", a=TOPK), tv[:, 0, :, None].to_broadcast([P, TOPK, TOPK]),
                                        tv[:, 1:2, :].to_broadcast([P, TOPK, TOPK]), ALU.add))
            settled()
            did(nc.vector.max(bs[s][:, 0:8], cand))
            settled()
            did(nc.vector.max_index(bj[:, 0:8], bs[s][:, 0:8], cand))
            did(nc.vector.match_replace(cand2, bs[s][:, 0:8], cand, NEG))
            settled()
            did(nc.vector.max(bs[s][:, 8:16], cand2))
            settled()
            did(nc.vector.max_index(bj[:, 8:16], bs[s][:, 8:16], cand2))
            nc.vector.tensor_scalar(nb[:, s:s + 1], bs[s][:, 0:1], -1.0, None, ALU.mult).then_inc(best_ready, 1)
            settled()
            did(nc.vector.tensor_scalar(ab[0], bj, 4, None, ALU.logical_shift_right))
            did(nc.vector.tensor_scalar(ab[1], bj, TOPK - 1, None, ALU.bitwise_and))
            settled()
            for k in range(2):
                did(nc.vector.tensor_tensor(eq[k], ab[k][:, :, None].to_broadcast([P, TOPK, TOPK]),
                                            iota16[:, None, :].to_broadcast([P, TOPK, TOPK]), ALU.is_equal))
            settled()
            for k in range(2):
                did(nc.vector.tensor_tensor(eq[k], eq[k], ti[:, k:k + 1, :].to_broadcast([P, TOPK, TOPK]), ALU.mult))
            settled()
            for k in range(2):
                did(nc.vector.tensor_reduce(ij[k], eq[k], AX_X, ALU.add))
            settled()
            nc.vector.scalar_tensor_tensor(idx[q], ij[0], float(NKEYS), ij[1], ALU.mult, ALU.add).then_inc(idx_ready, 1)

        def result(c):
            tile = m.h[:, bass.ds(c, 1), :].rearrange("p a (s n) -> p (a s) n", s=2)
            nc.vector.tensor_tensor(tile, tile, psum[:, 0:2, :], ALU.add).then_inc(y_done, 1)

        def step(c, h):
            s = h % 2
            if exists(c, h, 1):
                top(PH * c + (h + 1), (h + 1) % 4)
            if h == 0:
                dve.wait_ge(xs_copied, c + 1)
            for k in range(TOPK):
                dve.wait_ge(u_landed[k % U_RING], 16 * PH * TOPK // U_RING * c + 16 * (TOPK // U_RING * h + k // U_RING + 1))
                if not (isinstance(c, int) and PH * TOPK * c + TOPK * h + k < 2):
                    dve.wait_ge(dots, PH * TOPK * c + (TOPK * h + k - 1))
                nc.vector.tensor_tensor_reduce(junk[k % 2], urow[k % U_RING], xs, 1.0, 0.0, ALU.mult, ALU.add,
                                               a_dot[s][:, k:k + 1]).then_inc(dots, 1)
            if h == 0 and not (isinstance(c, int) and c == 0):
                dve.wait_ge(v_used, PH * TOPK * c)
                result(c - 1)
            dve.wait_ge(exp_ready, PH * c + (h + 1))
            steps.did(nc.vector.reciprocal(er[:, s:s + 1], esum[:, s:s + 1]))
            steps.settled()
            dve.wait_ge(acted, PH * c + (h + 1))
            nc.vector.scalar_tensor_tensor(wt[s], ex[s], er[:, s:s + 1], a_act[s], ALU.mult, ALU.mult).then_inc(w_ready, 1)
            steps.restart()

        top(0, 0)
        steps.restart()
        over_tiles(dve, step)
        dve.wait_ge(v_used, STEPS * TOPK)
        result(TILES - 1)


def program(nc, x, xT, w_in, cols_d, rows_d, ident_d, ck_T, cv, cc_T, w_ao, w_co, w_out, w_pq, sk_T, exp_u, exp_v,
            y_p, y_s, k_p, v_p, c_p, k_s, v_s, c_s):
    with ExitStack() as memory:
        m = Memory(nc, memory)
        for stage, args in ((project, (xT, w_in, cols_d, rows_d, ident_d, ck_T, cv, cc_T, k_p, k_s, v_p, v_s, c_p, c_s)),
                            (attend, (ck_T, cv, v_s)),
                            (merge, (x, w_in, w_ao, w_co, w_out, w_pq, sk_T)),
                            (retrieve, (w_pq, sk_T, exp_u, exp_v, y_p, y_s))):
            with ExitStack() as ctx:
                stage(nc, ctx, m, *args)


def lay_out(inp):
    import numpy as np

    c = np.ascontiguousarray
    f = np.float32
    x = np.concatenate([inp["x_prompt"].reshape(PROMPT, D), inp["x_sample"].reshape(STREAMS * NEW, D)])
    by_column = lambda a: a.reshape(-1, P).T
    m = (np.arange(P) // NEW % 2).astype(f)[:, None]
    sel = np.zeros((P, 2 * HEADS - 1), f)
    sel[:, HEADS - 1] = 1
    cols = np.concatenate([by_column(inp[n][0]) for n in ("g_mix", "b_gate", "b_dw", "g_cln", "b_cln", "g_ffn", "g_sub")]
                          + [m, 1 - m, sel, inp["w_dw"][0].reshape(TAPS, DT, P).transpose(2, 1, 0).reshape(P, DT * TAPS)], axis=1)
    row = np.concatenate([inp[n][0] for n in ("g_qn", "g_kn", "lam_q1", "lam_k1", "lam_q2", "lam_k2")]
                         + [np.arange(TOPK, dtype=f), inp["g_ffn"][0]])
    return {
        "x": c(x), "xT": c(x.T), "w_in": c(inp["w_in"][0]), "cols": c(cols), "rows": c(np.broadcast_to(row, (P, row.size))),
        "ident": np.eye(P, dtype=f),
        "ck_T": c(inp["cache_k"][0].reshape(STREAMS, PAST, HEADS, P).transpose(0, 3, 2, 1).reshape(STREAMS, P, D)),
        "cv": c(inp["cache_v"][0].reshape(STREAMS, PAST, D)),
        "cc_T": c(inp["cache_conv"][0].reshape(STREAMS, HIST, DT, P).transpose(2, 3, 0, 1)),
        "w_ao": c(inp["w_attn_out"][0]), "w_co": c(inp["w_conv_out"][0]), "w_out": c(inp["w_out"][0]), "w_pq": c(inp["w_pq"][0]),
        "sk_T": c(inp["sub_keys"][0].reshape(2 * PH, NKEYS, P).transpose(0, 2, 1)),
        "exp_u": c(inp["expert_u"][0]), "exp_v": c(inp["expert_v"][0]),
    }


def kernel(**inputs):
    import numpy as np
    from concourse import bacc
    from concourse.bass_utils import run_bass_kernel_spmd

    nc = bacc.Bacc("TRN2", target_bir_lowering=False, num_devices=1)
    arrays = {f"in_{n}": a for n, a in lay_out({n: np.asarray(a) for n, a in inputs.items()}).items()}
    args = [nc.dram_tensor(n, a.shape, mybir.dt.from_np(a.dtype), kind="ExternalInput").ap() for n, a in arrays.items()]
    shapes = [(PROMPT, D), (STREAMS * NEW, D), (PROMPT, D), (PROMPT, D), (DT, P, HIST), (STREAMS * NEW, D), (STREAMS * NEW, D),
              (DT, P, STREAMS, HIST)]
    outs = [nc.dram_tensor(f"out_{i}_dram", s, F32, kind="ExternalOutput").ap() for i, s in enumerate(shapes)]
    program(nc, *args, *outs)
    r = run_bass_kernel_spmd(nc, [arrays], core_ids=[0]).results[0]
    y_p, y_s, k_p, v_p, c_p, k_s, v_s, c_s = [r[f"out_{i}_dram"] for i in range(len(shapes))]
    return (y_p.reshape(1, PROMPT, D), y_s.reshape(STREAMS, NEW, D),
            k_p.reshape(1, 1, PROMPT, HEADS, 2, DH), v_p.reshape(1, 1, PROMPT, HEADS, P),
            c_p.reshape(D, HIST).T.reshape(1, 1, HIST, D),
            k_s.reshape(1, STREAMS, NEW, HEADS, 2, DH), v_s.reshape(1, STREAMS, NEW, HEADS, P),
            c_s.reshape(D, STREAMS, HIST).transpose(1, 2, 0).reshape(1, STREAMS, HIST, D))
```
